# Optimizing a Trainium2 kernel written in Bass

```python
import jax, jax.numpy as jnp
from jax import lax
import numpy as np

D_MODEL = 2048
BATCH = 1
SEQ = 512
DEPTH = 1

HEAD_DIM = 64
N_MIX_HEADS = D_MODEL // HEAD_DIM
MIX_WIDTH = N_MIX_HEADS * HEAD_DIM
A_HEADS = N_MIX_HEADS // 4
A_KV_HEADS = 2
A_WINDOW = 128
A_BLOCK = 128
B_HEADS = N_MIX_HEADS // 4
MOBA_BLOCK = 256
MOBA_TOPK = 3
MOBA_Q_CHUNK = 32
C_HEADS = N_MIX_HEADS - A_HEADS - B_HEADS
C_PATTERNS = ((128, 1), (512, 4), (2048, 16))
MEM_LEN = 256
X_HEADS = 4
X_HEAD_DIM = 128
X_WIDTH = X_HEADS * X_HEAD_DIM
D_FF = -(-8 * D_MODEL // (3 * 256)) * 256
EPS = 1e-5

SPLIT_WIDTHS = (A_HEADS * HEAD_DIM, A_KV_HEADS * HEAD_DIM, A_KV_HEADS * HEAD_DIM,
                B_HEADS * HEAD_DIM, B_HEADS * HEAD_DIM, B_HEADS * HEAD_DIM,
                C_HEADS * HEAD_DIM, C_HEADS * HEAD_DIM, C_HEADS * HEAD_DIM)
IN_WIDTH = sum(SPLIT_WIDTHS)

kernel_name = 'hybrid_swa_moba_dilated_trunk'

def rmsnorm(x, g):
    xf = x.astype(jnp.float32)
    y = xf * lax.rsqrt(jnp.mean(xf * xf, axis=-1, keepdims=True) + EPS)
    return (y * g.astype(jnp.float32)).astype(x.dtype)

def alibi_slopes(n):
    return jnp.asarray(2.0 ** (-8.0 * np.arange(1, n + 1) / n), jnp.float32)

def with_prev_block(x):
    prev = jnp.concatenate([jnp.zeros_like(x[..., :1, :, :]), x[..., :-1, :, :]], axis=-3)
    return jnp.concatenate([prev, x], axis=-2)

def sliding_window_sink_attn(q, k, v, sinks):
    B, Hk, G, S, hd = q.shape
    f32 = jnp.float32
    nb = S // A_BLOCK
    qb = q.reshape(B, Hk, G, nb, A_BLOCK, hd)
    kb = with_prev_block(k.reshape(B, Hk, nb, A_BLOCK, hd))
    vb = with_prev_block(v.reshape(B, Hk, nb, A_BLOCK, hd))
    s = jnp.einsum('bkgnqd,bknsd->bkgnqs', qb, kb).astype(f32) * (hd ** -0.5)
    dist = jnp.arange(A_BLOCK)[:, None] + A_BLOCK - jnp.arange(2 * A_BLOCK)[None, :]
    kpos_ok = ((jnp.arange(nb)[:, None] - 1) * A_BLOCK + jnp.arange(2 * A_BLOCK)[None, :]) >= 0
    valid = ((dist >= 0) & (dist < A_WINDOW))[None] & kpos_ok[:, None, :]
    slopes = alibi_slopes(Hk * G).reshape(Hk, G)[:, :, None, None, None]
    s = jnp.where(valid, s - slopes * dist.astype(f32), -jnp.inf)
    sink = sinks.astype(f32).reshape(Hk, G)[:, :, None, None, None]
    m = jnp.maximum(jnp.max(s, axis=-1, keepdims=True), sink)
    p = jnp.exp(s - m)
    p = p / (jnp.sum(p, axis=-1, keepdims=True) + jnp.exp(sink - m))
    o = jnp.einsum('bkgnqs,bknsd->bkgnqd', p.astype(v.dtype), vb)
    return o.reshape(B, Hk, G, S, hd)

def moba_attn(q, k, v):
    B, H, S, hd = q.shape
    f32 = jnp.float32
    sp = -(-S // MOBA_BLOCK) * MOBA_BLOCK
    pad = ((0, 0), (0, 0), (0, sp - S), (0, 0))
    q, k, v = jnp.pad(q, pad), jnp.pad(k, pad), jnp.pad(v, pad)
    nb = sp // MOBA_BLOCK
    kb = k.reshape(B, H, nb, MOBA_BLOCK, hd)
    vb = v.reshape(B, H, nb, MOBA_BLOCK, hd)
    n_sel = min(MOBA_TOPK, nb - 1)
    scale = hd ** -0.5
    slopes = alibi_slopes(H)
    QC = MOBA_Q_CHUNK
    nc = sp // QC
    qc = q.reshape(B, H, nc, QC, hd).transpose(2, 0, 1, 3, 4)
    xs = (jnp.arange(nc), qc)
    if n_sel > 0:
        kmean = jnp.mean(kb.astype(f32), axis=3)
        gate = jnp.einsum('bhtd,bhnd->bhtn', q.astype(f32), kmean)
        past = jnp.arange(nb)[None, :] < (jnp.arange(sp) // MOBA_BLOCK)[:, None]
        gate = jnp.where(past, gate, -jnp.inf)
        _, sel = lax.top_k(gate, n_sel)
        xs = xs + (sel.reshape(B, H, nc, QC, n_sel).transpose(2, 0, 1, 3, 4),)

    def chunk(args):
        ci, qi = args[0], args[1]
        t = ci * QC + jnp.arange(QC)
        blk = (ci * QC) // MOBA_BLOCK
        k_own = lax.dynamic_index_in_dim(kb, blk, axis=2, keepdims=False)
        v_own = lax.dynamic_index_in_dim(vb, blk, axis=2, keepdims=False)
        dist_own = t[:, None] - (blk * MOBA_BLOCK + jnp.arange(MOBA_BLOCK))[None, :]
        s_own = jnp.einsum('bhqd,bhsd->bhqs', qi, k_own).astype(f32) * scale - slopes[:, None, None] * dist_own.astype(f32)
        s_own = jnp.where(dist_own >= 0, s_own, -jnp.inf)
        if n_sel == 0:
            p = jax.nn.softmax(s_own, axis=-1).astype(v.dtype)
            return jnp.einsum('bhqs,bhsd->bhqd', p, v_own)
        si = args[2]
        bi = jnp.arange(B)[:, None, None, None]
        hi = jnp.arange(H)[None, :, None, None]
        k_sel = kb[bi, hi, si]
        v_sel = vb[bi, hi, si]
        dist_sel = t[:, None, None] - (si[..., None] * MOBA_BLOCK + jnp.arange(MOBA_BLOCK))
        s_sel = jnp.einsum('bhqd,bhqrsd->bhqrs', qi, k_sel).astype(f32) * scale - slopes[:, None, None, None] * dist_sel.astype(f32)
        s_sel = jnp.where((si < blk)[..., None], s_sel, -jnp.inf)
        s_all = jnp.concatenate([s_sel.reshape(B, H, QC, n_sel * MOBA_BLOCK), s_own], axis=-1)
        p = jax.nn.softmax(s_all, axis=-1).astype(v.dtype)
        p_sel = p[..., :n_sel * MOBA_BLOCK].reshape(B, H, QC, n_sel, MOBA_BLOCK)
        return (jnp.einsum('bhqrs,bhqrsd->bhqd', p_sel, v_sel)
                + jnp.einsum('bhqs,bhsd->bhqd', p[..., n_sel * MOBA_BLOCK:], v_own))

    o = lax.map(chunk, xs)
    return o.transpose(1, 2, 0, 3, 4).reshape(B, H, sp, hd)[:, :, :S]

def _residue_major(x, d, sp):
    B, H, S, e = x.shape
    x = jnp.pad(x, ((0, 0), (0, 0), (0, sp - S), (0, 0)))
    return x.reshape(B, H, sp // d, d, e).transpose(0, 1, 3, 2, 4)

def _seq_major(x, sp):
    B, H, d, L, e = x.shape
    return x.transpose(0, 1, 3, 2, 4).reshape(B, H, sp, e)

def dilated_mixture_attn(q, k, v):
    B, H, S, hd = q.shape
    f32 = jnp.float32
    scale = hd ** -0.5
    slopes = alibi_slopes(H)[:, None, None, None, None]
    outs, lses = [], []
    for (w, d) in C_PATTERNS:
        n = w // d
        unit = d * n
        sp = -(-S // unit) * unit
        L = sp // d
        nb = L // n
        qs = _residue_major(q, d, sp).reshape(B, H, d, nb, n, hd)
        ks = with_prev_block(_residue_major(k, d, sp).reshape(B, H, d, nb, n, hd))
        vs = with_prev_block(_residue_major(v, d, sp).reshape(B, H, d, nb, n, hd))
        s = jnp.einsum('bhrnqd,bhrnsd->bhrnqs', qs, ks).astype(f32) * scale
        step = jnp.arange(n)[:, None] + n - jnp.arange(2 * n)[None, :]
        kpos_ok = ((jnp.arange(nb)[:, None] - 1) * n + jnp.arange(2 * n)[None, :]) >= 0
        valid = ((step >= 0) & (step <= n))[None] & kpos_ok[:, None, :]
        s = jnp.where(valid, s - slopes * (step * d).astype(f32), -jnp.inf)
        m = jnp.max(s, axis=-1, keepdims=True)
        p = jnp.exp(s - m)
        l = jnp.sum(p, axis=-1, keepdims=True)
        o = jnp.einsum('bhrnqs,bhrnsd->bhrnqd', (p / l).astype(v.dtype), vs)
        outs.append(_seq_major(o.reshape(B, H, d, L, hd), sp)[:, :, :S])
        lses.append(_seq_major((m + jnp.log(l)).reshape(B, H, d, L, 1), sp)[:, :, :S])
    wts = jax.nn.softmax(jnp.stack(lses), axis=0)
    o = jnp.sum(wts * jnp.stack(outs).astype(f32), axis=0)
    return o.astype(q.dtype)

def _heads(x, n):
    B, S, _ = x.shape
    return x.reshape(B, S, n, HEAD_DIM).transpose(0, 2, 1, 3)

def _merge(x):
    B, H, S, hd = x.shape
    return x.transpose(0, 2, 1, 3).reshape(B, S, H * hd)

def hybrid_mixer(a, w_in, sinks, gain_a, gain_b, gain_c, w_out):
    B, S, _ = a.shape
    proj = a @ w_in
    offsets = np.cumsum(SPLIT_WIDTHS)[:-1].tolist()
    qa, ka, va, qb, kb, vb, qc, kc, vc = jnp.split(proj, offsets, axis=-1)
    G = A_HEADS // A_KV_HEADS
    qa = qa.reshape(B, S, A_KV_HEADS, G, HEAD_DIM).transpose(0, 2, 3, 1, 4)
    oa = sliding_window_sink_attn(qa, _heads(ka, A_KV_HEADS), _heads(va, A_KV_HEADS), sinks)
    oa = oa.transpose(0, 3, 1, 2, 4).reshape(B, S, A_HEADS * HEAD_DIM)
    ob = _merge(moba_attn(_heads(qb, B_HEADS), _heads(kb, B_HEADS), _heads(vb, B_HEADS)))
    oc = _merge(dilated_mixture_attn(_heads(qc, C_HEADS), _heads(kc, C_HEADS), _heads(vc, C_HEADS)))
    y = jnp.concatenate([rmsnorm(oa, gain_a), rmsnorm(ob, gain_b), rmsnorm(oc, gain_c)], axis=-1)
    return y @ w_out

def memory_cross_attn(h, mem_n, wq, wk, wv, wo):
    B, S, _ = h.shape
    M = mem_n.shape[1]
    q = (h @ wq).reshape(B, S, X_HEADS, X_HEAD_DIM)
    k = (mem_n @ wk).reshape(B, M, X_HEADS, X_HEAD_DIM)
    v = (mem_n @ wv).reshape(B, M, X_HEADS, X_HEAD_DIM)
    s = jnp.einsum('bqhd,bmhd->bhqm', q, k).astype(jnp.float32) * (X_HEAD_DIM ** -0.5)
    p = jax.nn.softmax(s, axis=-1).astype(v.dtype)
    o = jnp.einsum('bhqm,bmhd->bqhd', p, v).reshape(B, S, X_WIDTH)
    return o @ wo

def swiglu(h, w_gate, w_up, w_down):
    return (jax.nn.silu(h @ w_gate) * (h @ w_up)) @ w_down

def setup_inputs(seed: int = 0) -> dict:
    key = jax.random.key(seed)
    ks = jax.random.split(key, 20)
    f32 = jnp.float32

    def w(k, fan_in, fan_out):
        return jax.random.normal(k, (DEPTH, fan_in, fan_out), f32) * fan_in ** -0.5

    def gain(k, n):
        return 1.0 + 0.02 * jax.random.normal(k, (DEPTH, n), f32)

    return {
        'x': jax.random.normal(ks[0], (BATCH, SEQ, D_MODEL), f32),
        'mem': jax.random.normal(ks[1], (BATCH, MEM_LEN, D_MODEL), f32),
        'norm_mix': gain(ks[2], D_MODEL),
        'w_in': w(ks[3], D_MODEL, IN_WIDTH),
        'sinks': 0.5 * jax.random.normal(ks[4], (DEPTH, A_HEADS), f32),
        'gain_a': gain(ks[5], A_HEADS * HEAD_DIM),
        'gain_b': gain(ks[6], B_HEADS * HEAD_DIM),
        'gain_c': gain(ks[7], C_HEADS * HEAD_DIM),
        'w_out': w(ks[8], MIX_WIDTH, D_MODEL),
        'norm_xattn': gain(ks[9], D_MODEL),
        'norm_mem': gain(ks[10], D_MODEL),
        'wq_x': w(ks[11], D_MODEL, X_WIDTH),
        'wk_x': w(ks[12], D_MODEL, X_WIDTH),
        'wv_x': w(ks[13], D_MODEL, X_WIDTH),
        'wo_x': w(ks[14], X_WIDTH, D_MODEL),
        'norm_ffn': gain(ks[15], D_MODEL),
        'w_gate': w(ks[16], D_MODEL, D_FF),
        'w_up': w(ks[17], D_MODEL, D_FF),
        'w_down': w(ks[18], D_FF, D_MODEL),
        'norm_final': 1.0 + 0.02 * jax.random.normal(ks[19], (D_MODEL,), f32),
    }

def reference(x, mem, norm_mix, w_in, sinks, gain_a, gain_b, gain_c, w_out,
              norm_xattn, norm_mem, wq_x, wk_x, wv_x, wo_x,
              norm_ffn, w_gate, w_up, w_down, norm_final):
    h = x
    for l in range(DEPTH):
        a = rmsnorm(h, norm_mix[l])
        h = h + hybrid_mixer(a, w_in[l], sinks[l], gain_a[l], gain_b[l], gain_c[l], w_out[l])
        mem_n = rmsnorm(mem, norm_mem[l])
        h = h + memory_cross_attn(rmsnorm(h, norm_xattn[l]), mem_n, wq_x[l], wk_x[l], wv_x[l], wo_x[l])
        h = h + swiglu(rmsnorm(h, norm_ffn[l]), w_gate[l], w_up[l], w_down[l])
    return rmsnorm(h, norm_final)


_drawn_inputs = setup_inputs


def setup_inputs(seed=0):
    import zlib

    import numpy as np

    out = dict(_drawn_inputs(seed))
    spreads = {}
    factors = {'sinks': 4.393,
     'gain_a': 7.423,
     'gain_b': 7.189,
     'gain_c': 5.29,
     'norm_xattn': 8.0,
     'norm_mem': 8.0,
     'norm_ffn': 4.946,
     'norm_final': 2.917}
    for name, (base, spread) in spreads.items():
        noise = np.random.default_rng([zlib.crc32(name.encode()), seed]).standard_normal(out[name].shape)
        drawn = base * np.exp(spread * noise) if base else spread * noise
        out[name] = __import__('jax').numpy.asarray(drawn.astype(out[name].dtype))
    for name, factor in factors.items():
        out[name] = (out[name] * factor).astype(out[name].dtype)
    return out
```

```python
from contextlib import ExitStack

import concourse.bass as bass
from concourse import mybir

F32 = mybir.dt.float32
F32R = mybir.dt.float32r
ACT = mybir.ActivationFunctionType
ALU = mybir.AluOpType
AX_X = mybir.AxisListType.X

P = 128
SEQ = 512
D_MODEL = 2048
KT = D_MODEL // P
TB = SEQ // P
HEAD_DIM = 64
MEM_LEN = 256
MB = MEM_LEN // P
X_HEADS = 4
D_FF = 5632
FT = D_FF // P
UT = 8
NJ = 4
CH = 4
NCH = FT // CH
EPS = 1e-5
NEG = -1.0e30
LOWEST = -3.0e38
A_PAIRS, B_PAIRS, C_PAIRS = 4, 4, 8
PAIRS = A_PAIRS + B_PAIRS + C_PAIRS
VA_SLOT = PAIRS
MIX_SCALE = HEAD_DIM ** -0.5
X_SCALE = float(P) ** -0.5

Q_V = 0
Q_VA = 6
Q_QA = 7
Q_BC = 9
Q_OUT = Q_BC + B_PAIRS + C_PAIRS
Q_MEM = Q_OUT + KT // 2
Q_XQ = Q_MEM + KT // NJ
Q_XO = Q_XQ + X_HEADS // 2
Q_FFN = Q_XO + 2
N_QUADS = Q_FFN + FT + 2 * NCH

G_MIX, G_OUT, G_X, G_MEM, G_FFN, G_FIN = (KT * n for n in range(6))
N_GAINS = 6 * KT

S_X, S_A, S_B, S_C, S_H1, S_MEM, S_H2, S_FIN = range(1, 9)
R_X, R_XCOL, R_A, R_B, R_C, R_H1, R_MEM, R_MEMCOL, R_H2, R_FIN = range(1, 11)


class Layout:

    def __init__(self, rows, cols, banks):
        self.rows, self.cols, self.banks = rows, cols, banks
        self.widths = [0] * banks
        for _, _, w, c, _ in rows:
            self.widths[c // SEQ] = max(self.widths[c // SEQ], c % SEQ + w)


WINDOWED = Layout(
    rows=[(1, 0, 256, 0, 256), (2, 128, 256, 256, 256), (3, 256, 256, 512, 256), (0, 0, 128, 768, 384)],
    cols={0: (0, 0, 2), 1: (256, 1, 2), 2: (512, 2, 2), 3: (768, 3, 1)}, banks=2)
CAUSAL = Layout(
    rows=[(3, 0, 512, 0, 0), (2, 0, 384, 512, 128), (0, 0, 128, 896, 384), (1, 0, 256, 1024, 256)],
    cols={0: (0, 0, 4), 1: (512, 1, 3), 3: (896, 3, 1), 2: (1024, 2, 2)}, banks=3)
E_COLS = 1280


def build(nc, xT, memT, stream, gains, sinks, bias_table, identity, outT):
    with ExitStack() as ctx:
        def sb(stack, name, shape, dt=F32):
            return stack.enter_context(nc.sbuf_tensor(name, shape, dt))

        def sem(name):
            return ctx.enter_context(nc.semaphore(name))

        w_raw = sb(ctx, "w_raw", [P, NJ, UT * P])
        w_hi = sb(ctx, "w_hi", [P, NJ, UT * P], F32R)
        w_lo = sb(ctx, "w_lo", [P, NJ, UT * P], F32R)
        act_hi = sb(ctx, "act_hi", [P, KT, SEQ], F32R)
        act_lo = sb(ctx, "act_lo", [P, KT, SEQ], F32R)
        rstd = sb(ctx, "rstd", [P, SEQ])
        root = sb(ctx, "root", [P, SEQ])
        square_sum = sb(ctx, "square_sum", [P, 2, SEQ])
        squares = sb(ctx, "squares", [P, 2, SEQ])
        proj_raw = sb(ctx, "proj_raw", [P, SEQ])
        ident = sb(ctx, "ident", [P, P])
        ones = sb(ctx, "ones", [P, P])
        gain = sb(ctx, "gain", [P, N_GAINS])
        sink = sb(ctx, "sink", [P, 2 * A_PAIRS])
        small = sb(ctx, "small", [P, 64])
        eps = small[:, 0:1]
        root_col = small[:, 1:5]
        rstd_col = small[:, 5:9]
        row_max = [small[:, 16 + 4 * h:20 + 4 * h] for h in range(2)]
        neg_max = [small[:, 24 + 4 * h:28 + 4 * h] for h in range(2)]
        row_sum = [small[:, 32 + 4 * h:36 + 4 * h] for h in range(2)]
        row_inv = [small[:, 40 + 4 * h:44 + 4 * h] for h in range(2)]
        sink_arg = [small[:, 48 + 4 * h:52 + 4 * h] for h in range(2)]
        sink_exp = [small[:, 56 + 4 * h:60 + 4 * h] for h in range(2)]

        with ExitStack() as at_start:
            x_raw = sb(at_start, "x_raw", [P, KT, SEQ])
        with ExitStack() as mixing:
            probs = [sb(mixing, f"probs{h}", [P, E_COLS]) for h in range(2)]
            probsT_hi = sb(mixing, "probsT_hi", [P, E_COLS], F32R)
            probsT_lo = sb(mixing, "probsT_lo", [P, E_COLS], F32R)
            q_hi = sb(mixing, "q_hi", [P, SEQ], F32R)
            q_lo = sb(mixing, "q_lo", [P, SEQ], F32R)
            k_hi = sb(mixing, "k_hi", [P, SEQ], F32R)
            k_lo = sb(mixing, "k_lo", [P, SEQ], F32R)
            v_hi = sb(mixing, "v_hi", [P, TB, P], F32R)
            v_lo = sb(mixing, "v_lo", [P, TB, P], F32R)
            bias = sb(mixing, "bias", [P, 2, SEQ])
            vo = sb(mixing, "vo", [P, PAIRS + 1, SEQ])
            out_square_sum = sb(mixing, "out_square_sum", [P, 3, SEQ])
        with ExitStack() as later:
            h = sb(later, "h", [P, KT, SEQ])
            with ExitStack() as crossing:
                km_hi = sb(crossing, "km_hi", [P, X_HEADS, MEM_LEN], F32R)
                km_lo = sb(crossing, "km_lo", [P, X_HEADS, MEM_LEN], F32R)
                vm_hi = sb(crossing, "vm_hi", [P, MB, X_HEADS * P], F32R)
                vm_lo = sb(crossing, "vm_lo", [P, MB, X_HEADS * P], F32R)
                with ExitStack() as loading:
                    mem_raw = sb(loading, "mem_raw", [P, KT, MEM_LEN])
                    mem_hi = sb(loading, "mem_hi", [P, 4, MEM_LEN], F32R)
                    mem_lo = sb(loading, "mem_lo", [P, 4, MEM_LEN], F32R)
                    mem_rstd = sb(loading, "mem_rstd", [P, MEM_LEN])
                with ExitStack() as heads:
                    x_probs = sb(heads, "x_probs", [P, TB, MEM_LEN])
                    xpT_hi = sb(heads, "xpT_hi", [P, MB, SEQ], F32R)
                    xpT_lo = sb(heads, "xpT_lo", [P, MB, SEQ], F32R)
                    xq_hi = sb(heads, "xq_hi", [P, SEQ], F32R)
                    xq_lo = sb(heads, "xq_lo", [P, SEQ], F32R)
                    xo_hi = sb(heads, "xo_hi", [P, X_HEADS, SEQ], F32R)
                    xo_lo = sb(heads, "xo_lo", [P, X_HEADS, SEQ], F32R)
            with ExitStack() as feeding:
                g_hi = sb(feeding, "g_hi", [P, 2 * CH, SEQ], F32R)
                g_lo = sb(feeding, "g_lo", [P, 2 * CH, SEQ], F32R)
                gate_val = sb(feeding, "gate_val", [P, SEQ])
                up_val = sb(feeding, "up_val", [P, SEQ])

        ps = ctx.enter_context(nc.psum_tensor("ps", [P, 8, SEQ], F32))

        w_landed = [sem(f"w_landed{j}") for j in range(NJ)]
        w_hi_done = [sem(f"w_hi_done{j}") for j in range(NJ)]
        w_lo_done = [sem(f"w_lo_done{j}") for j in range(NJ)]
        w_used = [sem(f"w_used{j}") for j in range(NJ)]
        tables_landed = sem("tables_landed")
        x_landed = [sem(f"x_landed{n}") for n in range(8)]
        x_again_landed = sem("x_again_landed")
        mem_landed = sem("mem_landed")
        bias_landed = [sem(f"bias_landed{n}") for n in range(2)]
        consts_set = sem("consts_set")
        act_hi_done = sem("act_hi_done")
        act_lo_done = sem("act_lo_done")
        out_scaled = sem("out_scaled")
        squared = sem("squared")
        square_added = sem("square_added")
        square_sum_clear = sem("square_sum_clear")
        out_squared = sem("out_squared")
        out_square_added = sem("out_square_added")
        norm_summed = sem("norm_summed")
        norm_root = sem("norm_root")
        norm_ready = sem("norm_ready")
        v_copied = sem("v_copied")
        v_hi_done = sem("v_hi_done")
        v_lo_done = sem("v_lo_done")
        proj_raw_done = sem("proj_raw_done")
        proj_hi_done = sem("proj_hi_done")
        proj_lo_done = sem("proj_lo_done")
        scored = [[sem(f"scored{n}_{b}") for b in range(3)] for n in range(2)]
        max_taken = sem("max_taken")
        neg_ready = [sem(f"neg_ready{n}") for n in range(2)]
        exp_done = [sem(f"exp_done{n}") for n in range(2)]
        inv_step = sem("inv_step")
        probs_ready = [sem(f"probs_ready{n}") for n in range(2)]
        turned = [[sem(f"turned{n}_{b}") for b in range(3)] for n in range(2)]
        pT_hi_done = [[sem(f"pT_hi{n}_{b}") for b in range(3)] for n in range(2)]
        pT_lo_done = [[sem(f"pT_lo{n}_{b}") for b in range(3)] for n in range(2)]
        mixed = [sem(f"mixed{n}") for n in range(2)]
        out_copied = [sem(f"out_copied{n}") for n in range(2)]
        h_added = sem("h_added")
        mem_hi_done = sem("mem_hi_done")
        mem_lo_done = sem("mem_lo_done")
        km_raw_done = sem("km_raw_done")
        km_hi_done = sem("km_hi_done")
        km_lo_done = sem("km_lo_done")
        vm_hi_done = sem("vm_hi_done")
        vm_lo_done = sem("vm_lo_done")
        x_scored = sem("x_scored")
        x_neg = sem("x_neg")
        x_exp = sem("x_exp")
        x_ready = sem("x_ready")
        x_turned = sem("x_turned")
        xpT_hi_done = sem("xpT_hi_done")
        xpT_lo_done = sem("xpT_lo_done")
        x_mixed = sem("x_mixed")
        xo_hi_done = sem("xo_hi_done")
        xo_lo_done = sem("xo_lo_done")
        gate_scaled = sem("gate_scaled")
        gate_silu = sem("gate_silu")
        up_scaled = sem("up_scaled")
        g_raw_done = sem("g_raw_done")
        g_hi_done = sem("g_hi_done")
        g_lo_done = sem("g_lo_done")
        out_ready = sem("out_ready")
        out_stored = sem("out_stored")

        def one(ap, i):
            if isinstance(i, int):
                return ap[:, i, :]
            return ap[:, bass.ds(i, 1), :].rearrange("p a n -> p (a n)")

        def passed(eng, semaphore, count):
            if not isinstance(count, int) or count > 0:
                eng.wait_ge(semaphore, count)

        def own_wait(eng, count):
            if not isinstance(count, int):
                eng.wait_ge(tables_landed, 48)

        def in_register(eng, count):
            return count if isinstance(count, int) else eng.snap(eng.to_reg(count))

        def q_event(pair):
            return pair + 2 if isinstance(pair, int) and pair < A_PAIRS else 2 * pair - 2

        def k_event(pair):
            return 1 if isinstance(pair, int) and pair < A_PAIRS else 2 * pair - 1

        def bank_events(pair, b):
            return pair + 1 if b < 2 else pair + 1 - A_PAIRS

        def staged_v(pair):
            return 1 if isinstance(pair, int) and pair < A_PAIRS else pair - A_PAIRS + 2

        def head_bank(n, b):
            return 2 + 3 * n + b

        block = ctx.enter_context(nc.Block())

        @block.sync
        def _(sp):
            for j in range(NJ):
                sp.dma_start(w_raw[:, j, :], stream[j]).then_inc(w_landed[j], 16)
            with sp.Fori(1, N_QUADS) as q:
                for j in range(NJ):
                    sp.wait_ge(w_lo_done[j], q)
                    sp.dma_start(w_raw[:, j, :], stream[bass.ds(q * NJ + j, 1)].rearrange("a p n -> (a p) n"))\
                        .then_inc(w_landed[j], 16)
            for n in range(KT):
                sp.wait_ge(out_ready, n + 1)
                sp.dma_start(outT[n * P:(n + 1) * P, :], h[:, n, :]).then_inc(out_stored, 16)
            sp.wait_ge(out_stored, 16 * KT)

        @block.gpsimd
        def _(pool):
            nc.gpsimd.memset(ones[:, :], 1.0).then_inc(consts_set, 1)
            nc.gpsimd.memset(eps, EPS).then_inc(consts_set, 1)
            nc.gpsimd.memset(square_sum[:, :, :], 0.0).then_inc(square_sum_clear, 1)
            nc.gpsimd.memset(out_square_sum[:, :, :], 0.0).then_inc(square_sum_clear, 1)

            def load_bias(pair):
                for n in range(2):
                    if not isinstance(pair, int) or pair > 0:
                        pool.wait_ge(neg_ready[n], pair)
                    pool.dma_start(bias[:, n, :], bias_table[bass.ds(pair * 2 + n, 1)].rearrange("a p n -> (a p) n"))\
                        .then_inc(bias_landed[n], 16)

            def add_squares(base, slot, width):
                for k in range(KT):
                    pool.wait_ge(squared, base + k + 1)
                    if k:
                        pool.wait_ge(square_added, base + k)
                    nc.gpsimd.tensor_tensor(square_sum[:, slot, :width], square_sum[:, slot, :width],
                                            squares[:, k % 2, :width], ALU.add).then_inc(square_added, 1)

            pool.wait_ge(square_sum_clear, 2)
            add_squares(0, 0, SEQ)
            pool.wait_ge(act_lo_done, KT)
            pool.wait_ge(squared, KT)
            load_bias(0)

            def add_out_squares(group, pair):
                for n in range(2):
                    pool.wait_ge(out_copied[n], pair + 1)
                passed(pool, out_square_added, pair)
                nc.gpsimd.tensor_tensor(squares[:, 0, :], one(vo, pair), one(vo, pair), ALU.mult).then_inc(out_squared, 1)
                pool.wait_ge(out_squared, pair + 1)
                nc.gpsimd.tensor_tensor(out_square_sum[:, group, :], out_square_sum[:, group, :], squares[:, 0, :],
                                        ALU.add).then_inc(out_square_added, 1)

            for pair in range(A_PAIRS):
                load_bias(pair + 1)
                add_out_squares(0, pair)
            with pool.Fori(A_PAIRS, A_PAIRS + B_PAIRS) as pair:
                load_bias(pair + 1)
                add_out_squares(1, pair)
            with pool.Fori(A_PAIRS + B_PAIRS, PAIRS - 1) as pair:
                load_bias(pair + 1)
                add_out_squares(2, pair)
            add_out_squares(2, PAIRS - 1)
            pool.dma_start(h[:, :, :], xT.rearrange("(k p) n -> p k n", p=P)).then_inc(x_again_landed, 16)
            pool.wait_ge(act_lo_done, 2 * KT)
            pool.dma_start(mem_raw[:, :, :], memT.rearrange("(k p) n -> p k n", p=P)).then_inc(mem_landed, 16)
            add_squares(1 * KT, 1, SEQ)
            pool.wait_ge(norm_summed, S_X)
            nc.gpsimd.memset(square_sum[:, 0, :], 0.0).then_inc(square_sum_clear, 1)
            pool.wait_ge(square_sum_clear, 3)
            add_squares(2 * KT, 0, MEM_LEN)
            pool.wait_ge(norm_summed, S_H1)
            nc.gpsimd.memset(square_sum[:, 1, :], 0.0).then_inc(square_sum_clear, 1)
            pool.wait_ge(square_sum_clear, 4)
            add_squares(3 * KT, 1, SEQ)
            pool.wait_ge(norm_summed, S_MEM)
            nc.gpsimd.memset(square_sum[:, 0, :], 0.0).then_inc(square_sum_clear, 1)
            pool.wait_ge(square_sum_clear, 5)
            add_squares(4 * KT, 0, SEQ)

        @block.scalar
        def _(act):
            act.dma_start(gain[:, :], gains).then_inc(tables_landed, 16)
            for c in range(8):
                act.dma_start(x_raw[:, 2 * c:2 * c + 2, :],
                              xT[2 * c * P:(2 * c + 2) * P, :].rearrange("(k p) n -> p k n", p=P))\
                    .then_inc(x_landed[c], 16)
            act.dma_start(sink[:, :], sinks).then_inc(tables_landed, 16)
            act.dma_start(ident[:, :], identity).then_inc(tables_landed, 16)

            def split(q, j):
                act.wait_ge(w_landed[j], q * 16 + 16)
                passed(act, w_used[j], q)
                nc.scalar.activation(w_hi[:, j, :], w_raw[:, j, :], ACT.Copy).then_inc(w_hi_done[j], 1)

            def scaled_hi(k, src, column):
                nc.scalar.activation(one(act_hi, k), src, ACT.Copy, scale=gain_col(column, k)).then_inc(act_hi_done, 1)

            def gain_col(column, k):
                if isinstance(k, int):
                    return gain[:, column + k:column + k + 1]
                return gain[:, bass.ds(k + column, 1)]

            def square(count, src, width=SEQ):
                passed(act, square_added, count - 1)
                nc.scalar.activation(squares[:, count % 2, :width], src, ACT.Square).then_inc(squared, 1)

            def take_root(summed, event, dst, src, n_features):
                act.wait_ge(norm_summed, summed)
                passed(act, norm_ready, event - 1)
                nc.scalar.activation(dst, src, ACT.Sqrt, bias=eps, scale=1.0 / n_features).then_inc(norm_root, 1)

            act.wait_ge(tables_landed, 48)
            act.wait_ge(consts_set, 2)
            for u in range(2 * NJ):
                split(u // NJ, u % NJ)
                act.wait_ge(x_landed[u], 16)
                for k in (2 * u, 2 * u + 1):
                    scaled_hi(k, x_raw[:, k, :], G_MIX)
                    square(k, x_raw[:, k, :])
            for u in range(2 * NJ, Q_VA * NJ + NJ + 2):
                if u == 10:
                    take_root(S_X, R_X, root[:, :], ps[:, 4, :], D_MODEL)
                    take_root(S_X, R_XCOL, root_col, ps[:, 5, 0:TB], D_MODEL)
                split(u // NJ, u % NJ)
                if u % 8 == 3:
                    group = u // 8 - 1
                    act.wait_ge(w_used[3], 2 * group + 2)
                    act.wait_ge(norm_ready, R_XCOL)
                    for b in range(TB):
                        slots = vo[:, A_PAIRS * (group + 1):A_PAIRS * (group + 2), b * P:(b + 1) * P]
                        nc.scalar.activation(slots, ps[:, 4 * (group % 2) + b, :].rearrange("p (s n) -> p s n", n=P),
                                             ACT.Copy, scale=rstd_col[:, b:b + 1]).then_inc(v_copied, 1)
            def copy_va():
                act.wait_ge(w_used[1], Q_VA + 1)
                for b in range(TB):
                    nc.scalar.activation(vo[:, VA_SLOT, b * P:(b + 1) * P], ps[:, 4 + b, 0:P],
                                         ACT.Copy, scale=rstd_col[:, b:b + 1]).then_inc(v_copied, 1)

            def stage_v(pair):
                first = isinstance(pair, int) and pair == 0
                if first:
                    act.wait_ge(v_copied, 4 * TB)
                else:
                    own_wait(act, pair)
                    act.wait_ge(mixed[1], pair)
                src = one(vo, VA_SLOT if first else pair)
                nc.scalar.activation(v_hi[:, :, :].rearrange("p b n -> p (b n)"), src, ACT.Copy).then_inc(v_hi_done, 1)

            def proj_hi(event, dst):
                act.wait_ge(proj_raw_done, event)
                nc.scalar.activation(dst, proj_raw[:, :], ACT.Copy).then_inc(proj_hi_done, 1)

            def exponentials(n, pair, lay, with_sink):
                act.wait_ge(neg_ready[n], pair + 1)
                if with_sink:
                    nc.scalar.activation(sink_exp[n], sink_arg[n], ACT.Exp)
                for i, _, w, c, _ in lay.rows:
                    last = nc.scalar.activation(probs[n][:, c:c + w], probs[n][:, c:c + w], ACT.Exp,
                                                bias=neg_max[n][:, i:i + 1], accum_out=row_sum[n][:, i:i + 1])
                last.then_inc(exp_done[n], 1)

            def turned_hi(n, pair, lay):
                for b in range(lay.banks):
                    act.wait_ge(turned[n][b], bank_events(pair, b))
                    w = lay.widths[b]
                    nc.scalar.activation(probsT_hi[:, b * SEQ:b * SEQ + w], ps[:, head_bank(n, b), :w], ACT.Copy)\
                        .then_inc(pT_hi_done[n][b], 1)

            def copy_out(n, pair):
                own_wait(act, pair)
                act.wait_ge(mixed[n], pair + 1)
                rows = slice(n * HEAD_DIM, (n + 1) * HEAD_DIM)
                dst = vo[rows, pair, :] if isinstance(pair, int) else \
                    vo[rows, bass.ds(pair, 1), :].rearrange("p a n -> p (a n)")
                nc.scalar.activation(dst, ps[rows, head_bank(n, 2), :], ACT.Copy).then_inc(out_copied[n], 1)

            copy_va()
            proj_hi(1, k_hi[:, :])
            for q, j in ((Q_QA, 2), (Q_QA, 3)):
                split(q, j)
            proj_hi(2, q_hi[:, :])
            for j in range(2):
                split(Q_QA + 1, j)
            for pair in range(A_PAIRS):
                if pair == 0:
                    stage_v(0)
                for n in range(2):
                    exponentials(n, pair, WINDOWED, True)
                if pair < A_PAIRS - 1:
                    a, b = (2, 3) if pair % 2 == 0 else (0, 1)
                    q = Q_QA + (pair + 1) // 2
                    split(q + 1, a)
                    turned_hi(0, pair, WINDOWED)
                    split(q + 1, b)
                    proj_hi(q_event(pair + 1), q_hi[:, :])
                    copy_out(0, pair)
                    turned_hi(1, pair, WINDOWED)
                    copy_out(1, pair)
                else:
                    split(Q_BC + 1, 0)
                    proj_hi(q_event(pair + 1), q_hi[:, :])
                    split(Q_BC + 1, 1)
                    turned_hi(0, pair, WINDOWED)
                    split(Q_BC + 1, 2)
                    copy_out(0, pair)
                    turned_hi(1, pair, WINDOWED)
                    proj_hi(k_event(pair + 1), k_hi[:, :])
                    split(Q_BC + 1, 3)
                    copy_out(1, pair)
            with act.Fori(A_PAIRS, PAIRS - 1) as pair:
                q = pair + (Q_BC + 2 - A_PAIRS)
                stage_v(pair)
                for n in range(2):
                    exponentials(n, pair, CAUSAL, False)
                split(q, 0)
                proj_hi(q_event(pair + 1), q_hi[:, :])
                split(q, 1)
                turned_hi(0, pair, CAUSAL)
                split(q, 2)
                copy_out(0, pair)
                turned_hi(1, pair, CAUSAL)
                proj_hi(k_event(pair + 1), k_hi[:, :])
                split(q, 3)
                copy_out(1, pair)
            last_pair = PAIRS - 1
            stage_v(last_pair)
            for n in range(2):
                exponentials(n, last_pair, CAUSAL, False)
            take_root(S_A, R_A, root[:, :], ps[:, 0, :], A_PAIRS * P)
            turned_hi(0, last_pair, CAUSAL)
            copy_out(0, last_pair)
            turned_hi(1, last_pair, CAUSAL)
            take_root(S_B, R_B, root[:, :], ps[:, 1, :], B_PAIRS * P)
            copy_out(1, last_pair)

            def out_hi(t):
                act.wait_ge(out_scaled, t + 1)
                scaled_hi(t, vo[:, t, :], G_OUT)

            for t in range(A_PAIRS + B_PAIRS):
                out_hi(t)
            take_root(S_C, R_C, root[:, :], ps[:, 5, :], C_PAIRS * P)
            for t in range(A_PAIRS + B_PAIRS, PAIRS):
                out_hi(t)

            def square_h(count, n):
                act.wait_ge(square_added, count - 1)
                nc.scalar.activation(squares[:, n % 2 if isinstance(n, int) else 0, :], one(h, n), ACT.Square)\
                    .then_inc(squared, 1)

            with act.Fori(0, KT // 2) as g:
                q = g + (Q_OUT + 1)
                for j in range(3):
                    split(q, j)
                for m in range(2):
                    if m:
                        split(q, 3)
                    own_wait(act, g)
                    act.wait_ge(h_added, g * 2 + (m + 1))
                    act.wait_ge(square_added, g * 2 + (KT + m - 1))
                    nc.scalar.activation(squares[:, m, :], one(h, g * 2 + m), ACT.Square).then_inc(squared, 1)

            def mem_part(k):
                if k >= 4:
                    act.wait_ge(w_used[k % NJ], Q_MEM + k // NJ)
                nc.scalar.activation(mem_hi[:, k % 4, :], mem_raw[:, k, :], ACT.Copy,
                                     scale=gain_col(G_MEM, k)).then_inc(mem_hi_done, 1)

            act.wait_ge(mem_landed, 16)
            for k in range(4):
                mem_part(k)
            act.wait_ge(w_used[3], Q_MEM)
            for k in range(KT):
                split(Q_MEM + 1 + k // NJ, k % NJ)
                if k + 4 < KT:
                    mem_part(k + 4)
                scaled_hi(k, h[:, k, :], G_X)
                square(2 * KT + k, mem_raw[:, k, :], MEM_LEN)
                if k == 7:
                    take_root(S_H1, R_H1, root[:, :], ps[:, 0, :], D_MODEL)
            take_root(S_MEM, R_MEM, root[:, :MEM_LEN], ps[:, 1, :MEM_LEN], D_MODEL)
            take_root(S_MEM, R_MEMCOL, root_col[:, :MB], ps[:, 1, MEM_LEN:MEM_LEN + MB], D_MODEL)
            act.wait_ge(norm_ready, R_MEMCOL)
            for b in range(MB):
                nc.scalar.activation(vm_hi[:, b, :], ps[:, 6 + b, :], ACT.Copy,
                                     scale=rstd_col[:, b:b + 1]).then_inc(vm_hi_done, 1)
            for n in range(X_HEADS):
                act.wait_ge(km_raw_done, n + 1)
                nc.scalar.activation(km_hi[:, n, :], proj_raw[:, (n % 2) * MEM_LEN:(n % 2 + 1) * MEM_LEN], ACT.Copy)\
                    .then_inc(km_hi_done, 1)

            def x_exponentials(n):
                act.wait_ge(x_neg, n + 1)
                for i in range(TB):
                    last = nc.scalar.activation(x_probs[:, i, :], ps[:, 2 + i // 2, (i % 2) * MEM_LEN:(i % 2 + 1) * MEM_LEN],
                                                ACT.Exp, bias=neg_max[0][:, i:i + 1], accum_out=row_sum[0][:, i:i + 1])
                last.then_inc(x_exp, 1)

            def x_turned_hi(n):
                act.wait_ge(x_turned, n + 1)
                for b in range(MB):
                    nc.scalar.activation(xpT_hi[:, b, :], ps[:, 4 + b, :], ACT.Copy).then_inc(xpT_hi_done, 1)

            def x_out_hi(n):
                act.wait_ge(x_mixed, n + 1)
                nc.scalar.activation(xo_hi[:, n, :], ps[:, 6 + n % 2, :], ACT.Copy).then_inc(xo_hi_done, 1)

            for n in range(X_HEADS):
                for j in (2 * (n % 2), 2 * (n % 2) + 1):
                    split(Q_XQ + n // 2 + 1, j)
                proj_hi(k_event(last_pair) + n + 1, xq_hi[:, :])
                if n >= 2:
                    x_out_hi(n - 2)
                if n >= 1:
                    x_turned_hi(n - 1)
                x_exponentials(n)
            x_out_hi(X_HEADS - 2)
            x_turned_hi(X_HEADS - 1)
            x_out_hi(X_HEADS - 1)

            for u in range(KT // 2):
                split(Q_XO + 1 + u // NJ, u % NJ)
                for n in (2 * u, 2 * u + 1):
                    act.wait_ge(h_added, KT + n + 1)
                    scaled_hi(n, h[:, n, :], G_FFN)
                    square_h(3 * KT + n, n)

            def gate_up(c, f, q):
                tile = c * CH + f
                split(q + 1, 0)
                split(q + 1, 1)
                act.wait_ge(gate_scaled, tile + 1)
                nc.scalar.activation(gate_val[:, :], gate_val[:, :], ACT.Silu).then_inc(gate_silu, 1)
                split(q + 1, 2)
                split(q + 1, 3)
                own_wait(act, c)
                act.wait_ge(g_raw_done, tile + 1)
                nc.scalar.activation(one(g_hi, (c % 2) * CH + f), up_val[:, :], ACT.Copy).then_inc(g_hi_done, 1)

            for f in range(CH):
                if f == 0:
                    take_root(S_H2, R_H2, root[:, :], ps[:, 0, :], D_MODEL)
                gate_up(0, f, Q_FFN + f)
            with act.Fori(0, NCH - 1) as c:
                q = c * (CH + 2) + (Q_FFN + CH)
                for f in range(CH):
                    gate_up(c + 1, f, q + f)
                for u in range(2 * NJ):
                    split(q + (CH + 1 + u // NJ), u % NJ)
            for u in range(2 * NJ):
                if u < NJ:
                    split(N_QUADS - 1, u)
                for n in (2 * u, 2 * u + 1):
                    act.wait_ge(h_added, (2 + NCH - 1) * KT + n + 1)
                    square_h(4 * KT + n, n)
            take_root(S_FIN, R_FIN, root[:, :], ps[:, 4, :], D_MODEL)

        @block.vector
        def _(dve):
            def split(q, j):
                dve.wait_ge(w_hi_done[j], q + 1)
                nc.vector.tensor_tensor(w_lo[:, j, :], w_raw[:, j, :], w_hi[:, j, :].bitcast(F32), ALU.subtract)\
                    .then_inc(w_lo_done[j], 1)

            def scaled_lo(event, k, src, column):
                dve.wait_ge(act_hi_done, event)
                nc.vector.scalar_tensor_tensor(act_lo[:, k, :], src, gain[:, column + k:column + k + 1],
                                               act_hi[:, k, :].bitcast(F32), ALU.mult, ALU.subtract)\
                    .then_inc(act_lo_done, 1)

            def invert(event, dst, src):
                dve.wait_ge(norm_root, event)
                nc.vector.reciprocal(dst, src).then_inc(norm_ready, 1)

            dve.wait_ge(tables_landed, 48)
            for u in range(2 * NJ):
                split(u // NJ, u % NJ)
                dve.wait_ge(x_landed[u], 16)
                for k in (2 * u, 2 * u + 1):
                    scaled_lo(k + 1, k, x_raw[:, k, :], G_MIX)
            for u in range(2 * NJ, Q_VA * NJ + NJ + 2):
                if u == 10:
                    invert(R_X, rstd[:, :], root[:, :])
                    invert(R_XCOL, rstd_col, root_col)
                split(u // NJ, u % NJ)

            def stage_v(pair):
                dve.wait_ge(v_hi_done, staged_v(pair))
                first = isinstance(pair, int) and pair == 0
                nc.vector.tensor_tensor(v_lo[:, :, :].rearrange("p b n -> p (b n)"), one(vo, VA_SLOT if first else pair),
                                        v_hi[:, :, :].rearrange("p b n -> p (b n)").bitcast(F32), ALU.subtract)\
                    .then_inc(v_lo_done, 1)

            def proj_scaled(event, q, j, bank, scale):
                dve.wait_ge(w_used[j], q + 1)
                passed(dve, proj_lo_done, event - 1)
                nc.vector.scalar_tensor_tensor(proj_raw[:, :], ps[:, bank, :], scale, rstd[:, :], ALU.mult, ALU.mult)\
                    .then_inc(proj_raw_done, 1)

            def proj_lo(event, lo, hi):
                dve.wait_ge(proj_hi_done, event)
                nc.vector.tensor_tensor(lo, proj_raw[:, :], hi.bitcast(F32), ALU.subtract).then_inc(proj_lo_done, 1)

            def maxima(n, pair, lay, with_sink):
                landed = in_register(dve, pair * 16 + 16)
                counts = [in_register(dve, bank_events(pair, b)) for b in range(lay.banks)]
                bank = -1
                for at, (i, _, w, c, bias_at) in enumerate(lay.rows):
                    if c // SEQ != bank:
                        bank = c // SEQ
                        own_wait(dve, pair)
                        if at == 0:
                            dve.wait_ge(bias_landed[n], landed)
                        dve.wait_ge(scored[n][bank], counts[bank])
                    first = sink[:, 2 * pair + n:2 * pair + n + 1] if with_sink else LOWEST
                    nc.vector.tensor_tensor_reduce(probs[n][:, c:c + w], ps[:, head_bank(n, bank), c % SEQ:c % SEQ + w],
                                                   bias[:, n, bias_at:bias_at + w], 1.0, first, ALU.add, ALU.max,
                                                   row_max[n][:, i:i + 1]).then_inc(max_taken, 1)
                dve.wait_ge(max_taken, pair * (2 * TB) + (n + 1) * TB)
                last = nc.vector.tensor_scalar(neg_max[n], row_max[n], -1.0, None, ALU.mult)
                if with_sink:
                    last.then_inc(inv_step, 1)
                    dve.wait_ge(inv_step, 6 * pair + n + 1)
                    last = nc.vector.tensor_scalar(sink_arg[n], neg_max[n], sink[:, 2 * pair + n:2 * pair + n + 1],
                                                   None, ALU.add)
                last.then_inc(neg_ready[n], 1)

            def normalize(n, pair, lay, with_sink):
                dve.wait_ge(exp_done[n], pair + 1)
                if with_sink:
                    nc.vector.tensor_tensor(row_sum[n], row_sum[n], sink_exp[n], ALU.add).then_inc(inv_step, 1)
                    steps = 6 * pair + 2 * n + 3
                    dve.wait_ge(inv_step, steps)
                else:
                    steps = pair * 2 + (6 * A_PAIRS - 2 * A_PAIRS + n)
                nc.vector.reciprocal(row_inv[n], row_sum[n]).then_inc(inv_step, 1)
                dve.wait_ge(inv_step, steps + 1)
                for i, _, w, c, _ in lay.rows:
                    last = nc.vector.tensor_scalar(probs[n][:, c:c + w], probs[n][:, c:c + w], row_inv[n][:, i:i + 1],
                                                   None, ALU.mult)
                last.then_inc(probs_ready[n], 1)

            def turned_lo(n, pair, lay):
                for b in range(lay.banks):
                    dve.wait_ge(pT_hi_done[n][b], bank_events(pair, b))
                    w = lay.widths[b]
                    nc.vector.tensor_tensor(probsT_lo[:, b * SEQ:b * SEQ + w], ps[:, head_bank(n, b), :w],
                                            probsT_hi[:, b * SEQ:b * SEQ + w].bitcast(F32), ALU.subtract)\
                        .then_inc(pT_lo_done[n][b], 1)

            proj_scaled(1, Q_VA, 3, 1, 1.0)
            proj_lo(1, k_lo[:, :], k_hi[:, :])
            for q, j in ((Q_QA, 2), (Q_QA, 3)):
                split(q, j)
            proj_scaled(2, Q_QA, 1, 0, MIX_SCALE)
            proj_lo(2, q_lo[:, :], q_hi[:, :])
            for j in range(2):
                split(Q_QA + 1, j)
            for pair in range(A_PAIRS):
                if pair == 0:
                    stage_v(0)
                for n in range(2):
                    maxima(n, pair, WINDOWED, True)
                for n in range(2):
                    normalize(n, pair, WINDOWED, True)
                e = q_event(pair + 1)
                if pair < A_PAIRS - 1:
                    a, b = (2, 3) if pair % 2 == 0 else (0, 1)
                    q = Q_QA + (pair + 1) // 2
                    split(q + 1, a)
                    turned_lo(0, pair, WINDOWED)
                    split(q + 1, b)
                    proj_scaled(e, q, b, 0, MIX_SCALE)
                    proj_lo(e, q_lo[:, :], q_hi[:, :])
                    turned_lo(1, pair, WINDOWED)
                else:
                    split(Q_BC + 1, 0)
                    proj_scaled(e, Q_BC, 1, 0, MIX_SCALE)
                    proj_lo(e, q_lo[:, :], q_hi[:, :])
                    split(Q_BC + 1, 1)
                    turned_lo(0, pair, WINDOWED)
                    split(Q_BC + 1, 2)
                    turned_lo(1, pair, WINDOWED)
                    proj_scaled(e + 1, Q_BC, 3, 1, 1.0)
                    proj_lo(e + 1, k_lo[:, :], k_hi[:, :])
                    split(Q_BC + 1, 3)
            with dve.Fori(A_PAIRS, PAIRS - 1) as pair:
                q = pair + (Q_BC + 1 - A_PAIRS)
                for n in range(2):
                    maxima(n, pair, CAUSAL, False)
                    if n == 0:
                        stage_v(pair)
                for n in range(2):
                    normalize(n, pair, CAUSAL, False)
                split(q + 1, 0)
                proj_scaled(q_event(pair + 1), q, 1, 0, MIX_SCALE)
                proj_lo(q_event(pair + 1), q_lo[:, :], q_hi[:, :])
                split(q + 1, 1)
                turned_lo(0, pair, CAUSAL)
                split(q + 1, 2)
                turned_lo(1, pair, CAUSAL)
                proj_scaled(k_event(pair + 1), q, 3, 1, 1.0)
                proj_lo(k_event(pair + 1), k_lo[:, :], k_hi[:, :])
                split(q + 1, 3)
            last_pair = PAIRS - 1
            for n in range(2):
                maxima(n, last_pair, CAUSAL, False)
            stage_v(last_pair)
            for n in range(2):
                normalize(n, last_pair, CAUSAL, False)

            def scale_out(t):
                nc.vector.tensor_tensor(vo[:, t, :], vo[:, t, :], rstd[:, :], ALU.mult).then_inc(out_scaled, 1)

            def out_lo(t):
                scaled_lo(KT + t + 1, t, vo[:, t, :], G_OUT)

            turned_lo(0, last_pair, CAUSAL)
            invert(R_A, rstd[:, :], root[:, :])
            turned_lo(1, last_pair, CAUSAL)
            dve.wait_ge(norm_ready, R_A)
            for t in range(A_PAIRS):
                scale_out(t)
            dve.wait_ge(out_scaled, A_PAIRS)
            invert(R_B, rstd[:, :], root[:, :])
            dve.wait_ge(norm_ready, R_B)
            for t in range(A_PAIRS, A_PAIRS + B_PAIRS):
                scale_out(t)
            for t in range(A_PAIRS + B_PAIRS):
                out_lo(t)
            dve.wait_ge(out_scaled, A_PAIRS + B_PAIRS)
            invert(R_C, rstd[:, :], root[:, :])
            dve.wait_ge(norm_ready, R_C)
            for t in range(A_PAIRS + B_PAIRS, PAIRS):
                scale_out(t)
                if t > A_PAIRS + B_PAIRS:
                    out_lo(t - 1)
            out_lo(PAIRS - 1)

            def add_to_h(n, bank):
                nc.vector.tensor_tensor(one(h, n), ps[:, bank, :], one(h, n), ALU.add).then_inc(h_added, 1)

            dve.wait_ge(x_again_landed, 16)
            with dve.Fori(0, KT // 2) as g:
                q = g + Q_OUT
                split(q + 1, 0)
                split(q + 1, 1)
                for m in range(2):
                    dve.wait_ge(w_used[2 + m], q + 1)
                    add_to_h(g * 2 + m, m)
                    split(q + 1, 2 + m)

            def mem_part(k):
                dve.wait_ge(mem_hi_done, k + 1)
                nc.vector.scalar_tensor_tensor(mem_lo[:, k % 4, :], mem_raw[:, k, :], gain[:, G_MEM + k:G_MEM + k + 1],
                                               mem_hi[:, k % 4, :].bitcast(F32), ALU.mult, ALU.subtract)\
                    .then_inc(mem_lo_done, 1)

            for k in range(4):
                mem_part(k)
            for k in range(KT):
                split(Q_MEM + 1 + k // NJ, k % NJ)
                if k + 4 < KT:
                    mem_part(k + 4)
                scaled_lo(2 * KT + k + 1, k, h[:, k, :], G_X)
                if k == 7:
                    invert(R_H1, rstd[:, :], root[:, :])
            invert(R_MEM, mem_rstd[:, :], root[:, :MEM_LEN])
            invert(R_MEMCOL, rstd_col[:, :MB], root_col[:, :MB])
            dve.wait_ge(norm_ready, R_MEMCOL)
            for b in range(MB):
                dve.wait_ge(vm_hi_done, b + 1)
                nc.vector.scalar_tensor_tensor(vm_lo[:, b, :], ps[:, 6 + b, :], rstd_col[:, b:b + 1],
                                               vm_hi[:, b, :].bitcast(F32), ALU.mult, ALU.subtract)\
                    .then_inc(vm_lo_done, 1)
            for n in range(X_HEADS):
                half = proj_raw[:, (n % 2) * MEM_LEN:(n % 2 + 1) * MEM_LEN]
                if n >= 2:
                    dve.wait_ge(km_lo_done, n - 1)
                nc.vector.tensor_tensor(half, ps[:, 2 + n, :MEM_LEN], mem_rstd[:, :], ALU.mult).then_inc(km_raw_done, 1)
                if n >= 1:
                    m = n - 1
                    dve.wait_ge(km_hi_done, m + 1)
                    nc.vector.tensor_tensor(km_lo[:, m, :], proj_raw[:, (m % 2) * MEM_LEN:(m % 2 + 1) * MEM_LEN],
                                            km_hi[:, m, :].bitcast(F32), ALU.subtract).then_inc(km_lo_done, 1)
            dve.wait_ge(km_hi_done, X_HEADS)
            nc.vector.tensor_tensor(km_lo[:, 3, :], proj_raw[:, MEM_LEN:], km_hi[:, 3, :].bitcast(F32), ALU.subtract)\
                .then_inc(km_lo_done, 1)
            dve.wait_ge(km_lo_done, X_HEADS)

            x_steps = 0

            def x_maxima(n):
                dve.wait_ge(x_scored, n + 1)
                nc.vector.tensor_reduce(row_max[0], ps[:, 2:4, :].rearrange("p b (i n) -> p (b i) n", n=MEM_LEN),
                                        AX_X, ALU.max).then_inc(max_taken, 1)
                dve.wait_ge(max_taken, PAIRS * 2 * TB + n + 1)
                nc.vector.tensor_scalar(neg_max[0], row_max[0], -1.0, None, ALU.mult).then_inc(x_neg, 1)

            def x_normalize(n):
                dve.wait_ge(x_exp, n + 1)
                nc.vector.reciprocal(row_inv[0], row_sum[0]).then_inc(inv_step, 1)
                dve.wait_ge(inv_step, 6 * A_PAIRS + 2 * (B_PAIRS + C_PAIRS) + n + 1)
                for i in range(TB):
                    last = nc.vector.tensor_scalar(x_probs[:, i, :], x_probs[:, i, :], row_inv[0][:, i:i + 1], None,
                                                   ALU.mult)
                last.then_inc(x_ready, 1)

            def x_turned_lo(n):
                for b in range(MB):
                    dve.wait_ge(xpT_hi_done, MB * n + b + 1)
                    nc.vector.tensor_tensor(xpT_lo[:, b, :], ps[:, 4 + b, :], xpT_hi[:, b, :].bitcast(F32),
                                            ALU.subtract).then_inc(xpT_lo_done, 1)

            def x_out_lo(n):
                dve.wait_ge(xo_hi_done, n + 1)
                nc.vector.tensor_tensor(xo_lo[:, n, :], ps[:, 6 + n % 2, :], xo_hi[:, n, :].bitcast(F32), ALU.subtract)\
                    .then_inc(xo_lo_done, 1)

            for n in range(X_HEADS):
                j = 2 * (n % 2)
                split(Q_XQ + n // 2 + 1, j)
                split(Q_XQ + n // 2 + 1, j + 1)
                e = k_event(last_pair) + n + 1
                proj_scaled(e, Q_XQ + n // 2, j + 1, n % 2, X_SCALE)
                proj_lo(e, xq_lo[:, :], xq_hi[:, :])
                if n >= 2:
                    x_out_lo(n - 2)
                if n >= 1:
                    x_turned_lo(n - 1)
                x_maxima(n)
                x_normalize(n)
            x_out_lo(X_HEADS - 2)
            x_turned_lo(X_HEADS - 1)
            x_out_lo(X_HEADS - 1)

            for u in range(KT // 2):
                dve.wait_ge(w_used[u % NJ], Q_XO + u // NJ + 1)
                for m in range(2):
                    add_to_h(2 * u + m, 2 * (u % 2) + m)
                split(Q_XO + 1 + u // NJ, u % NJ)
                for n in (2 * u, 2 * u + 1):
                    scaled_lo(3 * KT + n + 1, n, h[:, n, :], G_FFN)

            def gate_up(c, f, q):
                tile = c * CH + f
                split(q + 1, 0)
                split(q + 1, 1)
                dve.wait_ge(w_used[1], q + 1)
                passed(dve, g_lo_done, tile)
                nc.vector.tensor_tensor(gate_val[:, :], ps[:, 4 + f % 2, :], rstd[:, :], ALU.mult)\
                    .then_inc(gate_scaled, 1)
                split(q + 1, 2)
                dve.wait_ge(w_used[3], q + 1)
                nc.vector.tensor_tensor(up_val[:, :], ps[:, 6 + f % 2, :], rstd[:, :], ALU.mult).then_inc(up_scaled, 1)
                dve.wait_ge(up_scaled, tile + 1)
                dve.wait_ge(gate_silu, tile + 1)
                nc.vector.tensor_tensor(up_val[:, :], gate_val[:, :], up_val[:, :], ALU.mult).then_inc(g_raw_done, 1)
                split(q + 1, 3)
                dve.wait_ge(g_hi_done, tile + 1)
                slot = (c % 2) * CH + f
                nc.vector.tensor_tensor(one(g_lo, slot), up_val[:, :], one(g_hi, slot).bitcast(F32), ALU.subtract)\
                    .then_inc(g_lo_done, 1)

            def down(q, with_split):
                for u in range(2 * NJ):
                    dve.wait_ge(w_used[u % NJ], q + (u // NJ + 1))
                    for m in range(2):
                        add_to_h(2 * u + m, 2 * (u % 2) + m)
                    if with_split or u < NJ:
                        split(q + (1 + u // NJ), u % NJ)

            for f in range(CH):
                if f == 0:
                    invert(R_H2, rstd[:, :], root[:, :])
                    dve.wait_ge(norm_ready, R_H2)
                gate_up(0, f, Q_FFN + f)
            with dve.Fori(0, NCH - 1) as c:
                q = c * (CH + 2) + (Q_FFN + CH)
                for f in range(CH):
                    gate_up(c + 1, f, q + f)
                down(q + CH, True)
            down(N_QUADS - 2, False)
            invert(R_FIN, rstd[:, :], root[:, :])
            dve.wait_ge(norm_ready, R_FIN)
            for n in range(KT):
                nc.vector.scalar_tensor_tensor(h[:, n, :], h[:, n, :], gain[:, G_FIN + n:G_FIN + n + 1], rstd[:, :],
                                               ALU.mult, ALU.mult).then_inc(out_ready, 1)

        @block.tensor
        def _(pe):
            def product(out, l_hi, l_lo, r_hi, r_lo, start, stop, **more):
                nc.tensor.matmul(out, l_hi, r_hi, start=start, stop=False, **more)
                nc.tensor.matmul(out, l_hi, r_lo, start=False, stop=False, **more)
                return nc.tensor.matmul(out, l_lo, r_hi, start=False, stop=stop, **more)

            def unit_ready(q, j):
                pe.wait_ge(w_lo_done[j], q + 1)

            def feature_unit(q, j, bank, half, act_event=None):
                unit_ready(q, j)
                for t in range(UT):
                    k = UT * half + t
                    if act_event is not None:
                        pe.wait_ge(act_lo_done, act_event + k + 1)
                    cols = slice(t * P, (t + 1) * P)
                    last = product(ps[:, bank, :], w_hi[:, j, cols], w_lo[:, j, cols], act_hi[:, k, :], act_lo[:, k, :],
                                   k == 0, k == KT - 1)
                last.then_inc(w_used[j], 1)

            def sum_squares(sums, bank, width=SEQ, cols=None):
                last = nc.tensor.matmul(ps[:, bank, :width], ones[:, :], sums, start=True, stop=True)
                if cols:
                    at, first, blocks = cols
                    for b in range(blocks):
                        last = nc.tensor.matmul(ps[:, at, first + b:first + b + 1], sums[:, b * P:(b + 1) * P],
                                                ones[:, 0:1], start=True, stop=True)
                last.then_inc(norm_summed, 1)

            for group in range(3):
                if group == 1:
                    pe.wait_ge(square_added, KT)
                    pe.wait_ge(consts_set, 2)
                    sum_squares(square_sum[:, 0, :], 4, cols=(5, 0, TB))
                    pe.wait_ge(norm_root, R_XCOL)
                if group == 2:
                    pe.wait_ge(v_copied, TB)
                for u in range(2 * NJ):
                    q, j = 2 * group + u // NJ, u % NJ
                    unit_ready(q, j)
                    for b in range(TB):
                        for t in range(2):
                            k = 2 * u + t
                            if group == 0 and b == 0:
                                pe.wait_ge(act_lo_done, k + 1)
                            tok = slice(b * P, (b + 1) * P)
                            cols = slice(t * SEQ, (t + 1) * SEQ)
                            last = product(ps[:, 4 * (group % 2) + b, :], act_hi[:, k, tok], act_lo[:, k, tok],
                                           w_hi[:, j, cols], w_lo[:, j, cols], k == 0, k == KT - 1)
                    last.then_inc(w_used[j], 1)
            pe.wait_ge(v_copied, 2 * TB)
            for u in range(2):
                unit_ready(Q_VA, u)
                for b in range(TB):
                    for t in range(UT):
                        k = UT * u + t
                        tok = slice(b * P, (b + 1) * P)
                        cols = slice(t * P, (t + 1) * P)
                        last = product(ps[:, 4 + b, :P], act_hi[:, k, tok], act_lo[:, k, tok],
                                       w_hi[:, u, cols], w_lo[:, u, cols], k == 0, k == KT - 1)
                last.then_inc(w_used[u], 1)
            pe.wait_ge(v_copied, 3 * TB)
            for half in range(2):
                feature_unit(Q_VA, 2 + half, 1, half)
            for half in range(2):
                feature_unit(Q_QA, half, 0, half)

            def scores(n, pair, lay):
                rows = slice(n * HEAD_DIM, (n + 1) * HEAD_DIM)
                for at, (i, first_key, w, c, _) in enumerate(lay.rows):
                    b = c // SEQ
                    if b == 2:
                        pe.wait_ge(out_copied[n], pair)
                    tok = slice(i * P, (i + 1) * P)
                    keys = slice(first_key, first_key + w)
                    last = product(ps[:, head_bank(n, b), c % SEQ:c % SEQ + w], q_hi[rows, tok], q_lo[rows, tok],
                                   k_hi[rows, keys], k_lo[rows, keys], True, True)
                    if at == len(lay.rows) - 1 or lay.rows[at + 1][3] // SEQ != b:
                        last.then_inc(scored[n][b], 1)

            def turn(n, pair, lay):
                pe.wait_ge(probs_ready[n], pair + 1)
                blocks = []
                for j, (c, i0, count) in lay.cols.items():
                    for i in range(i0, i0 + count):
                        first_key, at = next((r[1], r[3]) for r in lay.rows if r[0] == i)
                        blocks.append((c + (i - i0) * P, at + j * P - first_key))
                blocks.sort()
                for x, (dst, src) in enumerate(blocks):
                    b = dst // SEQ
                    last = nc.tensor.transpose(ps[:, head_bank(n, b), dst % SEQ:dst % SEQ + P], probs[n][:, src:src + P],
                                               ident[:, :])
                    if x == len(blocks) - 1 or blocks[x + 1][0] // SEQ != b:
                        last.then_inc(turned[n][b], 1)

            def mix(n, pair, lay):
                out = ps[:, head_bank(n, 2), :]
                if lay.banks < 3 and pair > 0:
                    pe.wait_ge(out_copied[n], pair)
                for b in reversed(range(lay.banks)):
                    pe.wait_ge(pT_lo_done[n][b], bank_events(pair, b))
                order = sorted(lay.cols)
                for j in order:
                    c, i0, count = lay.cols[j]
                    w = count * P
                    last = product(out[:, i0 * P:i0 * P + w], v_hi[:, j, :], v_lo[:, j, :],
                                   probsT_hi[:, c:c + w], probsT_lo[:, c:c + w], j == order[0], j == order[-1],
                                   skip_group_check=True)
                last.then_inc(mixed[n], 1)

            def attend(pair, lay, k_count, fill):
                pe.wait_ge(proj_lo_done, k_count)
                for n in range(2):
                    scores(n, pair, lay)
                fill(0)
                turn(0, pair, lay)
                fill(1)
                pe.wait_ge(v_lo_done, staged_v(pair))
                mix(0, pair, lay)
                turn(1, pair, lay)
                fill(2)
                mix(1, pair, lay)

            def bc_fill(q):
                def fill(part):
                    for j in ((0, 1), (2,), (3,))[part]:
                        feature_unit(q, j, j // 2, j % 2)
                return fill

            for pair in range(A_PAIRS):
                if pair < A_PAIRS - 1:
                    j0, q = (2, 0)[pair % 2], Q_QA + (pair + 1) // 2

                    def fill(part):
                        if part < 2:
                            feature_unit(q, j0 + part, 0, part)
                else:
                    fill = bc_fill(Q_BC)
                attend(pair, WINDOWED, q_event(pair), fill)
            with pe.Fori(A_PAIRS, PAIRS - 1) as pair:
                attend(pair, CAUSAL, k_event(pair), bc_fill(pair + (Q_BC + 1 - A_PAIRS)))

            def last_fill(part):
                if part == 0:
                    for group, bank in ((0, 0), (1, 1)):
                        pe.wait_ge(out_square_added, A_PAIRS * (group + 1))
                        sum_squares(out_square_sum[:, group, :], bank)

            attend(PAIRS - 1, CAUSAL, k_event(PAIRS - 1), last_fill)

            def out_quad(g, between):
                q = g + Q_OUT
                for half in range(2):
                    for m in range(2):
                        if half == 0 and (not isinstance(g, int) or g > 0):
                            pe.wait_ge(h_added, g * 2 + (m - 1))
                        feature_unit(q, 2 * half + m, m, half, KT if isinstance(g, int) else None)
                    if half == 0:
                        between()

            def sum_c():
                pe.wait_ge(out_square_added, PAIRS)
                sum_squares(out_square_sum[:, 2, :], 5)

            out_quad(0, sum_c)
            with pe.Fori(1, KT // 2) as g:
                out_quad(g, lambda: None)

            for k in range(KT):
                j = k % NJ
                if k == NJ:
                    pe.wait_ge(h_added, KT)
                    pe.wait_ge(square_added, 2 * KT)
                    sum_squares(square_sum[:, 1, :], 0)
                unit_ready(Q_MEM + k // NJ, j)
                pe.wait_ge(mem_lo_done, k + 1)
                m = k % 4
                for n in range(X_HEADS):
                    cols = slice(n * P, (n + 1) * P)
                    product(ps[:, 2 + n, :MEM_LEN], w_hi[:, j, cols], w_lo[:, j, cols], mem_hi[:, m, :], mem_lo[:, m, :],
                            k == 0, k == KT - 1)
                for b in range(MB):
                    tok = slice(b * P, (b + 1) * P)
                    last = product(ps[:, 6 + b, :], mem_hi[:, m, tok], mem_lo[:, m, tok], w_hi[:, j, X_HEADS * P:],
                                   w_lo[:, j, X_HEADS * P:], k == 0, k == KT - 1)
                last.then_inc(w_used[j], 1)
            pe.wait_ge(square_added, 3 * KT)
            sum_squares(square_sum[:, 0, :MEM_LEN], 1, MEM_LEN, cols=(1, MEM_LEN, MB))

            def x_query(n):
                if n == 0:
                    pe.wait_ge(norm_root, R_H1)
                if n == 1:
                    pe.wait_ge(norm_root, R_MEMCOL)
                for half in range(2):
                    feature_unit(Q_XQ + n // 2, 2 * (n % 2) + half, n % 2, half, 2 * KT if n == 0 else None)

            def x_scores(n):
                pe.wait_ge(proj_lo_done, k_event(PAIRS - 1) + n + 1)
                pe.wait_ge(km_lo_done, X_HEADS)
                for i in range(TB):
                    tok = slice(i * P, (i + 1) * P)
                    last = product(ps[:, 2 + i // 2, (i % 2) * MEM_LEN:(i % 2 + 1) * MEM_LEN], xq_hi[:, tok],
                                   xq_lo[:, tok], km_hi[:, n, :], km_lo[:, n, :], True, True)
                last.then_inc(x_scored, 1)

            def x_turn(n):
                pe.wait_ge(x_ready, n + 1)
                for b in range(MB):
                    for i in range(TB):
                        last = nc.tensor.transpose(ps[:, 4 + b, i * P:(i + 1) * P], x_probs[:, i, b * P:(b + 1) * P],
                                                   ident[:, :])
                last.then_inc(x_turned, 1)

            def x_mix(n):
                pe.wait_ge(xpT_lo_done, MB * (n + 1))
                pe.wait_ge(vm_lo_done, MB)
                if n >= 2:
                    pe.wait_ge(xo_lo_done, n - 1)
                cols = slice(n * P, (n + 1) * P)
                for b in range(MB):
                    last = product(ps[:, 6 + n % 2, :], vm_hi[:, b, cols], vm_lo[:, b, cols], xpT_hi[:, b, :],
                                   xpT_lo[:, b, :], b == 0, b == MB - 1)
                last.then_inc(x_mixed, 1)

            for n in range(X_HEADS):
                x_query(n)
                if n >= 2:
                    x_mix(n - 2)
                if n >= 1:
                    x_turn(n - 1)
                x_scores(n)
            x_mix(X_HEADS - 2)
            x_turn(X_HEADS - 1)
            x_mix(X_HEADS - 1)

            def narrow_quads(q, r_hi, r_lo, slot, added):
                for u in range(2 * NJ):
                    j = u % NJ
                    unit_ready(q + u // NJ, j)
                    pe.wait_ge(h_added, added + max(0, 2 * u - 2))
                    for m in range(2):
                        for k in range(CH):
                            cols = slice((m * CH + k) * P, (m * CH + k + 1) * P)
                            last = product(ps[:, 2 * (u % 2) + m, :], w_hi[:, j, cols], w_lo[:, j, cols],
                                           one(r_hi, slot + k), one(r_lo, slot + k), k == 0, k == CH - 1)
                    last.then_inc(w_used[j], 1)

            pe.wait_ge(xo_lo_done, X_HEADS)
            narrow_quads(Q_XO, xo_hi, xo_lo, 0, KT)

            def gate_up(c, f, q):
                tile = c * CH + f
                event = 3 * KT if isinstance(c, int) and f == 0 else None
                for half in range(2):
                    if half == 0:
                        passed(pe, gate_scaled, tile - 1)
                    feature_unit(q, half, 4 + f % 2, half, event)
                if event is not None:
                    pe.wait_ge(square_added, 4 * KT)
                    sum_squares(square_sum[:, 1, :], 0)
                for half in range(2):
                    if half == 0:
                        passed(pe, up_scaled, tile - 1)
                    feature_unit(q, 2 + half, 6 + f % 2, half)

            def down(c, q):
                pe.wait_ge(g_lo_done, c * CH + CH)
                narrow_quads(q, g_hi, g_lo, (c % 2) * CH, c * KT + 2 * KT)

            for f in range(CH):
                gate_up(0, f, Q_FFN + f)
            with pe.Fori(0, NCH - 1) as c:
                q = c * (CH + 2) + (Q_FFN + CH)
                for f in range(CH):
                    gate_up(c + 1, f, q + f)
                down(c, q + CH)
            down(NCH - 1, N_QUADS - 2)
            pe.wait_ge(square_added, 5 * KT)
            sum_squares(square_sum[:, 0, :], 4)


def bias_tables(np):
    dist = np.arange(P)[:, None] + (SEQ - P) - np.arange(SEQ)[None, :]
    causal = dist >= 0
    count_a = causal & (dist < 128)
    count_c = causal & (dist <= 128)
    count_c = count_c.astype(int) + (causal & (dist % 4 == 0)) + (causal & (dist % 16 == 0))

    def table(slope, count):
        times = np.log(np.maximum(count, 1).astype(np.float64)) - np.float64(slope) * dist
        return np.where(count > 0, times, NEG).astype(np.float32)

    def slopes(n):
        return (2.0 ** (-8.0 * np.arange(1, n + 1) / n)).astype(np.float32)

    a, b, c = slopes(2 * A_PAIRS), slopes(2 * B_PAIRS), slopes(2 * C_PAIRS)
    out = [table(a[n], count_a) for pair in range(A_PAIRS) for n in (pair, pair + A_PAIRS)]
    out += [table(s, causal.astype(int)) for s in b]
    out += [table(s, count_c) for s in c]
    return np.stack(out)


def weight_stream(np, w_in, w_out, wq, wk, wv, wo, w_gate, w_up, w_down):
    def tiles(w):
        return w.reshape(w.shape[0] // P, P, w.shape[1] // P, P).transpose(0, 2, 1, 3)

    def unit(parts):
        return np.concatenate(parts, axis=1)

    def features(w, n):
        return [unit([w[k, n] for k in range(UT * half, UT * half + UT)]) for half in range(2)]

    a_w, kv_w, b_w, c_w = 512, 128, 512, 1024
    at, parts = 0, []
    for width in (a_w, kv_w, kv_w, b_w, b_w, b_w, c_w, c_w, c_w):
        parts.append(w_in[:, at:at + width])
        at += width
    qa, ka, va, qb, kb, vb, qc, kc, vc = parts
    heads = [x for p in range(A_PAIRS) for x in (p, p + A_PAIRS)]
    qa = qa.reshape(D_MODEL, 2 * A_PAIRS, HEAD_DIM)[:, heads].reshape(D_MODEL, a_w)
    units = []
    for v in (vb, vc[:, :SEQ], vc[:, SEQ:]):
        v = v.reshape(KT, P, SEQ)
        units += [unit([v[2 * u], v[2 * u + 1]]) for u in range(KT // 2)]
    units += features(tiles(va), 0) + features(tiles(ka), 0)
    for p in range(A_PAIRS):
        units += features(tiles(qa), p)
    for q, k, n in ((qb, kb, B_PAIRS), (qc, kc, C_PAIRS)):
        q, k = tiles(q), tiles(k)
        for p in range(n):
            units += features(q, p) + features(k, p)
    rows_a = w_out[:a_w].reshape(2 * A_PAIRS, HEAD_DIM, D_MODEL)[heads].reshape(a_w, D_MODEL)
    o = tiles(np.concatenate([rows_a, w_out[a_w:]]))
    for g in range(KT // 2):
        (a0, c0), (a1, c1) = features(o, 2 * g), features(o, 2 * g + 1)
        units += [a0, a1, c0, c1]
    k3, v3 = wk.reshape(KT, P, X_HEADS * P), wv.reshape(KT, P, X_HEADS * P)
    units += [unit([k3[k], v3[k]]) for k in range(KT)]
    for n in range(X_HEADS):
        units += features(tiles(wq), n)

    def narrow(w, k0):
        return [unit([w[k0 + k, 2 * u + m] for m in range(2) for k in range(CH)]) for u in range(KT // 2)]

    units += narrow(tiles(wo), 0)
    gate, up, down = tiles(w_gate), tiles(w_up), tiles(w_down)

    def gate_up(c):
        return [x for f in range(CH) for w in (gate, up) for x in features(w, c * CH + f)]

    units += gate_up(0)
    for c in range(NCH - 1):
        units += gate_up(c + 1) + narrow(down, c * CH)
    units += narrow(down, (NCH - 1) * CH)
    assert len(units) == N_QUADS * NJ
    return np.stack(units)


def kernel(x, mem, norm_mix, w_in, sinks, gain_a, gain_b, gain_c, w_out, norm_xattn, norm_mem,
           wq_x, wk_x, wv_x, wo_x, norm_ffn, w_gate, w_up, w_down, norm_final):
    import numpy as np
    import concourse.bacc as bacc
    from concourse.bass_utils import run_bass_kernel_spmd

    def col(v):
        return np.asarray(v).reshape(-1, P).T

    heads = [n for p in range(A_PAIRS) for n in (p, p + A_PAIRS)]
    g_a = np.asarray(gain_a)[0].reshape(2 * A_PAIRS, HEAD_DIM)[heads].reshape(-1)
    arrays = {
        "xT": np.asarray(x)[0].T,
        "memT": np.asarray(mem)[0].T,
        "stream": weight_stream(np, *(np.asarray(w)[0] for w in (w_in, w_out, wq_x, wk_x, wv_x, wo_x, w_gate, w_up, w_down))),
        "gains": np.concatenate([col(norm_mix), col(g_a), col(gain_b), col(gain_c), col(norm_xattn), col(norm_mem),
                                 col(norm_ffn), col(norm_final)], axis=1),
        "sinks": np.broadcast_to(np.asarray(sinks)[0][heads], (P, 2 * A_PAIRS)),
        "bias_table": bias_tables(np),
        "identity": np.eye(P, dtype=np.float32),
    }
    arrays = {n: np.ascontiguousarray(a) for n, a in arrays.items()}
    nc = bacc.Bacc("TRN2", target_bir_lowering=False, num_devices=1)
    args = [nc.dram_tensor(n, a.shape, F32, kind="ExternalInput").ap() for n, a in arrays.items()]
    outT = nc.dram_tensor("outT", (D_MODEL, SEQ), F32, kind="ExternalOutput").ap()
    build(nc, *args, outT)
    result = run_bass_kernel_spmd(nc, [arrays], core_ids=[0]).results[0]["outT"]
    return np.ascontiguousarray(result.T).reshape(1, SEQ, D_MODEL)
```

```python
from contextlib import ExitStack

import concourse.bass as bass
from concourse import mybir

F32 = mybir.dt.float32
F32R = mybir.dt.float32r
ACT = mybir.ActivationFunctionType
ALU = mybir.AluOpType
AX_X = mybir.AxisListType.X

P = 128
SEQ = 512
D_MODEL = 2048
KT = D_MODEL // P
TB = SEQ // P
HEAD_DIM = 64
MEM_LEN = 256
MB = MEM_LEN // P
X_HEADS = 4
D_FF = 5632
FT = D_FF // P
UT = 8
NJ = 4
CH = 4
NCH = FT // CH
EPS = 1e-5
NEG = -1.0e30
LOWEST = -3.0e38
B_PAIRS, C_PAIRS, A_PAIRS = 4, 8, 4
BC_PAIRS = B_PAIRS + C_PAIRS
PAIRS = BC_PAIRS + A_PAIRS
MIX_SCALE = HEAD_DIM ** -0.5
X_SCALE = float(P) ** -0.5

Q_V = 0
Q_BC = 6
Q_KA = Q_BC + BC_PAIRS
Q_VA = Q_KA + 1
Q_QA = Q_VA + 1
Q_OUT = Q_QA + 1
Q_MEM = Q_OUT + KT // 2
Q_XQ = Q_MEM + KT // NJ
Q_XO = Q_XQ + X_HEADS // 2
Q_FFN = Q_XO + 2
N_QUADS = Q_FFN + FT + 2 * NCH

G_MIX, G_OUT, G_X, G_MEM, G_FFN, G_FIN = (KT * n for n in range(6))
N_GAINS = 6 * KT

S_X, S_B, S_C, S_A, S_H1, S_MEM, S_H2, S_FIN = range(1, 9)
R_X, R_XCOL, R_B, R_C, R_A, R_H1, R_MEM, R_MEMCOL, R_H2, R_FIN = range(1, 11)
SLOT_X, SLOT_B, SLOT_C, SLOT_A, SLOT_H1, SLOT_MEM, SLOT_H2, SLOT_FIN = 0, 1, 0, 1, 0, 1, 0, 1
OUT_ORDER = [*range(B_PAIRS, BC_PAIRS), *range(B_PAIRS), *range(BC_PAIRS, PAIRS)]


class Layout:

    def __init__(self, rows, cols, banks):
        self.rows, self.cols, self.banks = rows, cols, banks
        self.widths = [0] * banks
        for _, _, w, c, _ in rows:
            self.widths[c // SEQ] = max(self.widths[c // SEQ], c % SEQ + w)


WINDOWED = Layout(
    rows=[(1, 0, 256, 0, 256), (2, 128, 256, 256, 256), (3, 256, 256, 512, 256), (0, 0, 128, 768, 384)],
    cols={0: (0, 0, 2), 1: (256, 1, 2), 2: (512, 2, 2), 3: (768, 3, 1)}, banks=2)
CAUSAL = Layout(
    rows=[(3, 0, 512, 0, 0), (2, 0, 384, 512, 128), (0, 0, 128, 896, 384), (1, 0, 256, 1024, 256)],
    cols={0: (0, 0, 4), 1: (512, 1, 3), 3: (896, 3, 1), 2: (1024, 2, 2)}, banks=3)
E_COLS = 1280


def build(nc, xT, memT, stream, gains, sinks, bias_table, identity, outT):
    with ExitStack() as ctx:
        def sb(stack, name, shape, dt=F32):
            return stack.enter_context(nc.sbuf_tensor(name, shape, dt))

        def sem(name):
            return ctx.enter_context(nc.semaphore(name))

        w_raw = sb(ctx, "w_raw", [P, NJ, UT * P])
        w_hi = sb(ctx, "w_hi", [P, NJ, UT * P], F32R)
        w_lo = sb(ctx, "w_lo", [P, NJ, UT * P], F32R)
        act_hi = sb(ctx, "act_hi", [P, KT, SEQ], F32R)
        act_lo = sb(ctx, "act_lo", [P, KT, SEQ], F32R)
        rstd = sb(ctx, "rstd", [P, SEQ])
        root = sb(ctx, "root", [P, SEQ])
        square_sum = sb(ctx, "square_sum", [P, 2, SEQ])
        squares = sb(ctx, "squares", [P, 2, SEQ])
        proj_raw = sb(ctx, "proj_raw", [P, SEQ])
        ident = sb(ctx, "ident", [P, P], F32R)
        ones = sb(ctx, "ones", [P, P])
        gain = sb(ctx, "gain", [P, N_GAINS])
        sink = sb(ctx, "sink", [P, 2 * A_PAIRS])
        small = sb(ctx, "small", [P, 64])
        eps = small[:, 0:1]
        root_col = small[:, 1:5]
        rstd_col = small[:, 5:9]
        row_max = [small[:, 16 + 4 * h:20 + 4 * h] for h in range(2)]
        neg_max = [small[:, 24 + 4 * h:28 + 4 * h] for h in range(2)]
        row_sum = [small[:, 32 + 4 * h:36 + 4 * h] for h in range(2)]
        row_inv = [small[:, 40 + 4 * h:44 + 4 * h] for h in range(2)]
        sink_arg = [small[:, 48 + 4 * h:52 + 4 * h] for h in range(2)]
        sink_exp = [small[:, 56 + 4 * h:60 + 4 * h] for h in range(2)]

        with ExitStack() as at_start:
            x_raw = sb(at_start, "x_raw", [P, KT, SEQ])
        with ExitStack() as mixing:
            probs = [sb(mixing, f"probs{h}", [P, E_COLS]) for h in range(2)]
            probs_hi = sb(mixing, "probs_hi", [P, E_COLS], F32R)
            probs_lo = sb(mixing, "probs_lo", [P, E_COLS], F32R)
            probsT_hi = sb(mixing, "probsT_hi", [P, E_COLS], F32R)
            probsT_lo = sb(mixing, "probsT_lo", [P, E_COLS], F32R)
            q_both = sb(mixing, "q_both", [P, 2, SEQ], F32R)
            k_twice = sb(mixing, "k_twice", [P, 2, SEQ], F32R)
            k_lo = sb(mixing, "k_lo", [P, SEQ], F32R)
            v_hi = sb(mixing, "v_hi", [P, TB, P], F32R)
            v_lo = sb(mixing, "v_lo", [P, TB, P], F32R)
            bias = sb(mixing, "bias", [P, 2, SEQ])
            vo = sb(mixing, "vo", [P, PAIRS, SEQ])
        with ExitStack() as later:
            h = sb(later, "h", [P, KT, SEQ])
            with ExitStack() as crossing:
                km_hi = sb(crossing, "km_hi", [P, X_HEADS, MEM_LEN], F32R)
                km_lo = sb(crossing, "km_lo", [P, X_HEADS, MEM_LEN], F32R)
                vm_hi = sb(crossing, "vm_hi", [P, MB, X_HEADS * P], F32R)
                vm_lo = sb(crossing, "vm_lo", [P, MB, X_HEADS * P], F32R)
                with ExitStack() as loading:
                    mem_raw = sb(loading, "mem_raw", [P, KT, MEM_LEN])
                    mem_hi = sb(loading, "mem_hi", [P, 4, MEM_LEN], F32R)
                    mem_lo = sb(loading, "mem_lo", [P, 4, MEM_LEN], F32R)
                    mem_rstd = sb(loading, "mem_rstd", [P, MEM_LEN])
                with ExitStack() as heads:
                    x_probs = sb(heads, "x_probs", [P, TB, MEM_LEN])
                    xpT_hi = sb(heads, "xpT_hi", [P, MB, SEQ], F32R)
                    xpT_lo = sb(heads, "xpT_lo", [P, MB, SEQ], F32R)
                    xq_hi = sb(heads, "xq_hi", [P, SEQ], F32R)
                    xq_lo = sb(heads, "xq_lo", [P, SEQ], F32R)
                    xo_hi = sb(heads, "xo_hi", [P, X_HEADS, SEQ], F32R)
                    xo_lo = sb(heads, "xo_lo", [P, X_HEADS, SEQ], F32R)
            with ExitStack() as feeding:
                g_hi = sb(feeding, "g_hi", [P, 2 * CH, SEQ], F32R)
                g_lo = sb(feeding, "g_lo", [P, 2 * CH, SEQ], F32R)
                gate_val = sb(feeding, "gate_val", [P, SEQ])
                up_val = sb(feeding, "up_val", [P, SEQ])

        ps = ctx.enter_context(nc.psum_tensor("ps", [P, 8, SEQ], F32))

        w_landed = [sem(f"w_landed{j}") for j in range(NJ)]
        w_hi_done = [sem(f"w_hi_done{j}") for j in range(NJ)]
        w_lo_done = [sem(f"w_lo_done{j}") for j in range(NJ)]
        w_used = [sem(f"w_used{j}") for j in range(NJ)]
        gains_landed = sem("gains_landed")
        tables_landed = sem("tables_landed")
        ident_set = sem("ident_set")
        x_landed = [sem(f"x_landed{n}") for n in range(8)]
        x_again_landed = sem("x_again_landed")
        mem_landed = sem("mem_landed")
        bias_landed = [sem(f"bias_landed{n}") for n in range(2)]
        consts_set = sem("consts_set")
        act_hi_done = sem("act_hi_done")
        act_lo_done = sem("act_lo_done")
        out_scaled_a = sem("out_scaled_a")
        out_scaled_b = sem("out_scaled_b")
        out_scaled_c = sem("out_scaled_c")
        squared = sem("squared")
        square_added = sem("square_added")
        square_sum_clear = sem("square_sum_clear")
        out_squared = sem("out_squared")
        out_square_added = sem("out_square_added")
        norm_summed = sem("norm_summed")
        norm_root = sem("norm_root")
        norm_ready = sem("norm_ready")
        v_copied = sem("v_copied")
        v_hi_done = sem("v_hi_done")
        v_lo_done = sem("v_lo_done")
        proj_raw_done = sem("proj_raw_done")
        proj_hi_done = [sem(f"proj_hi_done{n}") for n in range(2)]
        proj_lo_done = [sem(f"proj_lo_done{n}") for n in range(2)]
        k_doubled = sem("k_doubled")
        va_raw_done = sem("va_raw_done")
        va_turned = sem("va_turned")
        xq_raw_done = sem("xq_raw_done")
        xq_hi_done = sem("xq_hi_done")
        xq_lo_done = sem("xq_lo_done")
        scored = [[sem(f"scored{n}_{b}") for b in range(3)] for n in range(2)]
        max_taken = sem("max_taken")
        neg_ready = [sem(f"neg_ready{n}") for n in range(2)]
        exp_done = [sem(f"exp_done{n}") for n in range(2)]
        neg_taken = sem("neg_taken")
        sink_added = sem("sink_added")
        inv_done = [sem(f"inv_done{n}") for n in range(2)]
        probs_hi_done = [sem(f"probs_hi_done{n}") for n in range(2)]
        probs_lo_done = [sem(f"probs_lo_done{n}") for n in range(2)]
        turned = [[sem(f"turned{n}_{b}") for b in range(3)] for n in range(2)]
        pT_hi_done = [[sem(f"pT_hi{n}_{b}") for b in range(3)] for n in range(2)]
        pT_lo_done = [[sem(f"pT_lo{n}_{b}") for b in range(3)] for n in range(2)]
        mixed = [sem(f"mixed{n}") for n in range(2)]
        out_copied = [sem(f"out_copied{n}") for n in range(2)]
        h_added = sem("h_added")
        mem_hi_done = sem("mem_hi_done")
        mem_lo_done = sem("mem_lo_done")
        km_raw_done = sem("km_raw_done")
        km_hi_done = sem("km_hi_done")
        km_lo_done = sem("km_lo_done")
        vm_hi_done = sem("vm_hi_done")
        vm_lo_done = sem("vm_lo_done")
        x_scored = sem("x_scored")
        x_neg = sem("x_neg")
        x_exp = sem("x_exp")
        x_ready = sem("x_ready")
        x_turned = sem("x_turned")
        xpT_hi_done = sem("xpT_hi_done")
        xpT_lo_done = sem("xpT_lo_done")
        x_mixed = sem("x_mixed")
        xo_hi_done = sem("xo_hi_done")
        xo_lo_done = sem("xo_lo_done")
        gate_scaled = sem("gate_scaled")
        gate_silu = sem("gate_silu")
        up_scaled = sem("up_scaled")
        g_raw_done = sem("g_raw_done")
        g_hi_done = sem("g_hi_done")
        g_lo_done = sem("g_lo_done")
        gained = sem("gained")
        out_ready = [sem("out_ready_dve"), sem("out_ready_pool")]
        out_stored = sem("out_stored")

        def one(ap, i):
            if isinstance(i, int):
                return ap[:, i, :]
            return ap[:, bass.ds(i, 1), :].rearrange("p a n -> p (a n)")

        def passed(eng, semaphore, count):
            if not isinstance(count, int) or count > 0:
                eng.wait_ge(semaphore, count)

        def own_wait(eng, count):
            if not isinstance(count, int):
                eng.wait_ge(tables_landed, 32)

        def in_register(eng, count):
            return count if isinstance(count, int) else eng.snap(eng.to_reg(count))

        def k_event(pair):
            return 2 * min(pair, BC_PAIRS) + 1 if isinstance(pair, int) else 2 * pair + 1

        def q_event(pair):
            return BC_PAIRS + pair + 2 if isinstance(pair, int) and pair > BC_PAIRS else 2 * pair + 2

        def fill_quad(pair):
            return pair + (Q_BC + 1)

        def at(pair, n):
            return isinstance(pair, int) and pair == n

        def rows_of(n):
            return slice(n * HEAD_DIM, (n + 1) * HEAD_DIM)

        def layout(pair):
            return WINDOWED if isinstance(pair, int) and pair >= BC_PAIRS else CAUSAL

        out_engine = [1 if n % 3 == 2 else 0 for n in range(KT)]

        def head_bank(n, b):
            return 2 + 3 * n + b

        block = ctx.enter_context(nc.Block())

        @block.sync
        def _(sp):
            for j in range(NJ):
                sp.dma_start(w_raw[:, j, :], stream[j]).then_inc(w_landed[j], 16)
            with sp.Fori(1, N_QUADS) as q:
                for j in range(NJ):
                    sp.wait_ge(w_lo_done[j], q)
                    sp.dma_start(w_raw[:, j, :], stream[bass.ds(q * NJ + j, 1)].rearrange("a p n -> (a p) n"))\
                        .then_inc(w_landed[j], 16)
            for n in range(KT):
                sp.wait_ge(out_ready[out_engine[n]], out_engine[:n + 1].count(out_engine[n]))
                sp.dma_start(outT[n * P:(n + 1) * P, :], h[:, n, :]).then_inc(out_stored, 16)
            sp.wait_ge(out_stored, 16 * KT)

        @block.gpsimd
        def _(pool):
            nc.gpsimd.memset(eps, EPS).then_inc(consts_set, 1)
            nc.gpsimd.memset(ones[:, :], 1.0).then_inc(consts_set, 1)
            nc.gpsimd.memset(square_sum[:, :, :], 0.0).then_inc(square_sum_clear, 1)

            def load_bias(pair):
                for n in range(2):
                    if not isinstance(pair, int) or pair > 0:
                        pool.wait_ge(neg_ready[n], pair)
                    pool.dma_start(bias[:, n, :], bias_table[bass.ds(pair * 2 + n, 1)].rearrange("a p n -> (a p) n"))\
                        .then_inc(bias_landed[n], 16)

            def clear_sum(slot, summed, cleared):
                pool.wait_ge(norm_summed, summed)
                nc.gpsimd.memset(square_sum[:, slot, :], 0.0).then_inc(square_sum_clear, 1)
                pool.wait_ge(square_sum_clear, cleared)

            def add_squares(base, slot, width):
                for k in range(KT):
                    pool.wait_ge(squared, base + k + 1)
                    if k:
                        pool.wait_ge(square_added, base + k)
                    nc.gpsimd.tensor_tensor(square_sum[:, slot, :width], square_sum[:, slot, :width],
                                            squares[:, k % 2, :width], ALU.add).then_inc(square_added, 1)

            pool.wait_ge(square_sum_clear, 1)
            add_squares(0, SLOT_X, SEQ)
            pool.wait_ge(act_lo_done, KT)
            load_bias(0)

            def add_out_squares(slot, pair):
                for n in range(2):
                    pool.wait_ge(out_copied[n], pair + 1)
                passed(pool, out_square_added, pair)
                nc.gpsimd.tensor_tensor(squares[:, 0, :], one(vo, pair), one(vo, pair), ALU.mult).then_inc(out_squared, 1)
                pool.wait_ge(out_squared, pair + 1)
                nc.gpsimd.tensor_tensor(square_sum[:, slot, :], square_sum[:, slot, :], squares[:, 0, :],
                                        ALU.add).then_inc(out_square_added, 1)

            load_bias(1)
            add_out_squares(SLOT_B, 0)
            with pool.Fori(1, B_PAIRS) as pair:
                load_bias(pair + 1)
                add_out_squares(SLOT_B, pair)
            clear_sum(SLOT_C, S_X, 2)
            with pool.Fori(B_PAIRS, BC_PAIRS) as pair:
                load_bias(pair + 1)
                add_out_squares(SLOT_C, pair)
            load_bias(BC_PAIRS + 1)
            clear_sum(SLOT_A, S_B, 3)

            def scale_outs(done, event, inverse, first, count):
                pool.wait_ge(norm_ready, event)
                for t in range(first, first + count):
                    nc.gpsimd.tensor_tensor(vo[:, t, :], vo[:, t, :], inverse, ALU.mult).then_inc(done, 1)

            scale_outs(out_scaled_b, R_B, root[:, :], 0, B_PAIRS)
            scale_outs(out_scaled_c, R_C, squares[:, 1, :], B_PAIRS, C_PAIRS)
            for pair in range(BC_PAIRS, PAIRS):
                if BC_PAIRS < pair < PAIRS - 1:
                    load_bias(pair + 1)
                add_out_squares(SLOT_A, pair)
            pool.dma_start(h[:, :, :], xT.rearrange("(k p) n -> p k n", p=P)).then_inc(x_again_landed, 16)
            pool.wait_ge(act_lo_done, 2 * KT)
            pool.dma_start(mem_raw[:, :, :], memT.rearrange("(k p) n -> p k n", p=P)).then_inc(mem_landed, 16)
            clear_sum(SLOT_H1, S_C, 4)
            add_squares(1 * KT, SLOT_H1, SEQ)
            clear_sum(SLOT_MEM, S_A, 5)
            add_squares(2 * KT, SLOT_MEM, MEM_LEN)
            clear_sum(SLOT_H2, S_H1, 6)
            add_squares(3 * KT, SLOT_H2, SEQ)
            clear_sum(SLOT_FIN, S_MEM, 7)
            add_squares(4 * KT, SLOT_FIN, SEQ)
            pool.wait_ge(norm_ready, R_FIN)
            for n in range(KT):
                if out_engine[n] == 1:
                    pool.wait_ge(gained, n + 1)
                    nc.gpsimd.tensor_tensor(h[:, n, :], h[:, n, :], rstd[:, :], ALU.mult).then_inc(out_ready[1], 1)

        @block.scalar
        def _(act):
            act.dma_start(gain[:, :], gains).then_inc(gains_landed, 16)
            for c in range(8):
                act.dma_start(x_raw[:, 2 * c:2 * c + 2, :],
                              xT[2 * c * P:(2 * c + 2) * P, :].rearrange("(k p) n -> p k n", p=P))\
                    .then_inc(x_landed[c], 16)
            act.dma_start(sink[:, :], sinks).then_inc(tables_landed, 16)
            act.dma_start(proj_raw[:, 0:P], identity).then_inc(tables_landed, 16)

            def split(q, j):
                act.wait_ge(w_landed[j], q * 16 + 16)
                passed(act, w_used[j], q)
                nc.scalar.activation(w_hi[:, j, :], w_raw[:, j, :], ACT.Copy).then_inc(w_hi_done[j], 1)

            def scaled_hi(k, src, column):
                nc.scalar.activation(one(act_hi, k), src, ACT.Copy, scale=gain_col(column, k)).then_inc(act_hi_done, 1)

            def gain_col(column, k):
                if isinstance(k, int):
                    return gain[:, column + k:column + k + 1]
                return gain[:, bass.ds(k + column, 1)]

            def square(count, src, width=SEQ):
                passed(act, square_added, count - 1)
                nc.scalar.activation(squares[:, count % 2, :width], src, ACT.Square).then_inc(squared, 1)

            def take_root(summed, event, dst, src, n_features, inverted=None):
                act.wait_ge(norm_summed, summed)
                passed(act, norm_ready, event - 1 if inverted is None else inverted)
                nc.scalar.activation(dst, src, ACT.Sqrt, bias=eps, scale=1.0 / n_features).then_inc(norm_root, 1)

            def k_hi(pair):
                for n in range(2):
                    act.wait_ge(proj_raw_done, k_event(pair))
                    nc.scalar.activation(k_twice[rows_of(n), n, :], proj_raw[rows_of(n), :], ACT.Copy)\
                        .then_inc(proj_hi_done[n], 1)
                for n in range(2):
                    last = nc.scalar.activation(k_twice[rows_of(1 - n), n, :], proj_raw[rows_of(n), :], ACT.Copy)
                last.then_inc(k_doubled, 1)

            def q_hi(pair):
                for n in range(2):
                    act.wait_ge(proj_raw_done, q_event(pair))
                    nc.scalar.activation(q_both[rows_of(n), n, :], proj_raw[rows_of(n), :], ACT.Copy)\
                        .then_inc(proj_hi_done[n], 1)

            act.wait_ge(gains_landed, 16)
            for u in range(2 * NJ):
                split(u // NJ, u % NJ)
                act.wait_ge(x_landed[u], 16)
                for k in (2 * u, 2 * u + 1):
                    scaled_hi(k, x_raw[:, k, :], G_MIX)
                    square(k, x_raw[:, k, :])
            act.wait_ge(tables_landed, 32)
            act.wait_ge(consts_set, 2)
            nc.scalar.activation(ident[:, :], proj_raw[:, 0:P], ACT.Copy).then_inc(ident_set, 1)
            for u in range(2 * NJ, NJ * (Q_BC + 1) + 3):
                split(u // NJ, u % NJ)
                if u == 9:
                    take_root(S_X, R_X, root[:, :], ps[:, 4, :], D_MODEL)
                    take_root(S_X, R_XCOL, root_col, ps[:, 5, 0:TB], D_MODEL)
                if u < NJ * Q_BC + NJ and u % 8 == 3:
                    group = u // 8 - 1
                    act.wait_ge(w_used[3], 2 * group + 2)
                    act.wait_ge(norm_ready, R_XCOL)
                    for b in range(TB):
                        slots = vo[:, NJ * group:NJ * (group + 1), b * P:(b + 1) * P]
                        nc.scalar.activation(slots, ps[:, 4 * (group % 2) + b, :].rearrange("p (s n) -> p s n", n=P),
                                             ACT.Copy, scale=rstd_col[:, b:b + 1]).then_inc(v_copied, 1)
                if u == NJ * Q_BC + 5:
                    k_hi(0)
            q_hi(0)

            def stage_v(pair):
                if at(pair, 0):
                    act.wait_ge(v_copied, 3 * TB)
                else:
                    own_wait(act, pair)
                    act.wait_ge(mixed[1], pair)
                nc.scalar.activation(v_hi[:, :, :].rearrange("p b n -> p (b n)"), one(vo, pair), ACT.Copy)\
                    .then_inc(v_hi_done, 1)

            def stage_va():
                act.wait_ge(va_turned, 1)
                act.wait_ge(mixed[1], BC_PAIRS)
                nc.scalar.activation(v_hi[:, :, :].rearrange("p b n -> p (b n)"), ps[:, 1, :], ACT.Copy)\
                    .then_inc(v_hi_done, 1)

            def exponentials(n, pair, with_sink):
                act.wait_ge(neg_ready[n], pair + 1)
                if with_sink:
                    nc.scalar.activation(sink_exp[n], sink_arg[n], ACT.Exp)
                for i, _, w, c, _ in layout(pair).rows:
                    last = nc.scalar.activation(probs[n][:, c:c + w], probs[n][:, c:c + w], ACT.Exp,
                                                bias=neg_max[n][:, i:i + 1], accum_out=row_sum[n][:, i:i + 1])
                last.then_inc(exp_done[n], 1)

            def normalized_hi(n, pair):
                lay = layout(pair)
                if n == 1:
                    act.wait_ge(turned[0][lay.banks - 1], pair + 1)
                else:
                    passed(act, turned[1][1], pair)
                act.wait_ge(inv_done[n], pair + 1)
                for i, _, w, c, _ in lay.rows:
                    last = nc.scalar.activation(probs_hi[:, c:c + w], probs[n][:, c:c + w], ACT.Copy,
                                                scale=row_inv[n][:, i:i + 1])
                last.then_inc(probs_hi_done[n], 1)

            def turned_hi(n, pair, lay=None):
                lay = lay or layout(pair)
                for b in range(lay.banks):
                    act.wait_ge(turned[n][b], pair + 1)
                    w = lay.widths[b]
                    nc.scalar.activation(probsT_hi[:, b * SEQ:b * SEQ + w], ps[:, head_bank(n, b), :w], ACT.Copy)\
                        .then_inc(pT_hi_done[n][b], 1)

            def copy_out(n, pair):
                own_wait(act, pair)
                act.wait_ge(mixed[n], pair + 1)
                rows = rows_of(n)
                dst = vo[rows, pair, :] if isinstance(pair, int) else \
                    vo[rows, bass.ds(pair, 1), :].rearrange("p a n -> p (a n)")
                nc.scalar.activation(dst, ps[rows, head_bank(n, 2), :], ACT.Copy).then_inc(out_copied[n], 1)

            def out_hi(t):
                if t < C_PAIRS:
                    act.wait_ge(out_scaled_c, t + 1)
                elif t < BC_PAIRS:
                    act.wait_ge(out_scaled_b, t - C_PAIRS + 1)
                else:
                    act.wait_ge(out_scaled_a, t - BC_PAIRS + 1)
                scaled_hi(t, vo[:, OUT_ORDER[t], :], G_OUT)

            def cycle(pair):
                f = fill_quad(pair)
                if not at(pair, 0):
                    turned_hi(1, pair - 1)
                    copy_out(1, pair - 1)
                stage_v(pair)
                exponentials(0, pair, False)
                normalized_hi(0, pair)
                split(f, 3)
                exponentials(1, pair, False)
                split(f + 1, 0)
                split(f + 1, 1)
                turned_hi(0, pair)
                normalized_hi(1, pair)
                k_hi(pair + 1)
                split(f + 1, 2)
                copy_out(0, pair)
                q_hi(pair + 1)

            def last_cycle(m):
                pair = BC_PAIRS + m
                turned_hi(1, pair - 1)
                for t in {2: range(4), 3: range(C_PAIRS, BC_PAIRS)}.get(m, ()):
                    if t % 4 == 0:
                        act.wait_ge(w_used[2 if t < UT else 3], Q_QA + 1)
                    out_hi(t)
                copy_out(1, pair - 1)
                exponentials(0, pair, True)
                normalized_hi(0, pair)
                if m < 2:
                    split(Q_VA + m, 3)
                if m == 2:
                    for t in range(4, C_PAIRS):
                        out_hi(t)
                exponentials(1, pair, True)
                if m == 0:
                    take_root(S_B, R_B, root[:, :], ps[:, 4, :], B_PAIRS * P)
                    take_root(S_C, R_C, squares[:, 1, :], ps[:, 7, :], C_PAIRS * P, R_B - 1)
                early, late = ((Q_QA, 0), (Q_OUT, 0), (Q_OUT, 2), (Q_OUT + 1, 0))[m], \
                    ((Q_QA, 1), (Q_OUT, 1), (Q_OUT, 3), (Q_OUT + 1, 1))[m]
                split(*early)
                turned_hi(0, pair)
                if m == 0:
                    stage_va()
                normalized_hi(1, pair)
                if m == 0:
                    split(*late)
                    split(Q_QA, 2)
                    copy_out(0, pair)
                    q_hi(pair + 1)
                else:
                    if m < 3:
                        q_hi(pair + 1)
                    copy_out(0, pair)
                    split(*late)

            cycle(0)
            with act.Fori(1, BC_PAIRS) as pair:
                cycle(pair)
            for m in range(A_PAIRS):
                last_cycle(m)
            turned_hi(1, PAIRS - 1)
            copy_out(1, PAIRS - 1)
            act.wait_ge(out_scaled_b, B_PAIRS)
            take_root(S_A, R_A, root[:, :], ps[:, 5, :], A_PAIRS * P)
            for t in range(BC_PAIRS, PAIRS):
                out_hi(t)

            def square_h(count, n):
                act.wait_ge(square_added, count - 1)
                nc.scalar.activation(squares[:, n % 2, :], h[:, n, :], ACT.Square).then_inc(squared, 1)

            def out_quad(g, units):
                q = g + (Q_OUT + 1)
                for j in units:
                    split(q, j)
                for m in range(2):
                    if m:
                        split(q, 3)
                    own_wait(act, g)
                    act.wait_ge(h_added, g * 2 + (m + 1))
                    act.wait_ge(square_added, g * 2 + (KT + m - 1))
                    nc.scalar.activation(squares[:, m, :], one(h, g * 2 + m), ACT.Square).then_inc(squared, 1)

            out_quad(0, (2,))
            for j in range(2):
                split(Q_OUT + 2, j)
            out_quad(1, (2,))
            with act.Fori(2, KT // 2 - 1) as g:
                out_quad(g, (0, 1, 2))

            def mem_part(k):
                if k >= 4:
                    act.wait_ge(w_used[k % NJ], Q_MEM + k // NJ)
                nc.scalar.activation(mem_hi[:, k % 4, :], mem_raw[:, k, :], ACT.Copy,
                                     scale=gain_col(G_MEM, k)).then_inc(mem_hi_done, 1)

            act.wait_ge(mem_landed, 16)
            for k in range(4):
                mem_part(k)
            out_quad(KT // 2 - 1, (0, 1, 2))
            act.wait_ge(w_used[3], Q_MEM)
            for k in range(KT):
                split(Q_MEM + 1 + k // NJ, k % NJ)
                if k + 4 < KT:
                    mem_part(k + 4)
                scaled_hi(k, h[:, k, :], G_X)
                square(2 * KT + k, mem_raw[:, k, :], MEM_LEN)
                if k == 7:
                    take_root(S_H1, R_H1, root[:, :], ps[:, 0, :], D_MODEL)

            def x_query_hi(n):
                act.wait_ge(xq_raw_done, n + 1)
                nc.scalar.activation(xq_hi[:, :], proj_raw[:, :], ACT.Copy).then_inc(xq_hi_done, 1)

            split(Q_XQ + 1, 0)
            split(Q_XQ + 1, 1)
            x_query_hi(0)
            take_root(S_MEM, R_MEM, root[:, :MEM_LEN], ps[:, 1, :MEM_LEN], D_MODEL)
            take_root(S_MEM, R_MEMCOL, root_col[:, :MB], ps[:, 1, MEM_LEN:MEM_LEN + MB], D_MODEL)
            act.wait_ge(norm_ready, R_MEMCOL)
            for b in range(MB):
                nc.scalar.activation(vm_hi[:, b, :], ps[:, 6 + b, :], ACT.Copy,
                                     scale=rstd_col[:, b:b + 1]).then_inc(vm_hi_done, 1)
            for n in range(X_HEADS):
                act.wait_ge(km_raw_done, n + 1)
                nc.scalar.activation(km_hi[:, n, :], proj_raw[:, (n % 2) * MEM_LEN:(n % 2 + 1) * MEM_LEN], ACT.Copy)\
                    .then_inc(km_hi_done, 1)

            def x_exponentials(n):
                act.wait_ge(x_neg, n + 1)
                for i in range(TB):
                    last = nc.scalar.activation(x_probs[:, i, :], ps[:, 2 + i // 2, (i % 2) * MEM_LEN:(i % 2 + 1) * MEM_LEN],
                                                ACT.Exp, bias=neg_max[0][:, i:i + 1], accum_out=row_sum[0][:, i:i + 1])
                last.then_inc(x_exp, 1)

            def x_turned_hi(n):
                act.wait_ge(x_turned, n + 1)
                for b in range(MB):
                    nc.scalar.activation(xpT_hi[:, b, :], ps[:, 4 + b, :], ACT.Copy).then_inc(xpT_hi_done, 1)

            def x_out_hi(n):
                act.wait_ge(x_mixed, n + 1)
                nc.scalar.activation(xo_hi[:, n, :], ps[:, 6 + n % 2, :], ACT.Copy).then_inc(xo_hi_done, 1)

            split(Q_XQ + 1, 2)
            split(Q_XQ + 1, 3)
            x_exponentials(0)
            x_query_hi(1)
            for n in range(2):
                split(Q_XO, 2 * n)
                x_turned_hi(n)
                x_exponentials(n + 1)
                split(Q_XO, 2 * n + 1)
                x_query_hi(n + 2)
                x_out_hi(n)
            x_turned_hi(2)
            x_exponentials(3)
            x_out_hi(2)
            x_turned_hi(3)
            x_out_hi(3)

            for u in range(KT // 2):
                split(Q_XO + 1 + u // NJ, u % NJ)
                for n in (2 * u, 2 * u + 1):
                    act.wait_ge(h_added, KT + n + 1)
                    scaled_hi(n, h[:, n, :], G_FFN)
                    square_h(3 * KT + n, n)

            def gate_up(c, f, q):
                tile = c * CH + f
                split(q + 1, 0)
                split(q + 1, 1)
                act.wait_ge(gate_scaled, tile + 1)
                nc.scalar.activation(gate_val[:, :], gate_val[:, :], ACT.Silu).then_inc(gate_silu, 1)
                split(q + 1, 2)
                split(q + 1, 3)
                own_wait(act, c)
                act.wait_ge(g_raw_done, tile + 1)
                nc.scalar.activation(one(g_hi, (c % 2) * CH + f), up_val[:, :], ACT.Copy).then_inc(g_hi_done, 1)

            for f in range(CH):
                if f == 0:
                    take_root(S_H2, R_H2, root[:, :], ps[:, 0, :], D_MODEL)
                gate_up(0, f, Q_FFN + f)
            with act.Fori(0, NCH - 1) as c:
                q = c * (CH + 2) + (Q_FFN + CH)
                for f in range(CH):
                    gate_up(c + 1, f, q + f)
                for u in range(2 * NJ):
                    split(q + (CH + 1 + u // NJ), u % NJ)

            def gain_h(n):
                act.wait_ge(squared, 4 * KT + n + 1)
                nc.scalar.activation(h[:, n, :], h[:, n, :], ACT.Copy, scale=gain_col(G_FIN, n)).then_inc(gained, 1)

            for u in range(2 * NJ):
                if u < NJ:
                    split(N_QUADS - 1, u)
                for n in (2 * u, 2 * u + 1):
                    act.wait_ge(h_added, (2 + NCH - 1) * KT + n + 1)
                    square_h(4 * KT + n, n)
                    if n:
                        gain_h(n - 1)
            gain_h(KT - 1)
            take_root(S_FIN, R_FIN, root[:, :], ps[:, 4, :], D_MODEL)

        @block.vector
        def _(dve):
            def split(q, j):
                dve.wait_ge(w_hi_done[j], q + 1)
                nc.vector.tensor_tensor(w_lo[:, j, :], w_raw[:, j, :], w_hi[:, j, :].bitcast(F32), ALU.subtract)\
                    .then_inc(w_lo_done[j], 1)

            def scaled_lo(event, k, src, column):
                dve.wait_ge(act_hi_done, event)
                nc.vector.scalar_tensor_tensor(act_lo[:, k, :], src, gain[:, column + k:column + k + 1],
                                               act_hi[:, k, :].bitcast(F32), ALU.mult, ALU.subtract)\
                    .then_inc(act_lo_done, 1)

            def invert(event, dst, src):
                dve.wait_ge(norm_root, event)
                nc.vector.reciprocal(dst, src).then_inc(norm_ready, 1)

            dve.wait_ge(gains_landed, 16)
            for u in range(2 * NJ):
                split(u // NJ, u % NJ)
                dve.wait_ge(x_landed[u], 16)
                for k in (2 * u, 2 * u + 1):
                    scaled_lo(k + 1, k, x_raw[:, k, :], G_MIX)
            def stage_v(pair):
                dve.wait_ge(v_hi_done, pair + 1)
                nc.vector.tensor_tensor(v_lo[:, :, :].rearrange("p b n -> p (b n)"), one(vo, pair),
                                        v_hi[:, :, :].rearrange("p b n -> p (b n)").bitcast(F32), ALU.subtract)\
                    .then_inc(v_lo_done, 1)

            def stage_va():
                dve.wait_ge(v_hi_done, BC_PAIRS + 1)
                nc.vector.tensor_tensor(v_lo[:, :, :].rearrange("p b n -> p (b n)"), ps[:, 1, :],
                                        v_hi[:, :, :].rearrange("p b n -> p (b n)").bitcast(F32), ALU.subtract)\
                    .then_inc(v_lo_done, 1)

            def proj_scaled(event, q, j, bank, scale):
                dve.wait_ge(w_used[j], q + 1)
                for n in range(2):
                    passed(dve, proj_lo_done[n], event - 1)
                return nc.vector.scalar_tensor_tensor(proj_raw[:, :], ps[:, bank, :], scale, rstd[:, :], ALU.mult, ALU.mult)

            def key(pair, q, bank=1):
                e = k_event(pair)
                proj_scaled(e, q, 1, bank, 1.0).then_inc(proj_raw_done, 1)
                for n in range(2):
                    dve.wait_ge(proj_hi_done[n], e)
                    nc.vector.tensor_tensor(k_lo[rows_of(n), :], proj_raw[rows_of(n), :],
                                            k_twice[rows_of(n), n, :].bitcast(F32), ALU.subtract)\
                        .then_inc(proj_lo_done[n], 1)

            def query(pair, q, j=3, bank=0):
                e = q_event(pair)
                dve.wait_ge(k_doubled, min(pair, BC_PAIRS) + 1 if isinstance(pair, int) else pair + 1)
                proj_scaled(e, q, j, bank, MIX_SCALE).then_inc(proj_raw_done, 1)
                for n in range(2):
                    dve.wait_ge(proj_hi_done[n], e)
                    nc.vector.tensor_tensor(q_both[rows_of(1 - n), n, :], proj_raw[rows_of(n), :],
                                            q_both[rows_of(n), n, :].bitcast(F32), ALU.subtract)\
                        .then_inc(proj_lo_done[n], 1)

            for u in range(2 * NJ, NJ * (Q_BC + 1) + 3):
                split(u // NJ, u % NJ)
                if u == 9:
                    invert(R_X, rstd[:, :], root[:, :])
                    invert(R_XCOL, rstd_col, root_col)
                    dve.wait_ge(norm_ready, R_X)
                if u == NJ * Q_BC + 5:
                    key(0, Q_BC, 7)
            query(0, Q_BC)

            def maxima(n, pair, with_sink):
                lay = layout(pair)
                landed = in_register(dve, pair * 16 + 16)
                count = in_register(dve, pair + 1)
                bank = -1
                col = 2 * (pair - BC_PAIRS) + n if with_sink else 0
                for m, (i, _, w, c, bias_at) in enumerate(lay.rows):
                    if c // SEQ != bank:
                        bank = c // SEQ
                        own_wait(dve, pair)
                        if m == 0:
                            dve.wait_ge(bias_landed[n], landed)
                        dve.wait_ge(scored[n][bank], count)
                    first = sink[:, col:col + 1] if with_sink else LOWEST
                    nc.vector.tensor_tensor_reduce(probs[n][:, c:c + w], ps[:, head_bank(n, bank), c % SEQ:c % SEQ + w],
                                                   bias[:, n, bias_at:bias_at + w], 1.0, first, ALU.add, ALU.max,
                                                   row_max[n][:, i:i + 1]).then_inc(max_taken, 1)
                dve.wait_ge(max_taken, pair * (2 * TB) + (n + 1) * TB)
                last = nc.vector.tensor_scalar(neg_max[n], row_max[n], -1.0, None, ALU.mult)
                if with_sink:
                    last.then_inc(neg_taken, 1)
                    dve.wait_ge(neg_taken, col + 1)
                    last = nc.vector.tensor_scalar(sink_arg[n], neg_max[n], sink[:, col:col + 1], None, ALU.add)
                last.then_inc(neg_ready[n], 1)

            def invert_sums(n, pair, with_sink):
                dve.wait_ge(exp_done[n], pair + 1)
                if with_sink:
                    nc.vector.tensor_tensor(row_sum[n], row_sum[n], sink_exp[n], ALU.add).then_inc(sink_added, 1)
                    dve.wait_ge(sink_added, 2 * (pair - BC_PAIRS) + n + 1)
                nc.vector.reciprocal(row_inv[n], row_sum[n]).then_inc(inv_done[n], 1)

            def normalized_lo(n, pair):
                dve.wait_ge(probs_hi_done[n], pair + 1)
                for i, _, w, c, _ in layout(pair).rows:
                    last = nc.vector.scalar_tensor_tensor(probs_lo[:, c:c + w], probs[n][:, c:c + w], row_inv[n][:, i:i + 1],
                                                          probs_hi[:, c:c + w].bitcast(F32), ALU.mult, ALU.subtract)
                last.then_inc(probs_lo_done[n], 1)

            def turned_lo(n, pair, lay=None):
                lay = lay or layout(pair)
                for b in range(lay.banks):
                    dve.wait_ge(pT_hi_done[n][b], pair + 1)
                    w = lay.widths[b]
                    nc.vector.tensor_tensor(probsT_lo[:, b * SEQ:b * SEQ + w], ps[:, head_bank(n, b), :w],
                                            probsT_hi[:, b * SEQ:b * SEQ + w].bitcast(F32), ALU.subtract)\
                        .then_inc(pT_lo_done[n][b], 1)

            def out_lo(t):
                scaled_lo(KT + t + 1, t, vo[:, OUT_ORDER[t], :], G_OUT)

            def cycle(pair):
                f = fill_quad(pair)
                if not at(pair, 0):
                    turned_lo(1, pair - 1)
                maxima(0, pair, False)
                stage_v(pair)
                maxima(1, pair, False)
                invert_sums(0, pair, False)
                normalized_lo(0, pair)
                split(f, 3)
                invert_sums(1, pair, False)
                split(f + 1, 0)
                split(f + 1, 1)
                turned_lo(0, pair)
                normalized_lo(1, pair)
                key(pair + 1, f)
                split(f + 1, 2)
                query(pair + 1, f)

            def last_cycle(m):
                pair = BC_PAIRS + m
                turned_lo(1, pair - 1)
                for t in {2: range(4), 3: range(C_PAIRS, BC_PAIRS)}.get(m, ()):
                    out_lo(t)
                maxima(0, pair, True)
                maxima(1, pair, True)
                invert_sums(0, pair, True)
                normalized_lo(0, pair)
                if m < 2:
                    split(Q_VA + m, 3)
                if m == 2:
                    for t in range(4, C_PAIRS):
                        out_lo(t)
                invert_sums(1, pair, True)
                if m == 0:
                    proj_scaled(q_event(pair) + 1, Q_VA, 1, 1, 1.0).then_inc(va_raw_done, 1)
                early, late = ((Q_QA, 0), (Q_OUT, 0), (Q_OUT, 2), (Q_OUT + 1, 0))[m], \
                    ((Q_QA, 1), (Q_OUT, 1), (Q_OUT, 3), (Q_OUT + 1, 1))[m]
                split(*early)
                turned_lo(0, pair)
                if m == 0:
                    stage_va()
                normalized_lo(1, pair)
                if m == 0:
                    invert(R_B, root[:, :], root[:, :])
                    invert(R_C, squares[:, 1, :], squares[:, 1, :])
                    split(*late)
                    split(Q_QA, 2)
                    query(pair + 1, Q_VA)
                else:
                    if m < 3:
                        query(pair + 1, Q_QA, 2 * m - 1, 2 - m)
                    split(*late)

            cycle(0)
            with dve.Fori(1, BC_PAIRS) as pair:
                cycle(pair)
            for m in range(A_PAIRS):
                last_cycle(m)
            turned_lo(1, PAIRS - 1)
            invert(R_A, root[:, :], root[:, :])
            dve.wait_ge(norm_ready, R_A)
            for t in range(BC_PAIRS, PAIRS):
                nc.vector.tensor_tensor(vo[:, t, :], vo[:, t, :], root[:, :], ALU.mult).then_inc(out_scaled_a, 1)
            for t in range(BC_PAIRS, PAIRS):
                out_lo(t)

            def add_to_h(n, bank):
                nc.vector.tensor_tensor(one(h, n), ps[:, bank, :], one(h, n), ALU.add).then_inc(h_added, 1)

            dve.wait_ge(x_again_landed, 16)

            def out_quad(g, units, banks=(0, 1)):
                q = g + Q_OUT
                for j in units:
                    split(q + 1, j)
                for m in range(2):
                    dve.wait_ge(w_used[2 + m], q + 1)
                    add_to_h(g * 2 + m, banks[m])
                    split(q + 1, 2 + m)

            out_quad(0, (), (1, 0))
            out_quad(1, (0, 1), (2, 3))
            with dve.Fori(2, KT // 2 - 1) as g:
                out_quad(g, (0, 1))

            def mem_part(k):
                dve.wait_ge(mem_hi_done, k + 1)
                nc.vector.scalar_tensor_tensor(mem_lo[:, k % 4, :], mem_raw[:, k, :], gain[:, G_MEM + k:G_MEM + k + 1],
                                               mem_hi[:, k % 4, :].bitcast(F32), ALU.mult, ALU.subtract)\
                    .then_inc(mem_lo_done, 1)

            for k in range(4):
                mem_part(k)
            out_quad(KT // 2 - 1, (0, 1))
            for k in range(KT):
                split(Q_MEM + 1 + k // NJ, k % NJ)
                if k + 4 < KT:
                    mem_part(k + 4)
                scaled_lo(2 * KT + k + 1, k, h[:, k, :], G_X)
                if k == 7:
                    invert(R_H1, rstd[:, :], root[:, :])
                    dve.wait_ge(norm_ready, R_H1)

            def x_query_raw(n):
                dve.wait_ge(w_used[2 * (n % 2) + 1], Q_XQ + n // 2 + 1)
                passed(dve, xq_lo_done, n)
                if n == 1:
                    dve.wait_ge(km_lo_done, X_HEADS)
                nc.vector.scalar_tensor_tensor(proj_raw[:, :], ps[:, n % 2, :], X_SCALE, rstd[:, :], ALU.mult, ALU.mult)\
                    .then_inc(xq_raw_done, 1)

            def x_query_lo(n):
                dve.wait_ge(xq_hi_done, n + 1)
                nc.vector.tensor_tensor(xq_lo[:, :], proj_raw[:, :], xq_hi[:, :].bitcast(F32), ALU.subtract)\
                    .then_inc(xq_lo_done, 1)

            split(Q_XQ + 1, 0)
            split(Q_XQ + 1, 1)
            x_query_raw(0)
            x_query_lo(0)
            invert(R_MEM, mem_rstd[:, :], root[:, :MEM_LEN])
            invert(R_MEMCOL, rstd_col[:, :MB], root_col[:, :MB])
            dve.wait_ge(norm_ready, R_MEMCOL)
            dve.wait_ge(xq_lo_done, 1)
            for b in range(MB):
                dve.wait_ge(vm_hi_done, b + 1)
                nc.vector.scalar_tensor_tensor(vm_lo[:, b, :], ps[:, 6 + b, :], rstd_col[:, b:b + 1],
                                               vm_hi[:, b, :].bitcast(F32), ALU.mult, ALU.subtract)\
                    .then_inc(vm_lo_done, 1)

            def km_lo_half(n):
                dve.wait_ge(km_hi_done, n + 1)
                nc.vector.tensor_tensor(km_lo[:, n, :], proj_raw[:, (n % 2) * MEM_LEN:(n % 2 + 1) * MEM_LEN],
                                        km_hi[:, n, :].bitcast(F32), ALU.subtract).then_inc(km_lo_done, 1)

            for n in range(X_HEADS):
                passed(dve, km_lo_done, n - 1)
                nc.vector.tensor_tensor(proj_raw[:, (n % 2) * MEM_LEN:(n % 2 + 1) * MEM_LEN], ps[:, 2 + n, :MEM_LEN],
                                        mem_rstd[:, :], ALU.mult).then_inc(km_raw_done, 1)
                if n:
                    km_lo_half(n - 1)
            km_lo_half(X_HEADS - 1)


            def x_maxima(n):
                dve.wait_ge(x_scored, n + 1)
                nc.vector.tensor_reduce(row_max[0], ps[:, 2:4, :].rearrange("p b (i n) -> p (b i) n", n=MEM_LEN),
                                        AX_X, ALU.max).then_inc(max_taken, 1)
                dve.wait_ge(max_taken, PAIRS * 2 * TB + n + 1)
                nc.vector.tensor_scalar(neg_max[0], row_max[0], -1.0, None, ALU.mult).then_inc(x_neg, 1)

            def x_normalize(n):
                dve.wait_ge(x_exp, n + 1)
                nc.vector.reciprocal(row_inv[0], row_sum[0]).then_inc(inv_done[0], 1)
                dve.wait_ge(inv_done[0], PAIRS + n + 1)
                for i in range(TB):
                    last = nc.vector.tensor_scalar(x_probs[:, i, :], x_probs[:, i, :], row_inv[0][:, i:i + 1], None,
                                                   ALU.mult)
                last.then_inc(x_ready, 1)

            def x_turned_lo(n):
                for b in range(MB):
                    dve.wait_ge(xpT_hi_done, MB * n + b + 1)
                    nc.vector.tensor_tensor(xpT_lo[:, b, :], ps[:, 4 + b, :], xpT_hi[:, b, :].bitcast(F32),
                                            ALU.subtract).then_inc(xpT_lo_done, 1)

            def x_out_lo(n):
                dve.wait_ge(xo_hi_done, n + 1)
                nc.vector.tensor_tensor(xo_lo[:, n, :], ps[:, 6 + n % 2, :], xo_hi[:, n, :].bitcast(F32), ALU.subtract)\
                    .then_inc(xo_lo_done, 1)

            split(Q_XQ + 1, 2)
            split(Q_XQ + 1, 3)
            x_maxima(0)
            x_query_raw(1)
            x_normalize(0)
            x_query_lo(1)
            for n in range(2):
                split(Q_XO, 2 * n)
                x_turned_lo(n)
                x_maxima(n + 1)
                x_normalize(n + 1)
                split(Q_XO, 2 * n + 1)
                x_query_raw(n + 2)
                x_query_lo(n + 2)
                x_out_lo(n)
            x_turned_lo(2)
            x_maxima(3)
            x_normalize(3)
            x_out_lo(2)
            x_turned_lo(3)
            x_out_lo(3)

            for u in range(KT // 2):
                dve.wait_ge(w_used[u % NJ], Q_XO + u // NJ + 1)
                for m in range(2):
                    add_to_h(2 * u + m, 2 * (u % 2) + m)
                split(Q_XO + 1 + u // NJ, u % NJ)
                for n in (2 * u, 2 * u + 1):
                    scaled_lo(3 * KT + n + 1, n, h[:, n, :], G_FFN)

            def gate_up(c, f, q):
                tile = c * CH + f
                split(q + 1, 0)
                split(q + 1, 1)
                dve.wait_ge(w_used[1], q + 1)
                passed(dve, g_lo_done, tile)
                nc.vector.tensor_tensor(gate_val[:, :], ps[:, 4 + f % 2, :], rstd[:, :], ALU.mult)\
                    .then_inc(gate_scaled, 1)
                split(q + 1, 2)
                dve.wait_ge(w_used[3], q + 1)
                nc.vector.tensor_tensor(up_val[:, :], ps[:, 6 + f % 2, :], rstd[:, :], ALU.mult).then_inc(up_scaled, 1)
                dve.wait_ge(up_scaled, tile + 1)
                dve.wait_ge(gate_silu, tile + 1)
                nc.vector.tensor_tensor(up_val[:, :], gate_val[:, :], up_val[:, :], ALU.mult).then_inc(g_raw_done, 1)
                split(q + 1, 3)
                dve.wait_ge(g_hi_done, tile + 1)
                slot = (c % 2) * CH + f
                nc.vector.tensor_tensor(one(g_lo, slot), up_val[:, :], one(g_hi, slot).bitcast(F32), ALU.subtract)\
                    .then_inc(g_lo_done, 1)

            def down(q, with_split):
                for u in range(2 * NJ):
                    dve.wait_ge(w_used[u % NJ], q + (u // NJ + 1))
                    for m in range(2):
                        add_to_h(2 * u + m, 2 * (u % 2) + m)
                    if with_split or u < NJ:
                        split(q + (1 + u // NJ), u % NJ)

            for f in range(CH):
                if f == 0:
                    invert(R_H2, rstd[:, :], root[:, :])
                    dve.wait_ge(norm_ready, R_H2)
                gate_up(0, f, Q_FFN + f)
            with dve.Fori(0, NCH - 1) as c:
                q = c * (CH + 2) + (Q_FFN + CH)
                for f in range(CH):
                    gate_up(c + 1, f, q + f)
                down(q + CH, True)
            down(N_QUADS - 2, False)
            invert(R_FIN, rstd[:, :], root[:, :])
            dve.wait_ge(norm_ready, R_FIN)
            for n in range(KT):
                if out_engine[n] == 0:
                    dve.wait_ge(gained, n + 1)
                    nc.vector.tensor_tensor(h[:, n, :], h[:, n, :], rstd[:, :], ALU.mult).then_inc(out_ready[0], 1)

        @block.tensor
        def _(pe):
            def product(out, l_hi, l_lo, r_hi, r_lo, start, stop, **more):
                nc.tensor.matmul(out, l_hi, r_hi, start=start, stop=False, **more)
                nc.tensor.matmul(out, l_hi, r_lo, start=False, stop=False, **more)
                return nc.tensor.matmul(out, l_lo, r_hi, start=False, stop=stop, **more)

            def unit_ready(q, j):
                pe.wait_ge(w_lo_done[j], q + 1)

            def feature_unit(q, j, bank, half, act_event=None, tiles=range(UT)):
                if tiles[0] == 0:
                    unit_ready(q, j)
                for t in tiles:
                    k = UT * half + t
                    if act_event is not None:
                        pe.wait_ge(act_lo_done, act_event + k + 1)
                    cols = slice(t * P, (t + 1) * P)
                    last = product(ps[:, bank, :], w_hi[:, j, cols], w_lo[:, j, cols], act_hi[:, k, :], act_lo[:, k, :],
                                   k == 0, k == KT - 1)
                if tiles[-1] == UT - 1:
                    last.then_inc(w_used[j], 1)

            def sum_squares(sums, bank, width=SEQ, cols=None):
                last = nc.tensor.matmul(ps[:, bank, :width], ones[:, :], sums, start=True, stop=True)
                if cols:
                    col_bank, first, blocks = cols
                    for b in range(blocks):
                        last = nc.tensor.matmul(ps[:, col_bank, first + b:first + b + 1], sums[:, b * P:(b + 1) * P],
                                                ones[:, 0:1], start=True, stop=True)
                last.then_inc(norm_summed, 1)

            for group in range(3):
                if group == 1:
                    pe.wait_ge(norm_root, R_XCOL)
                if group == 2:
                    pe.wait_ge(v_copied, TB)
                for u in range(2 * NJ):
                    q, j = 2 * group + u // NJ, u % NJ
                    if group == 0 and u == 2 * NJ - 1:
                        pe.wait_ge(square_added, KT)
                        pe.wait_ge(consts_set, 2)
                        sum_squares(square_sum[:, SLOT_X, :], 4, cols=(5, 0, TB))
                    unit_ready(q, j)
                    for b in range(TB):
                        for t in range(2):
                            k = 2 * u + t
                            if group == 0 and b == 0:
                                pe.wait_ge(act_lo_done, k + 1)
                            tok = slice(b * P, (b + 1) * P)
                            cols = slice(t * SEQ, (t + 1) * SEQ)
                            last = product(ps[:, 4 * (group % 2) + b, :], act_hi[:, k, tok], act_lo[:, k, tok],
                                           w_hi[:, j, cols], w_lo[:, j, cols], k == 0, k == KT - 1)
                    last.then_inc(w_used[j], 1)
            pe.wait_ge(v_copied, 2 * TB)
            for j in range(NJ):
                if j == 2:
                    pe.wait_ge(v_copied, 3 * TB)
                feature_unit(Q_BC, j, (7, 0)[j // 2], j % 2)

            def scores(n, pair, lay):
                rows = rows_of(n)
                pe.wait_ge(proj_lo_done[n], q_event(pair))
                pe.wait_ge(k_doubled, BC_PAIRS + 1 if lay is WINDOWED else pair + 1)
                for m, (i, first_key, w, c, _) in enumerate(lay.rows):
                    b = c // SEQ
                    if b == 2:
                        passed(pe, out_copied[n], pair)
                    tok = slice(i * P, (i + 1) * P)
                    keys = slice(first_key, first_key + w)
                    out = ps[:, head_bank(n, b), c % SEQ:c % SEQ + w]
                    nc.tensor.matmul(out, q_both[:, n, tok], k_twice[:, n, keys], start=True, stop=False)
                    last = nc.tensor.matmul(out, q_both[rows, n, tok], k_lo[rows, keys], start=False, stop=True)
                    if m == len(lay.rows) - 1 or lay.rows[m + 1][3] // SEQ != b:
                        last.then_inc(scored[n][b], 1)

            def turn(n, pair, lay):
                pe.wait_ge(probs_lo_done[n], pair + 1)
                if at(pair, 0):
                    pe.wait_ge(ident_set, 1)
                blocks = []
                for j, (c, i0, count) in lay.cols.items():
                    for i in range(i0, i0 + count):
                        first_key, start = next((r[1], r[3]) for r in lay.rows if r[0] == i)
                        blocks.append((c + (i - i0) * P, start + j * P - first_key))
                blocks.sort()
                for x, (dst, src) in enumerate(blocks):
                    b = dst // SEQ
                    out = ps[:, head_bank(n, b), dst % SEQ:dst % SEQ + P]
                    nc.tensor.matmul(out, probs_hi[:, src:src + P], ident[:, :], start=True, stop=False)
                    last = nc.tensor.matmul(out, probs_lo[:, src:src + P], ident[:, :], start=False, stop=True)
                    if x == len(blocks) - 1 or blocks[x + 1][0] // SEQ != b:
                        last.then_inc(turned[n][b], 1)

            def mix(n, pair, lay):
                out = ps[:, head_bank(n, 2), :]
                if lay.banks < 3:
                    pe.wait_ge(out_copied[n], pair)
                    if pair == BC_PAIRS:
                        pe.wait_ge(norm_root, (R_B, R_C)[n])
                for b in reversed(range(lay.banks)):
                    pe.wait_ge(pT_lo_done[n][b], pair + 1)
                order = sorted(lay.cols)
                for j in order:
                    c, i0, count = lay.cols[j]
                    w = count * P
                    last = product(out[:, i0 * P:i0 * P + w], v_hi[:, j, :], v_lo[:, j, :],
                                   probsT_hi[:, c:c + w], probsT_lo[:, c:c + w], j == order[0], j == order[-1],
                                   skip_group_check=True)
                last.then_inc(mixed[n], 1)

            def run(halves):
                for q, j, bank, half, tiles, event in halves:
                    feature_unit(q, j, bank, half, event, tiles)

            def attend(pair, fill, before_turn=None, after_turn=None):
                lay = layout(pair)
                pe.wait_ge(proj_raw_done, k_event(pair))
                run(fill[0])
                scores(0, pair, lay)
                if not at(pair, 0):
                    mix(1, pair - 1, layout(pair - 1))
                scores(1, pair, lay)
                run(fill[1])
                if before_turn:
                    before_turn()
                turn(0, pair, lay)
                if after_turn:
                    after_turn()
                run(fill[2])
                pe.wait_ge(v_lo_done, min(pair, BC_PAIRS) + 1 if isinstance(pair, int) else pair + 1)
                mix(0, pair, lay)
                run(fill[3])
                turn(1, pair, lay)

            FRONT, BACK = range(UT // 2), range(UT // 2, UT)

            def bc_fill(pair):
                q = fill_quad(pair)
                halves = [(q, j, 1 - j // 2, j % 2, tiles, None) for j in range(NJ) for tiles in (FRONT, BACK)]
                return halves[:1], halves[1:4], halves[4:6], halves[6:]

            attend(0, bc_fill(0))
            with pe.Fori(1, BC_PAIRS) as pair:
                attend(pair, bc_fill(pair))

            def turn_va():
                pe.wait_ge(va_raw_done, 1)
                for b in range(TB):
                    last = nc.tensor.transpose(ps[:, 1, b * P:(b + 1) * P], proj_raw[:, b * P:(b + 1) * P],
                                               ident[:, :].bitcast(F32))
                last.then_inc(va_turned, 1)

            def sum_outs():
                for slot, count, n in ((SLOT_B, B_PAIRS, 0), (SLOT_C, BC_PAIRS, 1)):
                    pe.wait_ge(out_square_added, count)
                    pe.wait_ge(out_copied[n], BC_PAIRS)
                    sum_squares(square_sum[:, slot, :], head_bank(n, 2))

            def halves_of(q, j, bank, half, event=None):
                return [(q, j, bank, half, tiles, event) for tiles in (FRONT, BACK)]

            va = halves_of(Q_VA, 0, 1, 0) + halves_of(Q_VA, 1, 1, 1)
            attend(BC_PAIRS, (va[:1], va[1:], halves_of(Q_VA, 2, 0, 0), halves_of(Q_VA, 3, 0, 1)), sum_outs, turn_va)
            q2 = halves_of(Q_QA, 0, 1, 0) + halves_of(Q_QA, 1, 1, 1)
            q3 = halves_of(Q_QA, 2, 0, 0) + halves_of(Q_QA, 3, 0, 1)
            attend(BC_PAIRS + 1, (q2[:1], q2[1:3], q2[3:] + q3[:1], q3[1:2]))
            over_c = [halves_of(Q_OUT, m, 1 - m, 0, KT) for m in range(2)]
            over_ba = [halves_of(Q_OUT, 2 + m, 1 - m, 1, KT) for m in range(2)]
            attend(BC_PAIRS + 2, (q3[2:3], q3[3:] + over_c[0][:1], over_c[0][1:], ()))
            pe.wait_ge(proj_raw_done, q_event(PAIRS - 1))
            attend(PAIRS - 1, (over_c[1][:1], over_c[1][1:] + over_ba[0][:1], over_ba[1][:1], ()))
            mix(1, PAIRS - 1, WINDOWED)
            feature_unit(Q_OUT + 1, 0, 2, 0)
            pe.wait_ge(out_square_added, PAIRS)
            sum_squares(square_sum[:, SLOT_A, :], 5)
            feature_unit(Q_OUT + 1, 1, 3, 0)
            for m in range(2):
                run([over_ba[m][1]])
            for m in range(2):
                feature_unit(Q_OUT + 1, 2 + m, 2 + m, 1)
            with pe.Fori(2, KT // 2) as g:
                for half in range(2):
                    for m in range(2):
                        if half == 0:
                            pe.wait_ge(h_added, g * 2 + (m - 1))
                        feature_unit(g + Q_OUT, 2 * half + m, m, half)

            for k in range(KT):
                j = k % NJ
                if k == NJ:
                    pe.wait_ge(h_added, KT)
                    pe.wait_ge(square_added, 2 * KT)
                    sum_squares(square_sum[:, SLOT_H1, :], 0)
                unit_ready(Q_MEM + k // NJ, j)
                pe.wait_ge(mem_lo_done, k + 1)
                m = k % 4
                for n in range(X_HEADS):
                    cols = slice(n * P, (n + 1) * P)
                    product(ps[:, 2 + n, :MEM_LEN], w_hi[:, j, cols], w_lo[:, j, cols], mem_hi[:, m, :], mem_lo[:, m, :],
                            k == 0, k == KT - 1)
                for b in range(MB):
                    tok = slice(b * P, (b + 1) * P)
                    last = product(ps[:, 6 + b, :], mem_hi[:, m, tok], mem_lo[:, m, tok], w_hi[:, j, X_HEADS * P:],
                                   w_lo[:, j, X_HEADS * P:], k == 0, k == KT - 1)
                last.then_inc(w_used[j], 1)
            def x_query(n, halves=(0, 1)):
                if n == 1:
                    pe.wait_ge(norm_root, R_MEMCOL)
                if n >= 2 and halves[0] == 0:
                    pe.wait_ge(xq_raw_done, n - 1)
                for half in halves:
                    feature_unit(Q_XQ + n // 2, 2 * (n % 2) + half, n % 2, half, 2 * KT if n == 0 else None)

            def x_scores(n):
                pe.wait_ge(xq_lo_done, n + 1)
                pe.wait_ge(km_lo_done, X_HEADS)
                for i in range(TB):
                    tok = slice(i * P, (i + 1) * P)
                    last = product(ps[:, 2 + i // 2, (i % 2) * MEM_LEN:(i % 2 + 1) * MEM_LEN], xq_hi[:, tok],
                                   xq_lo[:, tok], km_hi[:, n, :], km_lo[:, n, :], True, True)
                last.then_inc(x_scored, 1)

            def x_turn(n):
                pe.wait_ge(x_ready, n + 1)
                for b in range(MB):
                    for i in range(TB):
                        last = nc.tensor.transpose(ps[:, 4 + b, i * P:(i + 1) * P], x_probs[:, i, b * P:(b + 1) * P],
                                                   ident[:, :].bitcast(F32))
                last.then_inc(x_turned, 1)

            def x_mix(n):
                pe.wait_ge(xpT_lo_done, MB * (n + 1))
                pe.wait_ge(vm_lo_done, MB)
                if n >= 2:
                    pe.wait_ge(xo_lo_done, n - 1)
                cols = slice(n * P, (n + 1) * P)
                for b in range(MB):
                    last = product(ps[:, 6 + n % 2, :], vm_hi[:, b, cols], vm_lo[:, b, cols], xpT_hi[:, b, :],
                                   xpT_lo[:, b, :], b == 0, b == MB - 1)
                last.then_inc(x_mixed, 1)

            pe.wait_ge(norm_root, R_H1)
            x_query(0)
            pe.wait_ge(square_added, 3 * KT)
            sum_squares(square_sum[:, SLOT_MEM, :MEM_LEN], 1, MEM_LEN, cols=(1, MEM_LEN, MB))
            x_query(1)
            x_scores(0)
            for n in range(2):
                x_query(n + 2, (0,))
                x_turn(n)
                x_scores(n + 1)
                x_query(n + 2, (1,))
                x_mix(n)
            x_turn(2)
            x_scores(3)
            x_mix(2)
            x_turn(3)
            x_mix(3)

            def narrow_quads(q, r_hi, r_lo, slot, added):
                for u in range(2 * NJ):
                    j = u % NJ
                    unit_ready(q + u // NJ, j)
                    pe.wait_ge(h_added, added + max(0, 2 * u - 2))
                    for m in range(2):
                        for k in range(CH):
                            cols = slice((m * CH + k) * P, (m * CH + k + 1) * P)
                            last = product(ps[:, 2 * (u % 2) + m, :], w_hi[:, j, cols], w_lo[:, j, cols],
                                           one(r_hi, slot + k), one(r_lo, slot + k), k == 0, k == CH - 1)
                    last.then_inc(w_used[j], 1)

            pe.wait_ge(xo_lo_done, X_HEADS)
            narrow_quads(Q_XO, xo_hi, xo_lo, 0, KT)

            def gate_up(c, f, q):
                tile = c * CH + f
                event = 3 * KT if isinstance(c, int) and f == 0 else None
                for half in range(2):
                    if half == 0:
                        passed(pe, gate_scaled, tile - 1)
                    feature_unit(q, half, 4 + f % 2, half, event)
                if event is not None:
                    pe.wait_ge(square_added, 4 * KT)
                    sum_squares(square_sum[:, SLOT_H2, :], 0)
                for half in range(2):
                    if half == 0:
                        passed(pe, up_scaled, tile - 1)
                    feature_unit(q, 2 + half, 6 + f % 2, half)

            def down(c, q):
                pe.wait_ge(g_lo_done, c * CH + CH)
                narrow_quads(q, g_hi, g_lo, (c % 2) * CH, c * KT + 2 * KT)

            for f in range(CH):
                gate_up(0, f, Q_FFN + f)
            with pe.Fori(0, NCH - 1) as c:
                q = c * (CH + 2) + (Q_FFN + CH)
                for f in range(CH):
                    gate_up(c + 1, f, q + f)
                down(c, q + CH)
            down(NCH - 1, N_QUADS - 2)
            pe.wait_ge(square_added, 5 * KT)
            sum_squares(square_sum[:, SLOT_FIN, :], 4)


def bias_tables(np):
    dist = np.arange(P)[:, None] + (SEQ - P) - np.arange(SEQ)[None, :]
    causal = dist >= 0
    count_a = causal & (dist < 128)
    count_c = causal & (dist <= 128)
    count_c = count_c.astype(int) + (causal & (dist % 4 == 0)) + (causal & (dist % 16 == 0))

    def table(slope, count):
        times = np.log(np.maximum(count, 1).astype(np.float64)) - np.float64(slope) * dist
        return np.where(count > 0, times, NEG).astype(np.float32)

    def slopes(n):
        return (2.0 ** (-8.0 * np.arange(1, n + 1) / n)).astype(np.float32)

    a, b, c = slopes(2 * A_PAIRS), slopes(2 * B_PAIRS), slopes(2 * C_PAIRS)
    out = [table(s, causal.astype(int)) for s in b]
    out += [table(s, count_c) for s in c]
    out += [table(a[n], count_a) for pair in range(A_PAIRS) for n in (pair, pair + A_PAIRS)]
    return np.stack(out)


def weight_stream(np, w_in, w_out, wq, wk, wv, wo, w_gate, w_up, w_down):
    def tiles(w):
        return w.reshape(w.shape[0] // P, P, w.shape[1] // P, P).transpose(0, 2, 1, 3)

    def unit(parts):
        return np.concatenate(parts, axis=1)

    def features(w, n):
        return [unit([w[k, n] for k in range(UT * half, UT * half + UT)]) for half in range(2)]

    a_w, kv_w, b_w, c_w = 512, 128, 512, 1024
    at, parts = 0, []
    for width in (a_w, kv_w, kv_w, b_w, b_w, b_w, c_w, c_w, c_w):
        parts.append(w_in[:, at:at + width])
        at += width
    qa, ka, va, qb, kb, vb, qc, kc, vc = parts
    heads = [x for p in range(A_PAIRS) for x in (p, p + A_PAIRS)]
    qa = qa.reshape(D_MODEL, 2 * A_PAIRS, HEAD_DIM)[:, heads].reshape(D_MODEL, a_w)
    units = []
    for v in (vb, vc[:, :SEQ], vc[:, SEQ:]):
        v = v.reshape(KT, P, SEQ)
        units += [unit([v[2 * u], v[2 * u + 1]]) for u in range(KT // 2)]
    for q, k, n in ((qb, kb, B_PAIRS), (qc, kc, C_PAIRS)):
        q, k = tiles(q), tiles(k)
        for p in range(n):
            units += features(k, p) + features(q, p)
    qa = tiles(qa)
    units += features(tiles(ka), 0) + features(qa, 0) + features(tiles(va), 0)
    for p in range(1, A_PAIRS):
        units += features(qa, p)
    rows_a = w_out[:a_w].reshape(2 * A_PAIRS, HEAD_DIM, D_MODEL)[heads].reshape(a_w, D_MODEL)
    o = tiles(np.concatenate([w_out[a_w + b_w:], w_out[a_w:a_w + b_w], rows_a]))
    for g in range(KT // 2):
        (a0, c0), (a1, c1) = features(o, 2 * g), features(o, 2 * g + 1)
        units += [a0, a1, c0, c1]
    k3, v3 = wk.reshape(KT, P, X_HEADS * P), wv.reshape(KT, P, X_HEADS * P)
    units += [unit([k3[k], v3[k]]) for k in range(KT)]
    for n in range(X_HEADS):
        units += features(tiles(wq), n)

    def narrow(w, k0):
        return [unit([w[k0 + k, 2 * u + m] for m in range(2) for k in range(CH)]) for u in range(KT // 2)]

    units += narrow(tiles(wo), 0)
    gate, up, down = tiles(w_gate), tiles(w_up), tiles(w_down)

    def gate_up(c):
        return [x for f in range(CH) for w in (gate, up) for x in features(w, c * CH + f)]

    units += gate_up(0)
    for c in range(NCH - 1):
        units += gate_up(c + 1) + narrow(down, c * CH)
    units += narrow(down, (NCH - 1) * CH)
    assert len(units) == N_QUADS * NJ
    return np.stack(units)


def kernel(x, mem, norm_mix, w_in, sinks, gain_a, gain_b, gain_c, w_out, norm_xattn, norm_mem,
           wq_x, wk_x, wv_x, wo_x, norm_ffn, w_gate, w_up, w_down, norm_final):
    import numpy as np
    import concourse.bacc as bacc
    from concourse.bass_utils import run_bass_kernel_spmd

    def col(v):
        return np.asarray(v).reshape(-1, P).T

    heads = [n for p in range(A_PAIRS) for n in (p, p + A_PAIRS)]
    g_a = np.asarray(gain_a)[0].reshape(2 * A_PAIRS, HEAD_DIM)[heads].reshape(-1)
    arrays = {
        "xT": np.asarray(x)[0].T,
        "memT": np.asarray(mem)[0].T,
        "stream": weight_stream(np, *(np.asarray(w)[0] for w in (w_in, w_out, wq_x, wk_x, wv_x, wo_x, w_gate, w_up, w_down))),
        "gains": np.concatenate([col(norm_mix), col(gain_c), col(gain_b), col(g_a), col(norm_xattn), col(norm_mem),
                                 col(norm_ffn), col(norm_final)], axis=1),
        "sinks": np.broadcast_to(np.asarray(sinks)[0][heads], (P, 2 * A_PAIRS)),
        "bias_table": bias_tables(np),
        "identity": np.eye(P, dtype=np.float32),
    }
    arrays = {n: np.ascontiguousarray(a) for n, a in arrays.items()}
    nc = bacc.Bacc("TRN2", target_bir_lowering=False, num_devices=1)
    args = [nc.dram_tensor(n, a.shape, F32, kind="ExternalInput").ap() for n, a in arrays.items()]
    outT = nc.dram_tensor("outT", (D_MODEL, SEQ), F32, kind="ExternalOutput").ap()
    build(nc, *args, outT)
    result = run_bass_kernel_spmd(nc, [arrays], core_ids=[0]).results[0]["outT"]
    return np.ascontiguousarray(result.T).reshape(1, SEQ, D_MODEL)
```

```python
from contextlib import ExitStack

import concourse.bass as bass
from concourse import mybir

F32 = mybir.dt.float32
F32R = mybir.dt.float32r
ACT = mybir.ActivationFunctionType
ALU = mybir.AluOpType
AX_X = mybir.AxisListType.X

P = 128
SEQ = 512
D_MODEL = 2048
KT = D_MODEL // P
TB = SEQ // P
HEAD_DIM = 64
MEM_LEN = 256
MB = MEM_LEN // P
X_HEADS = 4
D_FF = 5632
FT = D_FF // P
UT = 8
NJ = 4
CH = 4
NCH = FT // CH
EPS = 1e-5
WARM_UP = 14
NEG = -1.0e30
LOWEST = -3.0e38
B_PAIRS, C_PAIRS, A_PAIRS = 4, 8, 4
BC_PAIRS = B_PAIRS + C_PAIRS
PAIRS = BC_PAIRS + A_PAIRS
MIX_SCALE = HEAD_DIM ** -0.5
X_SCALE = float(P) ** -0.5

Q_V = 0
Q_BC = 6
Q_KA = Q_BC + BC_PAIRS
Q_VA = Q_KA + 1
Q_QA = Q_VA + 1
Q_OUT = Q_QA + 1
Q_MEM = Q_OUT + KT // 2
Q_XQ = Q_MEM + KT // NJ
Q_XO = Q_XQ + X_HEADS // 2
Q_FFN = Q_XO + 2
N_QUADS = Q_FFN + FT + 2 * NCH

G_MIX, G_OUT, G_X, G_MEM, G_FFN, G_FIN = (KT * n for n in range(6))
N_GAINS = 6 * KT

S_X, S_B, S_C, S_A, S_H1, S_MEM, S_H2, S_FIN = range(1, 9)
R_X, R_XCOL, R_B, R_C, R_A, R_H1, R_MEM, R_MEMCOL, R_H2, R_FIN = range(1, 11)
HALF = SEQ // 2
HALVES = (slice(0, HALF), slice(HALF, SEQ))
SLOT_X, SLOT_B, SLOT_C, SLOT_A, SLOT_H1, SLOT_MEM, SLOT_H2, SLOT_FIN = 0, 1, 0, 1, 0, 1, 0, 1
OUT_BANKS = (1, 0, 2, 3)
X_OUT_BANKS = (6, 7, 6, 6)
XO_BANKS = ((0, 1, 7), (2, 3, 0, 1, 6, 7))
OUT_ORDER = [*range(B_PAIRS, BC_PAIRS), *range(B_PAIRS), *range(BC_PAIRS, PAIRS)]


class Layout:

    def __init__(self, rows, cols, banks):
        self.rows, self.cols, self.banks = rows, cols, banks
        self.widths = [0] * banks
        for _, _, w, c, _ in rows:
            self.widths[c // SEQ] = max(self.widths[c // SEQ], c % SEQ + w)


WINDOWED = Layout(
    rows=[(1, 0, 256, 0, 256), (2, 128, 256, 256, 256), (3, 256, 256, 512, 256), (0, 0, 128, 768, 384)],
    cols={0: (0, 0, 2), 1: (256, 1, 2), 2: (512, 2, 2), 3: (768, 3, 1)}, banks=2)
CAUSAL = Layout(
    rows=[(3, 0, 512, 0, 0), (2, 0, 384, 512, 128), (0, 0, 128, 896, 384), (1, 0, 256, 1024, 256)],
    cols={0: (0, 0, 4), 1: (512, 1, 3), 3: (896, 3, 1), 2: (1024, 2, 2)}, banks=3)
E_COLS = 1280


def build(nc, xT, memT, stream, gains, sinks, bias_table, identity, outT):
    with ExitStack() as ctx:
        def sb(stack, name, shape, dt=F32):
            return stack.enter_context(nc.sbuf_tensor(name, shape, dt))

        def sem(name):
            return ctx.enter_context(nc.semaphore(name))

        w_raw = sb(ctx, "w_raw", [P, NJ, UT * P])
        w_hi = sb(ctx, "w_hi", [P, NJ, UT * P], F32R)
        w_lo = sb(ctx, "w_lo", [P, NJ, UT * P], F32R)
        act_hi = sb(ctx, "act_hi", [P, KT, SEQ], F32R)
        act_lo = sb(ctx, "act_lo", [P, KT, SEQ], F32R)
        rstd = sb(ctx, "rstd", [P, SEQ])
        root = sb(ctx, "root", [P, SEQ])
        square_sum = sb(ctx, "square_sum", [P, 2, SEQ])
        squares = sb(ctx, "squares", [P, 2, SEQ])
        proj_raw = sb(ctx, "proj_raw", [P, SEQ])
        ident = sb(ctx, "ident", [P, P])
        ones = sb(ctx, "ones", [P, P])
        gain = sb(ctx, "gain", [P, N_GAINS])
        sink = sb(ctx, "sink", [P, 2 * A_PAIRS])
        small = sb(ctx, "small", [P, 64])
        eps = small[:, 0:1]
        root_col = small[:, 1:5]
        rstd_col = small[:, 5:9]
        spare = small[:, 9:10]
        row_max = [small[:, 16 + 4 * h:20 + 4 * h] for h in range(2)]
        neg_max = [small[:, 24 + 4 * h:28 + 4 * h] for h in range(2)]
        row_sum = [small[:, 32 + 4 * h:36 + 4 * h] for h in range(2)]
        row_inv = [small[:, 40 + 4 * h:44 + 4 * h] for h in range(2)]
        sink_arg = [small[:, 48 + 4 * h:52 + 4 * h] for h in range(2)]
        sink_exp = [small[:, 56 + 4 * h:60 + 4 * h] for h in range(2)]

        with ExitStack() as at_start:
            x_raw = sb(at_start, "x_raw", [P, KT, SEQ])
        with ExitStack() as mixing:
            probs = [sb(mixing, f"probs{h}", [P, E_COLS]) for h in range(2)]
            probsT_hi = sb(mixing, "probsT_hi", [P, E_COLS], F32R)
            probsT_lo = sb(mixing, "probsT_lo", [P, E_COLS], F32R)
            q_both = sb(mixing, "q_both", [P, 2, SEQ], F32R)
            k_twice = sb(mixing, "k_twice", [P, 2, SEQ], F32R)
            k_lo = sb(mixing, "k_lo", [P, SEQ], F32R)
            v_both = [sb(mixing, f"v_both{n}", [P, TB, P], F32R) for n in range(2)]
            bias = sb(mixing, "bias", [P, 2, SEQ])
            vo = sb(mixing, "vo", [P, PAIRS, SEQ])
        with ExitStack() as later:
            h = sb(later, "h", [P, KT, SEQ])
            with ExitStack() as crossing:
                km_hi = sb(crossing, "km_hi", [P, X_HEADS, MEM_LEN], F32R)
                km_lo = sb(crossing, "km_lo", [P, X_HEADS, MEM_LEN], F32R)
                vm_hi = sb(crossing, "vm_hi", [P, MB, X_HEADS * P], F32R)
                vm_lo = sb(crossing, "vm_lo", [P, MB, X_HEADS * P], F32R)
                with ExitStack() as loading:
                    mem_raw = sb(loading, "mem_raw", [P, KT, MEM_LEN])
                    mem_hi = sb(loading, "mem_hi", [P, 4, MEM_LEN], F32R)
                    mem_lo = sb(loading, "mem_lo", [P, 4, MEM_LEN], F32R)
                    mem_rstd = sb(loading, "mem_rstd", [P, MEM_LEN])
                with ExitStack() as heads:
                    x_probs = sb(heads, "x_probs", [P, TB, MEM_LEN])
                    xpT_hi = sb(heads, "xpT_hi", [P, MB, SEQ], F32R)
                    xpT_lo = sb(heads, "xpT_lo", [P, MB, SEQ], F32R)
                    xq_hi = sb(heads, "xq_hi", [P, SEQ], F32R)
                    xq_lo = sb(heads, "xq_lo", [P, SEQ], F32R)
                    xo_hi = sb(heads, "xo_hi", [P, X_HEADS, SEQ], F32R)
                    xo_lo = sb(heads, "xo_lo", [P, X_HEADS, SEQ], F32R)
            with ExitStack() as feeding:
                g_hi = sb(feeding, "g_hi", [P, 2 * CH, SEQ], F32R)
                g_lo = sb(feeding, "g_lo", [P, 2 * CH, SEQ], F32R)
                gate_val = sb(feeding, "gate_val", [P, SEQ])
                up_val = sb(feeding, "up_val", [P, SEQ])

        ps = ctx.enter_context(nc.psum_tensor("ps", [P, 8, SEQ], F32))

        w_landed = [sem(f"w_landed{j}") for j in range(NJ)]
        w_hi_done = [sem(f"w_hi_done{j}") for j in range(NJ)]
        w_lo_done = [sem(f"w_lo_done{j}") for j in range(NJ)]
        w_used = [sem(f"w_used{j}") for j in range(NJ)]
        gains_landed = sem("gains_landed")
        tables_landed = sem("tables_landed")
        x_landed = [sem(f"x_landed{n}") for n in range(8)]
        x_again_landed = sem("x_again_landed")
        mem_landed = sem("mem_landed")
        bias_landed = [sem(f"bias_landed{n}") for n in range(2)]
        consts_set = sem("consts_set")
        act_hi_done = sem("act_hi_done")
        act_lo_done = sem("act_lo_done")
        out_scaled_a = sem("out_scaled_a")
        out_scaled_b = sem("out_scaled_b")
        out_scaled_c = sem("out_scaled_c")
        squared = sem("squared")
        square_added = sem("square_added")
        square_sum_clear = sem("square_sum_clear")
        out_squared = sem("out_squared")
        out_square_added = sem("out_square_added")
        last_out_squared = sem("last_out_squared")
        norm_summed = sem("norm_summed")
        norm_root = sem("norm_root")
        norm_ready = sem("norm_ready")
        v_copied = sem("v_copied")
        v_hi_done = sem("v_hi_done")
        v_lo_done = sem("v_lo_done")
        proj_raw_done = sem("proj_raw_done")
        proj_hi_done = [sem(f"proj_hi_done{n}") for n in range(2)]
        proj_lo_done = [sem(f"proj_lo_done{n}") for n in range(2)]
        k_doubled = sem("k_doubled")
        va_raw_done = sem("va_raw_done")
        va_turned = sem("va_turned")
        xq_raw_done = sem("xq_raw_done")
        xq_hi_done = sem("xq_hi_done")
        xq_lo_done = sem("xq_lo_done")
        scored = [[sem(f"scored{n}_{b}") for b in range(3)] for n in range(2)]
        max_taken = sem("max_taken")
        neg_ready = [sem(f"neg_ready{n}") for n in range(2)]
        exp_done = [sem(f"exp_done{n}") for n in range(2)]
        neg_taken = sem("neg_taken")
        sink_added = sem("sink_added")
        inv_done = [sem(f"inv_done{n}") for n in range(2)]
        probs_ready = [sem(f"probs_ready{n}") for n in range(2)]
        turned = [[sem(f"turned{n}_{b}") for b in range(3)] for n in range(2)]
        pT_hi_done = [[sem(f"pT_hi{n}_{b}") for b in range(3)] for n in range(2)]
        pT_lo_done = [[sem(f"pT_lo{n}_{b}") for b in range(3)] for n in range(2)]
        mixed = [sem(f"mixed{n}") for n in range(2)]
        out_lo_copied = [sem(f"out_lo_copied{n}") for n in range(2)]
        out_copied = [sem(f"out_copied{n}") for n in range(2)]
        h_added = sem("h_added")
        mem_hi_done = sem("mem_hi_done")
        mem_lo_done = sem("mem_lo_done")
        km_raw_done = sem("km_raw_done")
        km_hi_done = sem("km_hi_done")
        km_lo_done = sem("km_lo_done")
        vm_hi_done = sem("vm_hi_done")
        vm_lo_done = sem("vm_lo_done")
        x_scored = sem("x_scored")
        x_neg = sem("x_neg")
        x_exp = sem("x_exp")
        x_ready = sem("x_ready")
        x_turned = sem("x_turned")
        xpT_hi_done = sem("xpT_hi_done")
        xpT_lo_done = sem("xpT_lo_done")
        x_mixed = sem("x_mixed")
        xo_summed = sem("xo_summed")
        xo_hi_done = sem("xo_hi_done")
        xo_lo_done = sem("xo_lo_done")
        gate_scaled = sem("gate_scaled")
        gate_silu = sem("gate_silu")
        up_scaled = sem("up_scaled")
        g_raw_done = sem("g_raw_done")
        g_hi_done = sem("g_hi_done")
        g_lo_done = sem("g_lo_done")
        last_summed = sem("last_summed")
        gained = sem("gained")
        out_ready = [sem("out_ready_dve"), sem("out_ready_pool")]
        out_stored = sem("out_stored")

        def one(ap, i):
            if isinstance(i, int):
                return ap[:, i, :]
            return ap[:, bass.ds(i, 1), :].rearrange("p a n -> p (a n)")

        def passed(eng, semaphore, count):
            if not isinstance(count, int) or count > 0:
                eng.wait_ge(semaphore, count)

        def own_wait(eng, count):
            if not isinstance(count, int):
                eng.wait_ge(tables_landed, 32)

        def in_register(eng, count):
            return count if isinstance(count, int) else eng.snap(eng.to_reg(count))

        def k_event(pair):
            return 2 * min(pair, BC_PAIRS) + 1 if isinstance(pair, int) else 2 * pair + 1

        def q_event(pair):
            return BC_PAIRS + pair + 2 if isinstance(pair, int) and pair > BC_PAIRS else 2 * pair + 2

        def fill_quad(pair):
            return pair + (Q_BC + 1)

        def at(pair, n):
            return isinstance(pair, int) and pair == n

        def rows_of(n):
            return slice(n * HEAD_DIM, (n + 1) * HEAD_DIM)

        def layout(pair):
            return WINDOWED if isinstance(pair, int) and pair >= BC_PAIRS else CAUSAL

        out_engine = [0] * NJ * 2 + [int(n % NJ == NJ - 1) for n in range(NJ * 2)]

        def last_weights(ring, act, u):
            if u < NJ:
                return ring[:, u, :]
            return act[:, 2 * (u - NJ):2 * (u - NJ) + 2, :].rearrange("p a n -> p (a n)")

        def head_bank(n, b):
            return 2 + 3 * n + b

        def scale_out(eng, unit, i):
            half, n = i // UT, 2 * (i % UT)
            for k in (n, n + 1):
                eng.wait_ge(gained, half * KT + k + 1)
                last = unit.tensor_tensor(h[:, k, HALVES[half]], h[:, k, HALVES[half]], rstd[:, HALVES[half]], ALU.mult)
            last.then_inc(out_ready[out_engine[i]], 1)

        block = ctx.enter_context(nc.Block())

        @block.sync
        def _(sp):
            for c in range(8):
                if c < NJ:
                    sp.dma_start(w_raw[:, c, :], stream[c]).then_inc(w_landed[c], 16)
                sp.dma_start(x_raw[:, 2 * c:2 * c + 2, :],
                             xT[2 * c * P:(2 * c + 2) * P, :].rearrange("(k p) n -> p k n", p=P))\
                    .then_inc(x_landed[c], 16)
            sp.dma_start(sink[:, :], sinks).then_inc(tables_landed, 16)
            sp.dma_start(ident[:, :], identity).then_inc(tables_landed, 16)
            with sp.Fori(1, N_QUADS) as q:
                for j in range(NJ):
                    sp.wait_ge(w_lo_done[j], q)
                    sp.dma_start(w_raw[:, j, :], stream[bass.ds(q * NJ + j, 1)].rearrange("a p n -> (a p) n"))\
                        .then_inc(w_landed[j], 16)
            for i, engine in enumerate(out_engine):
                sp.wait_ge(out_ready[engine], out_engine[:i + 1].count(engine))
                n, tok = 2 * (i % UT), HALVES[i // UT]
                sp.dma_start(outT[n * P:(n + 2) * P, tok].rearrange("(k p) n -> p k n", p=P), h[:, n:n + 2, tok])\
                    .then_inc(out_stored, 16)
            sp.wait_ge(out_stored, 16 * len(out_engine))

        @block.gpsimd
        def _(pool):
            nc.gpsimd.memset(eps, EPS).then_inc(consts_set, 1)
            nc.gpsimd.memset(ones[:, :], 1.0).then_inc(consts_set, 1)
            nc.gpsimd.memset(square_sum[:, :, :], 0.0).then_inc(square_sum_clear, 1)

            def load_bias(pair):
                for n in range(2):
                    if not isinstance(pair, int) or pair > 0:
                        pool.wait_ge(neg_ready[n], pair)
                    pool.dma_start(bias[:, n, :], bias_table[bass.ds(pair * 2 + n, 1)].rearrange("a p n -> (a p) n"))\
                        .then_inc(bias_landed[n], 16)

            def clear_sum(slot, summed, cleared):
                pool.wait_ge(norm_summed, summed)
                nc.gpsimd.memset(square_sum[:, slot, :], 0.0).then_inc(square_sum_clear, 1)
                pool.wait_ge(square_sum_clear, cleared)

            def add_squares(base, slot, width, tiles=KT, first=0):
                for k in range(tiles):
                    pool.wait_ge(squared, base + k + 1)
                    if k:
                        pool.wait_ge(square_added, base + k)
                    sums = square_sum[:, slot, first:first + width]
                    nc.gpsimd.tensor_tensor(sums, sums, squares[:, k % 2, :width], ALU.add).then_inc(square_added, 1)

            pool.wait_ge(square_sum_clear, 1)
            add_squares(0, SLOT_X, SEQ)
            pool.wait_ge(act_lo_done, KT)
            load_bias(0)

            def add_out_squares(slot, pair):
                for n in range(2):
                    pool.wait_ge(out_copied[n], pair + 1)
                passed(pool, out_square_added, pair)
                nc.gpsimd.tensor_tensor(squares[:, 0, :], one(vo, pair), one(vo, pair), ALU.mult)\
                    .then_inc(out_squared, 1)
                pool.wait_ge(out_squared, pair + 1)
                nc.gpsimd.tensor_tensor(square_sum[:, slot, :], square_sum[:, slot, :], squares[:, 0, :],
                                        ALU.add).then_inc(out_square_added, 1)

            load_bias(1)
            add_out_squares(SLOT_B, 0)
            with pool.Fori(1, B_PAIRS) as pair:
                load_bias(pair + 1)
                add_out_squares(SLOT_B, pair)
            clear_sum(SLOT_C, S_X, 2)
            with pool.Fori(B_PAIRS, BC_PAIRS) as pair:
                load_bias(pair + 1)
                add_out_squares(SLOT_C, pair)
            load_bias(BC_PAIRS + 1)
            clear_sum(SLOT_A, S_B, 3)

            def scale_outs(done, event, inverse, first, count):
                pool.wait_ge(norm_ready, event)
                for t in range(first, first + count):
                    nc.gpsimd.tensor_tensor(vo[:, t, :], vo[:, t, :], inverse, ALU.mult).then_inc(done, 1)

            scale_outs(out_scaled_b, R_B, root[:, :], 0, B_PAIRS)
            scale_outs(out_scaled_c, R_C, squares[:, 1, :], B_PAIRS, C_PAIRS)
            for pair in range(BC_PAIRS, PAIRS - 1):
                if pair > BC_PAIRS:
                    load_bias(pair + 1)
                add_out_squares(SLOT_A, pair)
            pool.wait_ge(out_copied[1], PAIRS)
            pool.dma_start(h[:, :, :], xT.rearrange("(k p) n -> p k n", p=P)).then_inc(x_again_landed, 16)
            pool.wait_ge(act_lo_done, 2 * KT)
            pool.dma_start(mem_raw[:, :, :], memT.rearrange("(k p) n -> p k n", p=P)).then_inc(mem_landed, 16)
            clear_sum(SLOT_H1, S_C, 4)
            add_squares(1 * KT, SLOT_H1, SEQ)
            clear_sum(SLOT_MEM, S_A, 5)
            add_squares(2 * KT, SLOT_MEM, MEM_LEN)
            clear_sum(SLOT_H2, S_H1, 6)
            add_squares(3 * KT, SLOT_H2, SEQ)
            clear_sum(SLOT_FIN, S_MEM, 7)
            add_squares(4 * KT, SLOT_FIN, HALF)
            add_squares(5 * KT, SLOT_FIN, HALF, KT - 2, HALF)
            pool.wait_ge(norm_ready, R_FIN + 1)
            for i, engine in enumerate(out_engine):
                if engine == 1:
                    scale_out(pool, nc.gpsimd, i)

        @block.scalar
        def _(act):
            act.dma_start(gain[:, :], gains).then_inc(gains_landed, 16)
            act.wait_ge(consts_set, 1)
            nc.scalar.activation(spare, eps, ACT.Copy)

            def split(q, j):
                act.wait_ge(w_landed[j], q * 16 + 16)
                passed(act, w_used[j], q)
                nc.scalar.activation(w_hi[:, j, :], w_raw[:, j, :], ACT.Copy).then_inc(w_hi_done[j], 1)

            def scaled_hi(k, src, column):
                nc.scalar.activation(one(act_hi, k), src, ACT.Copy, scale=gain_col(column, k)).then_inc(act_hi_done, 1)

            def gain_col(column, k):
                if isinstance(k, int):
                    return gain[:, column + k:column + k + 1]
                return gain[:, bass.ds(k + column, 1)]

            def square(count, src, width=SEQ):
                passed(act, square_added, count - 1)
                nc.scalar.activation(squares[:, count % 2, :width], src, ACT.Square).then_inc(squared, 1)

            def take_root(summed, event, dst, src, n_features, inverted=None):
                act.wait_ge(norm_summed, summed)
                passed(act, norm_ready, event - 1 if inverted is None else inverted)
                nc.scalar.activation(dst, src, ACT.Sqrt, bias=eps, scale=1.0 / n_features).then_inc(norm_root, 1)

            def k_hi(pair):
                for n in range(2):
                    act.wait_ge(proj_raw_done, k_event(pair))
                    nc.scalar.activation(k_twice[rows_of(n), n, :], proj_raw[rows_of(n), :], ACT.Copy)\
                        .then_inc(proj_hi_done[n], 1)
                for n in range(2):
                    last = nc.scalar.activation(k_twice[rows_of(1 - n), n, :], proj_raw[rows_of(n), :], ACT.Copy)
                last.then_inc(k_doubled, 1)

            def q_hi(pair):
                for n in range(2):
                    act.wait_ge(proj_raw_done, q_event(pair))
                    nc.scalar.activation(q_both[rows_of(n), n, :], proj_raw[rows_of(n), :], ACT.Copy)\
                        .then_inc(proj_hi_done[n], 1)

            act.wait_ge(gains_landed, 16)
            for u in range(2 * NJ):
                split(u // NJ, u % NJ)
                act.wait_ge(x_landed[u], 16)
                for k in (2 * u, 2 * u + 1):
                    scaled_hi(k, x_raw[:, k, :], G_MIX)
                    square(k, x_raw[:, k, :])
            act.wait_ge(tables_landed, 32)
            act.wait_ge(consts_set, 2)
            for u in range(2 * NJ, NJ * (Q_BC + 1) + 3):
                split(u // NJ, u % NJ)
                if u == 9:
                    take_root(S_X, R_X, root[:, :], ps[:, 4, :], D_MODEL)
                    take_root(S_X, R_XCOL, root_col, ps[:, 5, 0:TB], D_MODEL)
                if u < NJ * Q_BC + NJ and u % 8 == 3:
                    group = u // 8 - 1
                    act.wait_ge(w_used[3], 2 * group + 2)
                    act.wait_ge(norm_ready, R_XCOL)
                    for b in range(TB):
                        slots = vo[:, NJ * group:NJ * (group + 1), b * P:(b + 1) * P]
                        nc.scalar.activation(slots, ps[:, 4 * (group % 2) + b, :].rearrange("p (s n) -> p s n", n=P),
                                             ACT.Copy, scale=rstd_col[:, b:b + 1]).then_inc(v_copied, 1)
                if u == NJ * Q_BC + 5:
                    k_hi(0)
            q_hi(0)

            def stage_v(pair, src=None):
                if at(pair, 0):
                    act.wait_ge(v_copied, 3 * TB)
                else:
                    own_wait(act, pair)
                    act.wait_ge(mixed[1], pair)
                v = (one(vo, pair) if src is None else src).rearrange("p (b n) -> p b n", n=P)
                for n in range(2):
                    last = nc.scalar.activation(v_both[n][:, :, rows_of(n)], v[:, :, rows_of(n)], ACT.Copy)
                last.then_inc(v_hi_done, 1)

            def exponentials(n, pair, with_sink):
                act.wait_ge(neg_ready[n], pair + 1)
                if with_sink:
                    nc.scalar.activation(sink_exp[n], sink_arg[n], ACT.Exp)
                for i, _, w, c, _ in layout(pair).rows:
                    last = nc.scalar.activation(probs[n][:, c:c + w], probs[n][:, c:c + w], ACT.Exp,
                                                bias=neg_max[n][:, i:i + 1], accum_out=row_sum[n][:, i:i + 1])
                last.then_inc(exp_done[n], 1)

            def turned_hi(n, pair):
                lay = layout(pair)
                for b in range(lay.banks):
                    act.wait_ge(turned[n][b], pair + 1)
                    w = lay.widths[b]
                    nc.scalar.activation(probsT_hi[:, b * SEQ:b * SEQ + w], ps[:, head_bank(n, b), :w], ACT.Copy)\
                        .then_inc(pT_hi_done[n][b], 1)

            def copy_out(n, pair):
                own_wait(act, pair)
                act.wait_ge(mixed[n], pair + 1)
                rows = rows_of(n)
                dst = vo[rows, pair, :] if isinstance(pair, int) else \
                    vo[rows, bass.ds(pair, 1), :].rearrange("p a n -> p (a n)")
                nc.scalar.activation(dst, ps[rows_of(1 - n), head_bank(n, 2), :], ACT.Copy)\
                    .then_inc(out_lo_copied[n], 1)

            def out_hi(t):
                if t < C_PAIRS:
                    act.wait_ge(out_scaled_c, t + 1)
                elif t < BC_PAIRS:
                    act.wait_ge(out_scaled_b, t - C_PAIRS + 1)
                else:
                    act.wait_ge(out_scaled_a, t - BC_PAIRS + 1)
                scaled_hi(t, vo[:, OUT_ORDER[t], :], G_OUT)

            def cycle(pair):
                f = fill_quad(pair)
                if not at(pair, 0):
                    turned_hi(1, pair - 1)
                    copy_out(1, pair - 1)
                stage_v(pair)
                exponentials(0, pair, False)
                split(f, 3)
                exponentials(1, pair, False)
                split(f + 1, 0)
                split(f + 1, 1)
                turned_hi(0, pair)
                k_hi(pair + 1)
                split(f + 1, 2)
                copy_out(0, pair)
                q_hi(pair + 1)

            def last_cycle(m):
                pair = BC_PAIRS + m
                turned_hi(1, pair - 1)
                for t in {2: range(6), 3: range(C_PAIRS, BC_PAIRS)}.get(m, ()):
                    if t % 8 == 0:
                        act.wait_ge(w_used[2 + t // 8], Q_QA + 1)
                    out_hi(t)
                copy_out(1, pair - 1)
                exponentials(0, pair, True)
                if m < 2:
                    split(Q_VA + m, 3)
                if m == 2:
                    for t in range(6, C_PAIRS):
                        out_hi(t)
                exponentials(1, pair, True)
                if m == 0:
                    take_root(S_B, R_B, root[:, :], ps[:, 4, :], B_PAIRS * P)
                    take_root(S_C, R_C, squares[:, 1, :], ps[:, 7, :], C_PAIRS * P, R_B - 1)
                early = ((Q_QA, 0), (Q_OUT, 0), (Q_OUT, 2), (Q_OUT, 3))[m]
                late = ((Q_QA, 1), (Q_OUT, 1), None, None)[m]
                turned_hi(0, pair)
                if m == 0:
                    act.wait_ge(va_turned, 1)
                    stage_v(BC_PAIRS, ps[:, 1, :])
                split(*early)
                if m == 0:
                    split(*late)
                    split(Q_QA, 2)
                    copy_out(0, pair)
                    q_hi(pair + 1)
                else:
                    if m < 3:
                        q_hi(pair + 1)
                    copy_out(0, pair)
                    if late:
                        split(*late)

            cycle(0)
            with act.Fori(1, BC_PAIRS) as pair:
                cycle(pair)
            for m in range(A_PAIRS):
                last_cycle(m)
            turned_hi(1, PAIRS - 1)
            split(Q_OUT + 1, 0)
            copy_out(1, PAIRS - 1)
            act.wait_ge(out_square_added, PAIRS - 1)
            for n in range(2):
                act.wait_ge(out_copied[n], PAIRS)
            nc.scalar.activation(squares[:, 0, :], vo[:, PAIRS - 1, :], ACT.Square).then_inc(last_out_squared, 1)
            split(Q_OUT + 1, 1)
            split(Q_OUT + 1, 2)
            split(Q_OUT + 1, 3)
            act.wait_ge(out_scaled_b, B_PAIRS)
            take_root(S_A, R_A, root[:, :], ps[:, 5, :], A_PAIRS * P)
            for t in range(BC_PAIRS, PAIRS):
                out_hi(t)

            def square_h(count, n):
                act.wait_ge(square_added, count - 1)
                nc.scalar.activation(squares[:, n % 2, :], h[:, n, :], ACT.Square).then_inc(squared, 1)

            for j in range(2):
                split(Q_OUT + 2, j)
            for n in range(4):
                act.wait_ge(h_added, n + 1)
                square_h(KT + n, n)
                if n % 2:
                    split(Q_OUT + 2, 2 + n // 2)

            def out_quad(g):
                q = g + (Q_OUT + 1)
                for j in range(3):
                    split(q, j)
                for m in range(2):
                    if m:
                        split(q, 3)
                    own_wait(act, g)
                    act.wait_ge(h_added, g * 2 + (m + 1))
                    act.wait_ge(square_added, g * 2 + (KT + m - 1))
                    nc.scalar.activation(squares[:, m, :], one(h, g * 2 + m), ACT.Square).then_inc(squared, 1)

            with act.Fori(2, KT // 2 - 1) as g:
                out_quad(g)

            def mem_part(k):
                if k >= 4:
                    act.wait_ge(w_used[k % NJ], Q_MEM + k // NJ)
                nc.scalar.activation(mem_hi[:, k % 4, :], mem_raw[:, k, :], ACT.Copy,
                                     scale=gain_col(G_MEM, k)).then_inc(mem_hi_done, 1)

            act.wait_ge(mem_landed, 16)
            for k in range(4):
                mem_part(k)
            out_quad(KT // 2 - 1)
            act.wait_ge(w_used[3], Q_MEM)
            for k in range(KT):
                split(Q_MEM + 1 + k // NJ, k % NJ)
                if k + 4 < KT:
                    mem_part(k + 4)
                scaled_hi(k, h[:, k, :], G_X)
                square(2 * KT + k, mem_raw[:, k, :], MEM_LEN)
                if k == 7:
                    take_root(S_H1, R_H1, root[:, :], ps[:, 0, :], D_MODEL)

            def x_query_hi(n):
                act.wait_ge(xq_raw_done, n + 1)
                nc.scalar.activation(xq_hi[:, :], proj_raw[:, :], ACT.Copy).then_inc(xq_hi_done, 1)

            split(Q_XQ + 1, 0)
            split(Q_XQ + 1, 1)
            x_query_hi(0)
            take_root(S_MEM, R_MEM, root[:, :MEM_LEN], ps[:, 2, MEM_LEN:], D_MODEL)
            take_root(S_MEM, R_MEMCOL, root_col[:, :MB], ps[:, 3, MEM_LEN:MEM_LEN + MB], D_MODEL, R_H1)
            for n in range(X_HEADS):
                act.wait_ge(km_raw_done, n + 1)
                nc.scalar.activation(km_hi[:, n, :], proj_raw[:, (n % 2) * MEM_LEN:(n % 2 + 1) * MEM_LEN], ACT.Copy)\
                    .then_inc(km_hi_done, 1)
            act.wait_ge(norm_ready, R_MEMCOL)
            for b in range(MB):
                nc.scalar.activation(vm_hi[:, b, :], ps[:, 6 + b, :], ACT.Copy,
                                     scale=rstd_col[:, b:b + 1]).then_inc(vm_hi_done, 1)

            def x_exponentials(n):
                act.wait_ge(x_neg, n + 1)
                for i in range(TB):
                    scored_row = ps[:, 2 + i // 2, (i % 2) * MEM_LEN:(i % 2 + 1) * MEM_LEN]
                    last = nc.scalar.activation(x_probs[:, i, :], scored_row, ACT.Exp, bias=neg_max[0][:, i:i + 1],
                                                accum_out=row_sum[0][:, i:i + 1])
                last.then_inc(x_exp, 1)

            def x_turned_hi(n):
                act.wait_ge(x_turned, n + 1)
                for b in range(MB):
                    nc.scalar.activation(xpT_hi[:, b, :], ps[:, 4 + b, :], ACT.Copy).then_inc(xpT_hi_done, 1)

            def x_out_hi(n):
                act.wait_ge(x_mixed, n + 1)
                nc.scalar.activation(xo_hi[:, n, :], ps[:, X_OUT_BANKS[n], :], ACT.Copy).then_inc(xo_hi_done, 1)

            split(Q_XQ + 1, 2)
            split(Q_XQ + 1, 3)
            x_exponentials(0)
            x_query_hi(1)
            for n in range(2):
                split(Q_XO, 2 * n)
                x_turned_hi(n)
                x_exponentials(n + 1)
                x_out_hi(n)
                x_query_hi(n + 2)
                split(Q_XO, 2 * n + 1)
            x_turned_hi(2)
            split(Q_XO + 1, 0)
            x_exponentials(3)
            x_out_hi(2)
            x_turned_hi(3)
            split(Q_XO + 1, 1)
            split(Q_XO + 1, 2)
            x_out_hi(3)
            split(Q_XO + 1, 3)

            for n in range(KT):
                if n % CH == CH - 1:
                    split(Q_FFN, n // CH)
                act.wait_ge(h_added, 2 * KT + n + 1)
                scaled_hi(n, h[:, n, :], G_FFN)
                square_h(3 * KT + n, n)

            def gate_up(c, f, q):
                tile = c * CH + f
                split(q + 1, 0)
                split(q + 1, 1)
                act.wait_ge(gate_scaled, tile + 1)
                nc.scalar.activation(gate_val[:, :], gate_val[:, :], ACT.Silu).then_inc(gate_silu, 1)
                split(q + 1, 2)
                split(q + 1, 3)
                own_wait(act, c)
                act.wait_ge(g_raw_done, tile + 1)
                nc.scalar.activation(one(g_hi, (c % 2) * CH + f), up_val[:, :], ACT.Copy).then_inc(g_hi_done, 1)

            for f in range(CH):
                if f == 0:
                    take_root(S_H2, R_H2, root[:, :], ps[:, 0, :], D_MODEL)
                gate_up(0, f, Q_FFN + f)
            with act.Fori(0, NCH - 1) as c:
                q = c * (CH + 2) + (Q_FFN + CH)
                for f in range(CH):
                    gate_up(c + 1, f, q + f)
                for u in range(2 * NJ):
                    split(q + (CH + 1 + u // NJ), u % NJ)

            def gain_h(half, n):
                act.wait_ge(squared, (4 + half) * KT + n + 1)
                nc.scalar.activation(h[:, n, HALVES[half]], h[:, n, HALVES[half]], ACT.Copy, scale=gain_col(G_FIN, n))\
                    .then_inc(gained, 1)

            def split_last(j):
                act.wait_ge(w_landed[j], N_QUADS * 16)
                nc.scalar.activation(last_weights(w_hi, act_hi, NJ + j), w_raw[:, j, :], ACT.Copy)\
                    .then_inc(w_hi_done[j], 1)

            split_last(0)
            nc.scalar.activation(spare, eps, ACT.Sqrt)
            for half in range(2):
                for n in range(KT):
                    count = half * KT + n
                    if half == 0 and n in (0, 2, 4):
                        split_last(n // 2 + 1)
                    act.wait_ge(h_added, (3 + NCH - 1) * KT + count + 1)
                    act.wait_ge(square_added, 4 * KT + count - 1)
                    nc.scalar.activation(squares[:, n % 2, :HALF], h[:, n, HALVES[half]], ACT.Square)\
                        .then_inc(squared, 1)
                    if n and (half == 0 or n < KT - 2):
                        gain_h(half, n - 1)
                    if half == 1 and n == 3:
                        take_root(S_FIN, R_FIN, root[:, HALVES[0]], ps[:, 4, :HALF], D_MODEL)
                if half == 0:
                    gain_h(half, KT - 1)
            take_root(S_FIN + 1, R_FIN + 1, root[:, HALVES[1]], ps[:, 5, :HALF], D_MODEL)
            for n in range(KT - 3, KT):
                gain_h(1, n)

        @block.vector
        def _(dve):
            def split(q, j):
                dve.wait_ge(w_hi_done[j], q + 1)
                nc.vector.tensor_tensor(w_lo[:, j, :], w_raw[:, j, :], w_hi[:, j, :].bitcast(F32), ALU.subtract)\
                    .then_inc(w_lo_done[j], 1)

            def scaled_lo(event, k, src, column):
                dve.wait_ge(act_hi_done, event)
                nc.vector.scalar_tensor_tensor(act_lo[:, k, :], src, gain[:, column + k:column + k + 1],
                                               act_hi[:, k, :].bitcast(F32), ALU.mult, ALU.subtract)\
                    .then_inc(act_lo_done, 1)

            def invert(event, dst, src):
                dve.wait_ge(norm_root, event)
                nc.vector.reciprocal(dst, src).then_inc(norm_ready, 1)

            dve.wait_ge(gains_landed, 16)
            for u in range(2 * NJ):
                split(u // NJ, u % NJ)
                dve.wait_ge(x_landed[u], 16)
                for k in (2 * u, 2 * u + 1):
                    scaled_lo(k + 1, k, x_raw[:, k, :], G_MIX)

            def stage_v(pair, src=None):
                dve.wait_ge(v_hi_done, pair + 1)
                v = (one(vo, pair) if src is None else src).rearrange("p (b n) -> p b n", n=P)
                for n in range(2):
                    last = nc.vector.tensor_tensor(v_both[n][:, :, rows_of(1 - n)], v[:, :, rows_of(n)],
                                                   v_both[n][:, :, rows_of(n)].bitcast(F32), ALU.subtract)
                last.then_inc(v_lo_done, 1)

            def add_out(n, pair):
                own_wait(dve, pair)
                dve.wait_ge(out_lo_copied[n], pair + 1)
                rows = rows_of(n)
                dst = vo[rows, pair, :] if isinstance(pair, int) else \
                    vo[rows, bass.ds(pair, 1), :].rearrange("p a n -> p (a n)")
                nc.vector.tensor_tensor(dst, ps[rows, head_bank(n, 2), :], dst, ALU.add).then_inc(out_copied[n], 1)

            def proj_scaled(event, q, j, bank, scale):
                dve.wait_ge(w_used[j], q + 1)
                for n in range(2):
                    passed(dve, proj_lo_done[n], event - 1)
                return nc.vector.scalar_tensor_tensor(proj_raw[:, :], ps[:, bank, :], scale, rstd[:, :],
                                                      ALU.mult, ALU.mult)

            def key(pair, q, bank=1):
                e = k_event(pair)
                proj_scaled(e, q, 1, bank, 1.0).then_inc(proj_raw_done, 1)
                for n in range(2):
                    dve.wait_ge(proj_hi_done[n], e)
                    nc.vector.tensor_tensor(k_lo[rows_of(n), :], proj_raw[rows_of(n), :],
                                            k_twice[rows_of(n), n, :].bitcast(F32), ALU.subtract)\
                        .then_inc(proj_lo_done[n], 1)

            def query(pair, q, j=3, bank=0):
                e = q_event(pair)
                dve.wait_ge(k_doubled, min(pair, BC_PAIRS) + 1 if isinstance(pair, int) else pair + 1)
                proj_scaled(e, q, j, bank, MIX_SCALE).then_inc(proj_raw_done, 1)
                for n in range(2):
                    dve.wait_ge(proj_hi_done[n], e)
                    nc.vector.tensor_tensor(q_both[rows_of(1 - n), n, :], proj_raw[rows_of(n), :],
                                            q_both[rows_of(n), n, :].bitcast(F32), ALU.subtract)\
                        .then_inc(proj_lo_done[n], 1)

            for u in range(2 * NJ, NJ * (Q_BC + 1) + 3):
                split(u // NJ, u % NJ)
                if u == 9:
                    invert(R_X, rstd[:, :], root[:, :])
                    invert(R_XCOL, rstd_col, root_col)
                    dve.wait_ge(norm_ready, R_X)
                if u == NJ * Q_BC + 5:
                    key(0, Q_BC, 7)
            query(0, Q_BC)

            def maxima(n, pair, with_sink):
                lay = layout(pair)
                landed = in_register(dve, pair * 16 + 16)
                count = in_register(dve, pair + 1)
                bank = -1
                col = 2 * (pair - BC_PAIRS) + n if with_sink else 0
                for m, (i, _, w, c, bias_at) in enumerate(lay.rows):
                    if c // SEQ != bank:
                        bank = c // SEQ
                        own_wait(dve, pair)
                        if m == 0:
                            dve.wait_ge(bias_landed[n], landed)
                        dve.wait_ge(scored[n][bank], count)
                    first = sink[:, col:col + 1] if with_sink else LOWEST
                    nc.vector.tensor_tensor_reduce(probs[n][:, c:c + w], ps[:, head_bank(n, bank), c % SEQ:c % SEQ + w],
                                                   bias[:, n, bias_at:bias_at + w], 1.0, first, ALU.add, ALU.max,
                                                   row_max[n][:, i:i + 1]).then_inc(max_taken, 1)
                dve.wait_ge(max_taken, pair * (2 * TB) + (n + 1) * TB)
                last = nc.vector.tensor_scalar(neg_max[n], row_max[n], -1.0, None, ALU.mult)
                if with_sink:
                    last.then_inc(neg_taken, 1)
                    dve.wait_ge(neg_taken, col + 1)
                    last = nc.vector.tensor_scalar(sink_arg[n], neg_max[n], sink[:, col:col + 1], None, ALU.add)
                last.then_inc(neg_ready[n], 1)

            def normalize(n, pair, with_sink):
                dve.wait_ge(exp_done[n], pair + 1)
                if with_sink:
                    nc.vector.tensor_tensor(row_sum[n], row_sum[n], sink_exp[n], ALU.add).then_inc(sink_added, 1)
                    dve.wait_ge(sink_added, 2 * (pair - BC_PAIRS) + n + 1)
                nc.vector.reciprocal(row_inv[n], row_sum[n]).then_inc(inv_done[n], 1)
                count = in_register(dve, pair + 1)
                own_wait(dve, pair)
                dve.wait_ge(inv_done[n], count)
                for i, _, w, c, _ in layout(pair).rows:
                    weights = probs[n][:, c:c + w]
                    last = nc.vector.tensor_scalar(weights, weights, row_inv[n][:, i:i + 1], None, ALU.mult)
                last.then_inc(probs_ready[n], 1)

            def turned_lo(n, pair):
                lay = layout(pair)
                for b in range(lay.banks):
                    dve.wait_ge(pT_hi_done[n][b], pair + 1)
                    w = lay.widths[b]
                    nc.vector.tensor_tensor(probsT_lo[:, b * SEQ:b * SEQ + w], ps[:, head_bank(n, b), :w],
                                            probsT_hi[:, b * SEQ:b * SEQ + w].bitcast(F32), ALU.subtract)\
                        .then_inc(pT_lo_done[n][b], 1)

            def out_lo(t):
                scaled_lo(KT + t + 1, t, vo[:, OUT_ORDER[t], :], G_OUT)

            def cycle(pair):
                f = fill_quad(pair)
                if not at(pair, 0):
                    turned_lo(1, pair - 1)
                maxima(0, pair, False)
                if not at(pair, 0):
                    add_out(1, pair - 1)
                stage_v(pair)
                maxima(1, pair, False)
                normalize(0, pair, False)
                split(f, 3)
                normalize(1, pair, False)
                split(f + 1, 0)
                split(f + 1, 1)
                turned_lo(0, pair)
                key(pair + 1, f)
                split(f + 1, 2)
                add_out(0, pair)
                query(pair + 1, f)

            def last_cycle(m):
                pair = BC_PAIRS + m
                turned_lo(1, pair - 1)
                if m == 2:
                    for t in range(4):
                        out_lo(t)
                maxima(0, pair, True)
                add_out(1, pair - 1)
                maxima(1, pair, True)
                normalize(0, pair, True)
                if m == 3:
                    for t in range(C_PAIRS, BC_PAIRS):
                        out_lo(t)
                if m < 2:
                    split(Q_VA + m, 3)
                if m == 2:
                    for t in range(4, C_PAIRS):
                        out_lo(t)
                if m < 2:
                    normalize(1, pair, True)
                if m == 0:
                    proj_scaled(q_event(pair) + 1, Q_VA, 1, 1, 1.0).then_inc(va_raw_done, 1)
                early = ((Q_QA, 0), (Q_OUT, 0), (Q_OUT, 2), (Q_OUT, 3))[m]
                late = ((Q_QA, 1), (Q_OUT, 1), None, None)[m]
                turned_lo(0, pair)
                if m >= 2:
                    normalize(1, pair, True)
                if m == 0:
                    stage_v(BC_PAIRS, ps[:, 1, :])
                split(*early)
                if m == 0:
                    invert(R_B, root[:, :], root[:, :])
                    invert(R_C, squares[:, 1, :], squares[:, 1, :])
                    split(*late)
                    split(Q_QA, 2)
                    add_out(0, pair)
                    query(pair + 1, Q_VA)
                else:
                    if m < 3:
                        query(pair + 1, Q_QA, 2 * m - 1, 2 - m)
                    add_out(0, pair)
                    if late:
                        split(*late)

            cycle(0)
            with dve.Fori(1, BC_PAIRS) as pair:
                cycle(pair)
            for m in range(A_PAIRS):
                last_cycle(m)
            turned_lo(1, PAIRS - 1)
            split(Q_OUT + 1, 0)
            add_out(1, PAIRS - 1)
            split(Q_OUT + 1, 1)
            split(Q_OUT + 1, 2)
            split(Q_OUT + 1, 3)
            invert(R_A, root[:, :], root[:, :])
            dve.wait_ge(norm_ready, R_A)
            for t in range(BC_PAIRS, PAIRS):
                nc.vector.tensor_tensor(vo[:, t, :], vo[:, t, :], root[:, :], ALU.mult).then_inc(out_scaled_a, 1)
            for t in range(BC_PAIRS, PAIRS):
                out_lo(t)

            def add_to_h(n, bank):
                nc.vector.tensor_tensor(one(h, n), ps[:, bank, :], one(h, n), ALU.add).then_inc(h_added, 1)

            dve.wait_ge(x_again_landed, 16)
            for j in range(2):
                split(Q_OUT + 2, j)
            for n in range(4):
                dve.wait_ge(w_used[2 + n // 2], Q_OUT + 2)
                add_to_h(n, OUT_BANKS[n])
                if n % 2:
                    split(Q_OUT + 2, 2 + n // 2)

            def out_quad(g):
                q = g + Q_OUT
                for j in range(2):
                    split(q + 1, j)
                for m in range(2):
                    dve.wait_ge(w_used[2 + m], q + 1)
                    add_to_h(g * 2 + m, m)
                    split(q + 1, 2 + m)

            with dve.Fori(2, KT // 2 - 1) as g:
                out_quad(g)

            def mem_part(k):
                dve.wait_ge(mem_hi_done, k + 1)
                nc.vector.scalar_tensor_tensor(mem_lo[:, k % 4, :], mem_raw[:, k, :], gain[:, G_MEM + k:G_MEM + k + 1],
                                               mem_hi[:, k % 4, :].bitcast(F32), ALU.mult, ALU.subtract)\
                    .then_inc(mem_lo_done, 1)

            for k in range(4):
                mem_part(k)
            out_quad(KT // 2 - 1)
            for k in range(KT):
                split(Q_MEM + 1 + k // NJ, k % NJ)
                if k + 4 < KT:
                    mem_part(k + 4)
                scaled_lo(2 * KT + k + 1, k, h[:, k, :], G_X)
                if k == 7:
                    invert(R_H1, rstd[:, :], root[:, :])
                    dve.wait_ge(norm_ready, R_H1)

            def x_query_raw(n):
                dve.wait_ge(w_used[2 * (n % 2) + 1], Q_XQ + n // 2 + 1)
                passed(dve, xq_lo_done, n)
                if n == 1:
                    dve.wait_ge(km_lo_done, X_HEADS)
                nc.vector.scalar_tensor_tensor(proj_raw[:, :], ps[:, n % 2, :], X_SCALE, rstd[:, :], ALU.mult, ALU.mult)\
                    .then_inc(xq_raw_done, 1)

            def x_query_lo(n):
                dve.wait_ge(xq_hi_done, n + 1)
                nc.vector.tensor_tensor(xq_lo[:, :], proj_raw[:, :], xq_hi[:, :].bitcast(F32), ALU.subtract)\
                    .then_inc(xq_lo_done, 1)

            split(Q_XQ + 1, 0)
            split(Q_XQ + 1, 1)
            x_query_raw(0)
            x_query_lo(0)
            invert(R_MEM, mem_rstd[:, :], root[:, :MEM_LEN])
            invert(R_MEMCOL, rstd_col[:, :MB], root_col[:, :MB])
            dve.wait_ge(norm_ready, R_MEMCOL)
            dve.wait_ge(xq_lo_done, 1)

            def km_lo_half(n):
                dve.wait_ge(km_hi_done, n + 1)
                nc.vector.tensor_tensor(km_lo[:, n, :], proj_raw[:, (n % 2) * MEM_LEN:(n % 2 + 1) * MEM_LEN],
                                        km_hi[:, n, :].bitcast(F32), ALU.subtract).then_inc(km_lo_done, 1)

            for n in range(X_HEADS):
                passed(dve, km_lo_done, n - 1)
                nc.vector.tensor_tensor(proj_raw[:, (n % 2) * MEM_LEN:(n % 2 + 1) * MEM_LEN], ps[:, 2 + n, :MEM_LEN],
                                        mem_rstd[:, :], ALU.mult).then_inc(km_raw_done, 1)
                if n:
                    km_lo_half(n - 1)
            km_lo_half(X_HEADS - 1)
            for b in range(MB):
                dve.wait_ge(vm_hi_done, b + 1)
                nc.vector.scalar_tensor_tensor(vm_lo[:, b, :], ps[:, 6 + b, :], rstd_col[:, b:b + 1],
                                               vm_hi[:, b, :].bitcast(F32), ALU.mult, ALU.subtract)\
                    .then_inc(vm_lo_done, 1)

            def x_maxima(n):
                dve.wait_ge(x_scored, n + 1)
                nc.vector.tensor_reduce(row_max[0], ps[:, 2:4, :].rearrange("p b (i n) -> p (b i) n", n=MEM_LEN),
                                        AX_X, ALU.max).then_inc(max_taken, 1)
                dve.wait_ge(max_taken, PAIRS * 2 * TB + n + 1)
                nc.vector.tensor_scalar(neg_max[0], row_max[0], -1.0, None, ALU.mult).then_inc(x_neg, 1)

            def x_normalize(n):
                dve.wait_ge(x_exp, n + 1)
                nc.vector.reciprocal(row_inv[0], row_sum[0]).then_inc(inv_done[0], 1)
                dve.wait_ge(inv_done[0], PAIRS + n + 1)
                for i in range(TB):
                    last = nc.vector.tensor_scalar(x_probs[:, i, :], x_probs[:, i, :], row_inv[0][:, i:i + 1], None,
                                                   ALU.mult)
                last.then_inc(x_ready, 1)

            def x_turned_lo(n):
                for b in range(MB):
                    dve.wait_ge(xpT_hi_done, MB * n + b + 1)
                    nc.vector.tensor_tensor(xpT_lo[:, b, :], ps[:, 4 + b, :], xpT_hi[:, b, :].bitcast(F32),
                                            ALU.subtract).then_inc(xpT_lo_done, 1)

            def x_out_lo(n):
                dve.wait_ge(xo_hi_done, n + 1)
                nc.vector.tensor_tensor(xo_lo[:, n, :], ps[:, X_OUT_BANKS[n], :], xo_hi[:, n, :].bitcast(F32),
                                        ALU.subtract).then_inc(xo_lo_done, 1)

            x_maxima(0)
            x_query_raw(1)
            split(Q_XQ + 1, 2)
            x_normalize(0)
            x_query_lo(1)
            split(Q_XQ + 1, 3)
            for n in range(2):
                split(Q_XO, 2 * n)
                x_turned_lo(n)
                x_maxima(n + 1)
                x_normalize(n + 1)
                x_out_lo(n)
                x_query_raw(n + 2)
                x_query_lo(n + 2)
                split(Q_XO, 2 * n + 1)

            def x_add(part, tiles):
                for n in tiles:
                    if n % CH == CH - 1:
                        dve.wait_ge(w_used[n // CH], Q_XO + part + 1)
                    else:
                        dve.wait_ge(xo_summed, (part * KT + n) // CH * (CH - 1) + n % CH + 1)
                    add_to_h(n, XO_BANKS[part][n % len(XO_BANKS[part])])

            x_turned_lo(2)
            x_add(0, range(4))
            x_maxima(3)
            split(Q_XO + 1, 0)
            x_add(0, range(4, 6))
            x_normalize(3)
            x_add(0, range(6, 7))
            x_out_lo(2)
            x_add(0, range(7, 8))
            x_turned_lo(3)
            split(Q_XO + 1, 1)
            x_add(0, range(8, 12))
            split(Q_XO + 1, 2)
            x_out_lo(3)
            x_add(0, range(12, 16))
            split(Q_XO + 1, 3)

            for n in range(KT):
                x_add(1, [n])
                if n >= CH and n % CH == 2:
                    split(Q_FFN, n // CH - 1)
                if n >= 4:
                    scaled_lo(3 * KT + n - 3, n - 4, h[:, n - 4, :], G_FFN)
            for n in range(KT - 4, KT):
                scaled_lo(3 * KT + n + 1, n, h[:, n, :], G_FFN)
            split(Q_FFN, 3)

            def gate_up(c, f, q):
                tile = c * CH + f
                split(q + 1, 0)
                split(q + 1, 1)
                dve.wait_ge(w_used[1], q + 1)
                passed(dve, g_lo_done, tile)
                nc.vector.tensor_tensor(gate_val[:, :], ps[:, 4 + f % 2, :], rstd[:, :], ALU.mult)\
                    .then_inc(gate_scaled, 1)
                split(q + 1, 2)
                dve.wait_ge(w_used[3], q + 1)
                nc.vector.tensor_tensor(up_val[:, :], ps[:, 6 + f % 2, :], rstd[:, :], ALU.mult).then_inc(up_scaled, 1)
                dve.wait_ge(up_scaled, tile + 1)
                dve.wait_ge(gate_silu, tile + 1)
                nc.vector.tensor_tensor(up_val[:, :], gate_val[:, :], up_val[:, :], ALU.mult).then_inc(g_raw_done, 1)
                split(q + 1, 3)
                dve.wait_ge(g_hi_done, tile + 1)
                slot = (c % 2) * CH + f
                nc.vector.tensor_tensor(one(g_lo, slot), up_val[:, :], one(g_hi, slot).bitcast(F32), ALU.subtract)\
                    .then_inc(g_lo_done, 1)

            def down(q):
                for u in range(2 * NJ):
                    dve.wait_ge(w_used[u % NJ], q + (u // NJ + 1))
                    for m in range(2):
                        add_to_h(2 * u + m, 2 * (u % 2) + m)
                    split(q + (1 + u // NJ), u % NJ)

            for f in range(CH):
                if f == 0:
                    invert(R_H2, rstd[:, :], root[:, :])
                    dve.wait_ge(norm_ready, R_H2)
                gate_up(0, f, Q_FFN + f)
            with dve.Fori(0, NCH - 1) as c:
                q = c * (CH + 2) + (Q_FFN + CH)
                for f in range(CH):
                    gate_up(c + 1, f, q + f)
                down(q + CH)

            def split_last(j):
                dve.wait_ge(w_hi_done[j], N_QUADS)
                hi = last_weights(w_hi, act_hi, NJ + j).bitcast(F32)
                nc.vector.tensor_tensor(last_weights(w_lo, act_lo, NJ + j), w_raw[:, j, :], hi, ALU.subtract)\
                    .then_inc(w_lo_done[j], 1)

            split_last(0)
            for half in range(2):
                for u in range(2 * NJ):
                    i = 2 * NJ * half + u
                    dve.wait_ge(last_summed, i + 1)
                    for m in range(2):
                        tile = h[:, 2 * u + m, HALVES[half]]
                        nc.vector.tensor_tensor(tile, ps[:, 2 * (u % 2) + m, :HALF], tile, ALU.add).then_inc(h_added, 1)
                    if half == 0 and u < NJ - 1:
                        split_last(u + 1)
                    if half == 1 and u == 2:
                        invert(R_FIN, rstd[:, HALVES[0]], root[:, HALVES[0]])
                        dve.wait_ge(norm_ready, R_FIN)
                    if half == 1 and u >= 3:
                        for out in range(2 * (u - 3), min(2 * (u - 2), UT)):
                            scale_out(dve, nc.vector, out)
            invert(R_FIN + 1, rstd[:, HALVES[1]], root[:, HALVES[1]])
            dve.wait_ge(norm_ready, R_FIN + 1)
            for i, engine in enumerate(out_engine):
                if i >= UT and engine == 0:
                    scale_out(dve, nc.vector, i)

        @block.tensor
        def _(pe):
            def product(out, l_hi, l_lo, r_hi, r_lo, start, stop, **more):
                nc.tensor.matmul(out, l_hi, r_hi, start=start, stop=False, **more)
                nc.tensor.matmul(out, l_hi, r_lo, start=False, stop=False, **more)
                return nc.tensor.matmul(out, l_lo, r_hi, start=False, stop=stop, **more)

            def unit_ready(q, j):
                pe.wait_ge(w_lo_done[j], q + 1)

            def feature_unit(q, j, bank, half, act_event=None, tiles=range(UT)):
                if tiles[0] == 0:
                    unit_ready(q, j)
                for t in tiles:
                    k = UT * half + t
                    if act_event is not None:
                        pe.wait_ge(act_lo_done, act_event + k + 1)
                    cols = slice(t * P, (t + 1) * P)
                    last = product(ps[:, bank, :], w_hi[:, j, cols], w_lo[:, j, cols], act_hi[:, k, :], act_lo[:, k, :],
                                   k == 0, k == KT - 1)
                if tiles[-1] == UT - 1:
                    last.then_inc(w_used[j], 1)

            def sum_squares(sums, bank, at=0, width=SEQ, cols=None):
                last = nc.tensor.matmul(ps[:, bank, at:at + width], ones[:, :], sums, start=True, stop=True)
                if cols:
                    col_bank, first, blocks = cols
                    for b in range(blocks):
                        last = nc.tensor.matmul(ps[:, col_bank, first + b:first + b + 1], sums[:, b * P:(b + 1) * P],
                                                ones[:, 0:1], start=True, stop=True)
                last.then_inc(norm_summed, 1)

            pe.wait_ge(consts_set, 2)
            for _ in range(WARM_UP):
                nc.tensor.matmul(ps[:, 7, :P], ones[:, :], ones[:, :], start=True, stop=True)
            for group in range(3):
                if group == 1:
                    pe.wait_ge(norm_root, R_XCOL)
                if group == 2:
                    pe.wait_ge(v_copied, TB)
                for u in range(2 * NJ):
                    q, j = 2 * group + u // NJ, u % NJ
                    if group == 0 and u == 2 * NJ - 1:
                        pe.wait_ge(square_added, KT)
                        sum_squares(square_sum[:, SLOT_X, :], 4, cols=(5, 0, TB))
                    unit_ready(q, j)
                    for b in range(TB):
                        for t in range(2):
                            k = 2 * u + t
                            if group == 0 and b == 0:
                                pe.wait_ge(act_lo_done, k + 1)
                            tok = slice(b * P, (b + 1) * P)
                            cols = slice(t * SEQ, (t + 1) * SEQ)
                            last = product(ps[:, 4 * (group % 2) + b, :], act_hi[:, k, tok], act_lo[:, k, tok],
                                           w_hi[:, j, cols], w_lo[:, j, cols], k == 0, k == KT - 1)
                    last.then_inc(w_used[j], 1)
            pe.wait_ge(v_copied, 2 * TB)
            for j in range(NJ):
                if j == 2:
                    pe.wait_ge(v_copied, 3 * TB)
                feature_unit(Q_BC, j, (7, 0)[j // 2], j % 2)

            def scores(n, pair, lay):
                rows = rows_of(n)
                pe.wait_ge(proj_lo_done[n], q_event(pair))
                pe.wait_ge(k_doubled, BC_PAIRS + 1 if lay is WINDOWED else pair + 1)
                for m, (i, first_key, w, c, _) in enumerate(lay.rows):
                    b = c // SEQ
                    if b == 2:
                        passed(pe, out_copied[n], pair)
                    tok = slice(i * P, (i + 1) * P)
                    keys = slice(first_key, first_key + w)
                    out = ps[:, head_bank(n, b), c % SEQ:c % SEQ + w]
                    nc.tensor.matmul(out, q_both[:, n, tok], k_twice[:, n, keys], start=True, stop=False)
                    last = nc.tensor.matmul(out, q_both[rows, n, tok], k_lo[rows, keys], start=False, stop=True)
                    if m == len(lay.rows) - 1 or lay.rows[m + 1][3] // SEQ != b:
                        last.then_inc(scored[n][b], 1)

            def turn(n, pair, lay):
                pe.wait_ge(probs_ready[n], pair + 1)
                if at(pair, 0):
                    pe.wait_ge(tables_landed, 32)
                blocks = []
                for j, (c, i0, count) in lay.cols.items():
                    for i in range(i0, i0 + count):
                        first_key, start = next((r[1], r[3]) for r in lay.rows if r[0] == i)
                        blocks.append((c + (i - i0) * P, start + j * P - first_key))
                blocks.sort()
                for x, (dst, src) in enumerate(blocks):
                    b = dst // SEQ
                    out = ps[:, head_bank(n, b), dst % SEQ:dst % SEQ + P]
                    last = nc.tensor.transpose(out, probs[n][:, src:src + P], ident[:, :])
                    if x == len(blocks) - 1 or blocks[x + 1][0] // SEQ != b:
                        last.then_inc(turned[n][b], 1)

            def mix(n, pair, lay):
                out = ps[:, head_bank(n, 2), :]
                if lay.banks < 3:
                    pe.wait_ge(out_copied[n], pair)
                    if pair == BC_PAIRS:
                        pe.wait_ge(norm_root, (R_B, R_C)[n])
                for b in reversed(range(lay.banks)):
                    pe.wait_ge(pT_lo_done[n][b], pair + 1)
                order = sorted(lay.cols)
                for j in order:
                    c, i0, count = lay.cols[j]
                    w = count * P
                    for weights in (probsT_hi, probsT_lo):
                        last = nc.tensor.matmul(out[:, i0 * P:i0 * P + w], v_both[n][:, j, :], weights[:, c:c + w],
                                                start=j == order[0] and weights is probsT_hi,
                                                stop=j == order[-1] and weights is probsT_lo, skip_group_check=True)
                last.then_inc(mixed[n], 1)

            def run(halves):
                for q, j, bank, half, tiles, event in halves:
                    feature_unit(q, j, bank, half, event, tiles)

            def attend(pair, fill, before_turn=None, after_turn=None):
                lay = layout(pair)
                pe.wait_ge(proj_raw_done, k_event(pair))
                run(fill[0])
                scores(0, pair, lay)
                if not at(pair, 0):
                    mix(1, pair - 1, layout(pair - 1))
                if lay is CAUSAL:
                    run(fill[1][:1])
                scores(1, pair, lay)
                run(fill[1][1:] if lay is CAUSAL else fill[1])
                if before_turn:
                    before_turn()
                turn(0, pair, lay)
                if after_turn:
                    after_turn()
                run(fill[2])
                pe.wait_ge(v_lo_done, min(pair, BC_PAIRS) + 1 if isinstance(pair, int) else pair + 1)
                mix(0, pair, lay)
                run(fill[3])
                turn(1, pair, lay)

            FRONT, BACK = range(UT // 2), range(UT // 2, UT)

            def bc_fill(pair):
                q = fill_quad(pair)
                halves = [(q, j, 1 - j // 2, j % 2, tiles, None) for j in range(NJ) for tiles in (FRONT, BACK)]
                return halves[:1], halves[1:4], halves[4:6], halves[6:]

            attend(0, bc_fill(0))
            with pe.Fori(1, BC_PAIRS) as pair:
                attend(pair, bc_fill(pair))

            def turn_va():
                pe.wait_ge(va_raw_done, 1)
                for b in range(TB):
                    last = nc.tensor.transpose(ps[:, 1, b * P:(b + 1) * P], proj_raw[:, b * P:(b + 1) * P],
                                               ident[:, :])
                last.then_inc(va_turned, 1)

            def sum_outs():
                for slot, count, n in ((SLOT_B, B_PAIRS, 0), (SLOT_C, BC_PAIRS, 1)):
                    pe.wait_ge(out_square_added, count)
                    pe.wait_ge(out_copied[n], BC_PAIRS)
                    sum_squares(square_sum[:, slot, :], head_bank(n, 2))

            def halves_of(q, j, bank, half, event=None):
                return [(q, j, bank, half, tiles, event) for tiles in (FRONT, BACK)]

            va = halves_of(Q_VA, 0, 1, 0) + halves_of(Q_VA, 1, 1, 1)
            attend(BC_PAIRS, (va[:1], va[1:], halves_of(Q_VA, 2, 0, 0), halves_of(Q_VA, 3, 0, 1)), sum_outs, turn_va)
            q2 = halves_of(Q_QA, 0, 1, 0) + halves_of(Q_QA, 1, 1, 1)
            q3 = halves_of(Q_QA, 2, 0, 0) + halves_of(Q_QA, 3, 0, 1)
            attend(BC_PAIRS + 1, (q2[:1], q2[1:3], q2[3:] + q3[:1], q3[1:2]))

            def out_half(q, j, n, m, first):
                if m == 0:
                    unit_ready(q, j)
                for t in range(CH):
                    k = first + t
                    pe.wait_ge(act_lo_done, KT + k + 1)
                    cols = slice((m * CH + t) * P, (m * CH + t + 1) * P)
                    last = product(ps[:, OUT_BANKS[n + m], :], w_hi[:, j, cols], w_lo[:, j, cols], act_hi[:, k, :],
                                   act_lo[:, k, :], False, k == KT - 1)
                if m:
                    last.then_inc(w_used[j], 1)

            def first_two_over_b():
                for m in range(2):
                    out_half(Q_OUT, 2, 0, m, C_PAIRS)

            over_c = [halves_of(Q_OUT + (n == 3), (0, 1, 3, 0)[n], OUT_BANKS[n], 0, KT) for n in range(4)]
            attend(BC_PAIRS + 2, (q3[2:3], q3[3:] + over_c[0][:1], over_c[0][1:], ()))
            pe.wait_ge(proj_raw_done, q_event(PAIRS - 1))
            attend(PAIRS - 1, (over_c[1][:1], over_c[1][1:], (), ()), after_turn=first_two_over_b)
            run(over_c[2][:1])
            mix(1, PAIRS - 1, WINDOWED)
            run(over_c[2][1:])
            pe.wait_ge(out_square_added, PAIRS - 1)
            nc.tensor.matmul(ps[:, 5, :], ones[:, :], square_sum[:, SLOT_A, :], start=True, stop=False)
            pe.wait_ge(last_out_squared, 1)
            nc.tensor.matmul(ps[:, 5, :], ones[:, :], squares[:, 0, :], start=False, stop=True).then_inc(norm_summed, 1)
            run(over_c[3])
            for j, n, first in ((1, 2, C_PAIRS), (2, 0, BC_PAIRS), (3, 2, BC_PAIRS)):
                for m in range(2):
                    out_half(Q_OUT + 1, j, n, m, first)
            with pe.Fori(2, KT // 2) as g:
                for half in range(2):
                    for m in range(2):
                        if half == 0:
                            pe.wait_ge(h_added, g * 2 + (m - 1))
                        feature_unit(g + Q_OUT, 2 * half + m, m, half)

            for k in range(KT):
                j = k % NJ
                if k == NJ:
                    pe.wait_ge(h_added, KT)
                    pe.wait_ge(square_added, 2 * KT)
                    sum_squares(square_sum[:, SLOT_H1, :], 0)
                unit_ready(Q_MEM + k // NJ, j)
                pe.wait_ge(mem_lo_done, k + 1)
                m = k % 4
                for n in range(X_HEADS):
                    cols = slice(n * P, (n + 1) * P)
                    product(ps[:, 2 + n, :MEM_LEN], w_hi[:, j, cols], w_lo[:, j, cols], mem_hi[:, m, :],
                            mem_lo[:, m, :],
                            k == 0, k == KT - 1)
                for b in range(MB):
                    tok = slice(b * P, (b + 1) * P)
                    last = product(ps[:, 6 + b, :], mem_hi[:, m, tok], mem_lo[:, m, tok], w_hi[:, j, X_HEADS * P:],
                                   w_lo[:, j, X_HEADS * P:], k == 0, k == KT - 1)
                last.then_inc(w_used[j], 1)

            def x_query(n, halves=(0, 1), tiles=range(UT)):
                if n >= 2 and halves[0] == 0:
                    pe.wait_ge(xq_raw_done, n - 1)
                for half in halves:
                    feature_unit(Q_XQ + n // 2, 2 * (n % 2) + half, n % 2, half, 2 * KT if n == 0 else None, tiles)

            def x_scores(n):
                pe.wait_ge(xq_lo_done, n + 1)
                pe.wait_ge(km_lo_done, X_HEADS)
                for i in range(TB):
                    tok = slice(i * P, (i + 1) * P)
                    last = product(ps[:, 2 + i // 2, (i % 2) * MEM_LEN:(i % 2 + 1) * MEM_LEN], xq_hi[:, tok],
                                   xq_lo[:, tok], km_hi[:, n, :], km_lo[:, n, :], True, True)
                last.then_inc(x_scored, 1)

            def x_turn(n):
                pe.wait_ge(x_ready, n + 1)
                for b in range(MB):
                    for i in range(TB):
                        last = nc.tensor.transpose(ps[:, 4 + b, i * P:(i + 1) * P], x_probs[:, i, b * P:(b + 1) * P],
                                                   ident[:, :])
                last.then_inc(x_turned, 1)

            def x_mix(n):
                pe.wait_ge(xpT_lo_done, MB * (n + 1))
                pe.wait_ge(vm_lo_done, MB)
                if n >= 2:
                    pe.wait_ge(xo_lo_done, (1, 3)[n - 2])
                cols = slice(n * P, (n + 1) * P)
                for b in range(MB):
                    last = product(ps[:, X_OUT_BANKS[n], :], vm_hi[:, b, cols], vm_lo[:, b, cols], xpT_hi[:, b, :],
                                   xpT_lo[:, b, :], b == 0, b == MB - 1)
                last.then_inc(x_mixed, 1)

            pe.wait_ge(norm_root, R_H1)
            x_query(0)
            pe.wait_ge(square_added, 3 * KT)
            sum_squares(square_sum[:, SLOT_MEM, :MEM_LEN], 2, MEM_LEN, MEM_LEN, cols=(3, MEM_LEN, MB))
            x_query(1)
            x_scores(0)
            for n in range(2):
                x_query(n + 2, (0,))
                x_turn(n)
                x_scores(n + 1)
                x_query(n + 2, (1,), FRONT)
                x_mix(n)
                x_query(n + 2, (1,), BACK)

            def x_project(part, tiles):
                pe.wait_ge(xo_lo_done, 2 * part + 2)
                banks = XO_BANKS[part]
                for n in tiles:
                    if n % CH == 0:
                        unit_ready(Q_XO + part, n // CH)
                    if n >= len(banks):
                        pe.wait_ge(h_added, (1 + part) * KT + n + 1 - len(banks))
                    elif part == 1 and n == 2:
                        pe.wait_ge(h_added, 2 * KT)
                    if part == 0 and n == 1:
                        pe.wait_ge(xq_raw_done, X_HEADS)
                    for k in range(2):
                        cols = slice((n % CH * 2 + k) * P, (n % CH * 2 + k + 1) * P)
                        last = product(ps[:, banks[n % len(banks)], :], w_hi[:, n // CH, cols], w_lo[:, n // CH, cols],
                                       xo_hi[:, 2 * part + k, :], xo_lo[:, 2 * part + k, :], k == 0, k == 1)
                    last.then_inc(w_used[n // CH] if n % CH == CH - 1 else xo_summed, 1)

            x_turn(2)
            x_project(0, range(0, 4))
            x_scores(3)
            x_mix(2)
            x_project(0, range(4, 8))
            x_turn(3)
            x_project(0, range(8, 12))
            x_mix(3)
            x_project(0, range(12, 16))
            x_project(1, range(KT))

            def narrow_quads(q, r_hi, r_lo, slot, added):
                for u in range(2 * NJ):
                    j = u % NJ
                    unit_ready(q + u // NJ, j)
                    pe.wait_ge(h_added, added + (2 * u - 2))
                    for m in range(2):
                        for k in range(CH):
                            cols = slice((m * CH + k) * P, (m * CH + k + 1) * P)
                            last = product(ps[:, 2 * (u % 2) + m, :], w_hi[:, j, cols], w_lo[:, j, cols],
                                           one(r_hi, slot + k), one(r_lo, slot + k), k == 0, k == CH - 1)
                    last.then_inc(w_used[j], 1)

            def gate_up(c, f, q):
                tile = c * CH + f
                event = 3 * KT if isinstance(c, int) and f == 0 else None
                for half in range(2):
                    if half == 0:
                        passed(pe, gate_scaled, tile - 1)
                    feature_unit(q, half, 4 + f % 2, half, event)
                if event is not None:
                    pe.wait_ge(square_added, 4 * KT)
                    sum_squares(square_sum[:, SLOT_H2, :], 0)
                for half in range(2):
                    if half == 0:
                        passed(pe, up_scaled, tile - 1)
                    feature_unit(q, 2 + half, 6 + f % 2, half)

            def down(c, q):
                pe.wait_ge(g_lo_done, c * CH + CH)
                narrow_quads(q, g_hi, g_lo, (c % 2) * CH, c * KT + 3 * KT)

            for f in range(CH):
                gate_up(0, f, Q_FFN + f)
            with pe.Fori(0, NCH - 1) as c:
                q = c * (CH + 2) + (Q_FFN + CH)
                for f in range(CH):
                    gate_up(c + 1, f, q + f)
                down(c, q + CH)
            pe.wait_ge(g_lo_done, FT)
            slot = (NCH - 1) % 2 * CH
            for half in range(2):
                for u in range(2 * NJ):
                    i = 2 * NJ * half + u
                    unit_ready(N_QUADS - 2 + u // NJ, u % NJ)
                    pe.wait_ge(h_added, (NCH + 2) * KT + 2 * i - 2)
                    for m in range(2):
                        for k in range(CH):
                            cols = slice((m * CH + k) * P, (m * CH + k + 1) * P)
                            last = product(ps[:, 2 * (u % 2) + m, :HALF], last_weights(w_hi, act_hi, u)[:, cols],
                                           last_weights(w_lo, act_lo, u)[:, cols], g_hi[:, slot + k, HALVES[half]],
                                           g_lo[:, slot + k, HALVES[half]], k == 0, k == CH - 1)
                    last.then_inc(last_summed, 1)
                    if half == 1 and u == 1:
                        pe.wait_ge(square_added, 5 * KT)
                        sum_squares(square_sum[:, SLOT_FIN, HALVES[0]], 4, 0, HALF)
            pe.wait_ge(square_added, 6 * KT - 2)
            nc.tensor.matmul(ps[:, 5, :HALF], ones[:, :], square_sum[:, SLOT_FIN, HALVES[1]], start=True, stop=False)
            for m in range(2):
                pe.wait_ge(squared, 6 * KT - 1 + m)
                last = nc.tensor.matmul(ps[:, 5, :HALF], ones[:, :], squares[:, m, :HALF], start=False, stop=m == 1)
            last.then_inc(norm_summed, 1)


def bias_tables(np):
    dist = np.arange(P)[:, None] + (SEQ - P) - np.arange(SEQ)[None, :]
    causal = dist >= 0
    count_a = causal & (dist < 128)
    count_c = causal & (dist <= 128)
    count_c = count_c.astype(int) + (causal & (dist % 4 == 0)) + (causal & (dist % 16 == 0))

    def table(slope, count):
        times = np.log(np.maximum(count, 1).astype(np.float64)) - np.float64(slope) * dist
        return np.where(count > 0, times, NEG).astype(np.float32)

    def slopes(n):
        return (2.0 ** (-8.0 * np.arange(1, n + 1) / n)).astype(np.float32)

    a, b, c = slopes(2 * A_PAIRS), slopes(2 * B_PAIRS), slopes(2 * C_PAIRS)
    out = [table(s, causal.astype(int)) for s in b]
    out += [table(s, count_c) for s in c]
    out += [table(a[n], count_a) for pair in range(A_PAIRS) for n in (pair, pair + A_PAIRS)]
    return np.stack(out)


def weight_stream(np, w_in, w_out, wq, wk, wv, wo, w_gate, w_up, w_down):
    def tiles(w):
        return w.reshape(w.shape[0] // P, P, w.shape[1] // P, P).transpose(0, 2, 1, 3)

    def unit(parts):
        return np.concatenate(parts, axis=1)

    def features(w, n):
        return [unit([w[k, n] for k in range(UT * half, UT * half + UT)]) for half in range(2)]

    a_w, kv_w, b_w, c_w = 512, 128, 512, 1024
    at, parts = 0, []
    for width in (a_w, kv_w, kv_w, b_w, b_w, b_w, c_w, c_w, c_w):
        parts.append(w_in[:, at:at + width])
        at += width
    qa, ka, va, qb, kb, vb, qc, kc, vc = parts
    heads = [x for p in range(A_PAIRS) for x in (p, p + A_PAIRS)]
    qa = qa.reshape(D_MODEL, 2 * A_PAIRS, HEAD_DIM)[:, heads].reshape(D_MODEL, a_w)
    units = []
    for v in (vb, vc[:, :SEQ], vc[:, SEQ:]):
        v = v.reshape(KT, P, SEQ)
        units += [unit([v[2 * u], v[2 * u + 1]]) for u in range(KT // 2)]
    for q, k, n in ((qb, kb, B_PAIRS), (qc, kc, C_PAIRS)):
        q, k = tiles(q), tiles(k)
        for p in range(n):
            units += features(k, p) + features(q, p)
    qa = tiles(qa)
    units += features(tiles(ka), 0) + features(qa, 0) + features(tiles(va), 0)
    for p in range(1, A_PAIRS):
        units += features(qa, p)
    rows_a = w_out[:a_w].reshape(2 * A_PAIRS, HEAD_DIM, D_MODEL)[heads].reshape(a_w, D_MODEL)
    o = tiles(np.concatenate([w_out[a_w + b_w:], w_out[a_w:a_w + b_w], rows_a]))

    def two(n, first):
        return unit([o[first + k, n + m] for m in range(2) for k in range(CH)])

    c = [features(o, n)[0] for n in range(4)]
    units += [c[0], c[1], two(0, C_PAIRS), c[2], c[3], two(2, C_PAIRS), two(0, BC_PAIRS), two(2, BC_PAIRS)]
    for g in range(2, KT // 2):
        (c0, ba0), (c1, ba1) = features(o, 2 * g), features(o, 2 * g + 1)
        units += [c0, c1, ba0, ba1]
    k3, v3 = wk.reshape(KT, P, X_HEADS * P), wv.reshape(KT, P, X_HEADS * P)
    units += [unit([k3[k], v3[k]]) for k in range(KT)]
    for n in range(X_HEADS):
        units += features(tiles(wq), n)

    def narrow(w, k0):
        return [unit([w[k0 + k, 2 * u + m] for m in range(2) for k in range(CH)]) for u in range(KT // 2)]

    o = tiles(wo)
    units += [unit([o[2 * part + k, 4 * u + m] for m in range(4) for k in range(2)])
              for part in range(2) for u in range(4)]
    gate, up, down = tiles(w_gate), tiles(w_up), tiles(w_down)

    def gate_up(c):
        return [x for f in range(CH) for w in (gate, up) for x in features(w, c * CH + f)]

    units += gate_up(0)
    for c in range(NCH - 1):
        units += gate_up(c + 1) + narrow(down, c * CH)
    units += narrow(down, (NCH - 1) * CH)
    assert len(units) == N_QUADS * NJ
    return np.stack(units)


def kernel(x, mem, norm_mix, w_in, sinks, gain_a, gain_b, gain_c, w_out, norm_xattn, norm_mem,
           wq_x, wk_x, wv_x, wo_x, norm_ffn, w_gate, w_up, w_down, norm_final):
    import numpy as np
    import concourse.bacc as bacc
    from concourse.bass_utils import run_bass_kernel_spmd

    def col(v):
        return np.asarray(v).reshape(-1, P).T

    heads = [n for p in range(A_PAIRS) for n in (p, p + A_PAIRS)]
    g_a = np.asarray(gain_a)[0].reshape(2 * A_PAIRS, HEAD_DIM)[heads].reshape(-1)
    arrays = {
        "xT": np.asarray(x)[0].T,
        "memT": np.asarray(mem)[0].T,
        "stream": weight_stream(np, *(np.asarray(w)[0] for w in (w_in, w_out, wq_x, wk_x, wv_x, wo_x, w_gate, w_up,
                                                                 w_down))),
        "gains": np.concatenate([col(norm_mix), col(gain_c), col(gain_b), col(g_a), col(norm_xattn), col(norm_mem),
                                 col(norm_ffn), col(norm_final)], axis=1),
        "sinks": np.broadcast_to(np.asarray(sinks)[0][heads], (P, 2 * A_PAIRS)),
        "bias_table": bias_tables(np),
        "identity": np.eye(P, dtype=np.float32),
    }
    arrays = {n: np.ascontiguousarray(a) for n, a in arrays.items()}
    nc = bacc.Bacc("TRN2", target_bir_lowering=False, num_devices=1)
    args = [nc.dram_tensor(n, a.shape, F32, kind="ExternalInput").ap() for n, a in arrays.items()]
    outT = nc.dram_tensor("outT", (D_MODEL, SEQ), F32, kind="ExternalOutput").ap()
    build(nc, *args, outT)
    result = run_bass_kernel_spmd(nc, [arrays], core_ids=[0]).results[0]["outT"]
    return np.ascontiguousarray(result.T).reshape(1, SEQ, D_MODEL)
```
